# Optimizing a Trainium2 kernel written in Bass

```python
import jax, jax.numpy as jnp
from jax import lax
import numpy as np

D_MODEL = 1024
BATCH = 1
SEQ = 1024
DEPTH = 1

N_MEM = 256
EPS = 1e-6
D_A = D_MODEL
CONV_A_WIDTH = 3
FOX_HEADS = 16
FOX_HEAD_DIM = D_MODEL // FOX_HEADS
D_B = FOX_HEADS * FOX_HEAD_DIM
Q_BLOCK = 128
D_C = D_MODEL
CONV_C_WIDTH = 31
N_BRANCH = 3
X_HEADS = 4
X_HEAD_DIM = 128
D_X = X_HEADS * X_HEAD_DIM
D_FF = -(-8 * D_MODEL // (3 * 256)) * 256
IN_SIZES = (D_A, D_A, D_A, D_B, D_B, D_B, FOX_HEADS, D_C, D_C, D_MODEL, D_MODEL, D_MODEL)
D_IN_TOTAL = sum(IN_SIZES)

kernel_name = "hybrid_gated_conv_fox_conformer_decoder"

def rms_norm(x, g):
    xf = x.astype(jnp.float32)
    y = xf * lax.rsqrt(jnp.mean(xf * xf, axis=-1, keepdims=True) + EPS)
    return (y * g.astype(jnp.float32)).astype(x.dtype)

def layer_norm(x, g, b):
    xf = x.astype(jnp.float32)
    mu = jnp.mean(xf, axis=-1, keepdims=True)
    xc = xf - mu
    y = xc * lax.rsqrt(jnp.mean(xc * xc, axis=-1, keepdims=True) + EPS)
    return (y * g.astype(jnp.float32) + b.astype(jnp.float32)).astype(x.dtype)

def causal_depthwise_conv(x, w):
    K, C = w.shape
    return lax.conv_general_dilated(
        x, w[:, None, :].astype(x.dtype), window_strides=(1,), padding=[(K - 1, 0)],
        dimension_numbers=("NWC", "WIO", "NWC"), feature_group_count=C)

def split_columns(z):
    offs = np.cumsum(np.array(IN_SIZES))[:-1]
    return jnp.split(z, [int(o) for o in offs], axis=-1)

def forgetting_attention(q, k, v, log_f):
    B, T, H, Dh = q.shape
    c = jnp.cumsum(log_f, axis=1).transpose(0, 2, 1)
    scale = Dh ** -0.5
    outs = []
    for i in range(T // Q_BLOCK):
        q0 = i * Q_BLOCK
        k_end = q0 + Q_BLOCK
        s = jnp.einsum("bqhd,bkhd->bhqk", q[:, q0:k_end], k[:, :k_end]).astype(jnp.float32) * scale
        decay = c[:, :, q0:k_end, None] - c[:, :, None, :k_end]
        causal = (q0 + jnp.arange(Q_BLOCK))[:, None] >= jnp.arange(k_end)[None, :]
        s = jnp.where(causal, s + decay, -jnp.inf)
        p = jax.nn.softmax(s, axis=-1)
        outs.append(jnp.einsum("bhqk,bkhd->bqhd", p.astype(v.dtype), v[:, :k_end]))
    return jnp.concatenate(outs, axis=1)

def hybrid_mixer(h, w_in, b_gate, b_forget, conv_a, w_out_a, w_out_b, conv_c, conv_c_bias,
                 ln_c_gain, ln_c_bias, w_out_c, w_o):
    B, T, _ = h.shape
    z = jnp.einsum("btd,de->bte", h, w_in)
    (a_b, a_c, a_u, q, k, v, f_logit, c_val, c_gate, g_a, g_b, g_c) = split_columns(z)
    y_a = a_b * causal_depthwise_conv(a_c * a_u, conv_a)
    y_a = jnp.einsum("btc,cd->btd", y_a, w_out_a)
    log_f = jax.nn.log_sigmoid(f_logit.astype(jnp.float32) + b_forget.astype(jnp.float32))
    o = forgetting_attention(q.reshape(B, T, FOX_HEADS, FOX_HEAD_DIM),
                             k.reshape(B, T, FOX_HEADS, FOX_HEAD_DIM),
                             v.reshape(B, T, FOX_HEADS, FOX_HEAD_DIM), log_f)
    y_b = jnp.einsum("btc,cd->btd", o.reshape(B, T, D_B), w_out_b)
    u = c_val * jax.nn.sigmoid(c_gate)
    u = causal_depthwise_conv(u, conv_c) + conv_c_bias.astype(u.dtype)
    u = jax.nn.silu(layer_norm(u, ln_c_gain, ln_c_bias))
    y_c = jnp.einsum("btc,cd->btd", u, w_out_c)
    ga, gb, gc = jnp.split(jax.nn.sigmoid(jnp.concatenate([g_a, g_b, g_c], axis=-1) + b_gate), N_BRANCH, axis=-1)
    merged = ga * y_a + gb * y_b + gc * y_c
    return jnp.einsum("btd,de->bte", merged, w_o)

def memory_cross_attention(h, mem_n, w_xq, w_xkv, w_xo):
    B, T, _ = h.shape
    q = jnp.einsum("btd,de->bte", h, w_xq).reshape(B, T, X_HEADS, X_HEAD_DIM)
    kv = jnp.einsum("bmd,de->bme", mem_n, w_xkv)
    k, v = jnp.split(kv, 2, axis=-1)
    k = k.reshape(B, -1, X_HEADS, X_HEAD_DIM)
    v = v.reshape(B, -1, X_HEADS, X_HEAD_DIM)
    s = jnp.einsum("bthd,bmhd->bhtm", q, k).astype(jnp.float32) * (X_HEAD_DIM ** -0.5)
    p = jax.nn.softmax(s, axis=-1)
    o = jnp.einsum("bhtm,bmhd->bthd", p.astype(v.dtype), v).reshape(B, T, D_X)
    return jnp.einsum("btc,cd->btd", o, w_xo)

def swiglu_ffn(h, w_gate_up, w_down):
    g, u = jnp.split(jnp.einsum("btd,df->btf", h, w_gate_up), 2, axis=-1)
    return jnp.einsum("btf,fd->btd", jax.nn.silu(g) * u, w_down)

def setup_inputs(seed: int = 0) -> dict:
    key = jax.random.key(seed)
    ks = jax.random.split(key, 24)
    f32 = jnp.float32

    def w(k, shape, fan_in):
        return jax.random.normal(k, shape, f32) * (fan_in ** -0.5)

    def gain(k, shape):
        return 1.0 + 0.02 * jax.random.normal(k, shape, f32)

    def small(k, shape, s=0.02):
        return s * jax.random.normal(k, shape, f32)

    L, D = DEPTH, D_MODEL
    return {
        "x": jax.random.normal(ks[0], (BATCH, SEQ, D), f32),
        "mem": jax.random.normal(ks[1], (BATCH, N_MEM, D), f32),
        "mix_norm": gain(ks[2], (L, D)),
        "w_in": w(ks[3], (L, D, D_IN_TOTAL), D),
        "b_gate": small(ks[4], (L, N_BRANCH * D)),
        "b_forget": 2.0 + 0.5 * jax.random.normal(ks[5], (L, FOX_HEADS), f32),
        "conv_a": w(ks[6], (L, CONV_A_WIDTH, D_A), CONV_A_WIDTH),
        "w_out_a": w(ks[7], (L, D_A, D), D_A),
        "w_out_b": w(ks[8], (L, D_B, D), D_B),
        "conv_c": w(ks[9], (L, CONV_C_WIDTH, D_C), CONV_C_WIDTH),
        "conv_c_bias": small(ks[10], (L, D_C)),
        "ln_c_gain": gain(ks[11], (L, D_C)),
        "ln_c_bias": small(ks[12], (L, D_C)),
        "w_out_c": w(ks[13], (L, D_C, D), D_C),
        "w_o": w(ks[14], (L, D, D), D),
        "xattn_norm": gain(ks[15], (L, D)),
        "mem_norm": gain(ks[16], (D,)),
        "w_xq": w(ks[17], (L, D, D_X), D),
        "w_xkv": w(ks[18], (L, D, 2 * D_X), D),
        "w_xo": w(ks[19], (L, D_X, D), D_X),
        "ffn_norm": gain(ks[20], (L, D)),
        "w_gate_up": w(ks[21], (L, D, 2 * D_FF), D),
        "w_down": w(ks[22], (L, D_FF, D), D_FF),
        "final_norm": gain(ks[23], (D,)),
    }

def reference(x, mem, mix_norm, w_in, b_gate, b_forget, conv_a, w_out_a, w_out_b, conv_c,
              conv_c_bias, ln_c_gain, ln_c_bias, w_out_c, w_o, xattn_norm, mem_norm, w_xq,
              w_xkv, w_xo, ffn_norm, w_gate_up, w_down, final_norm):
    mem_n = rms_norm(mem, mem_norm)
    for l in range(DEPTH):
        x = x + hybrid_mixer(rms_norm(x, mix_norm[l]), w_in[l], b_gate[l], b_forget[l], conv_a[l],
                             w_out_a[l], w_out_b[l], conv_c[l], conv_c_bias[l], ln_c_gain[l],
                             ln_c_bias[l], w_out_c[l], w_o[l])
        x = x + memory_cross_attention(rms_norm(x, xattn_norm[l]), mem_n, w_xq[l], w_xkv[l], w_xo[l])
        x = x + swiglu_ffn(rms_norm(x, ffn_norm[l]), w_gate_up[l], w_down[l])
    return rms_norm(x, final_norm)


_drawn_inputs = setup_inputs


def setup_inputs(seed=0):
    import zlib

    import numpy as np

    out = dict(_drawn_inputs(seed))
    spreads = {}
    factors = {'mix_norm': 2.801,
     'b_gate': 8.0,
     'conv_c_bias': 4.981,
     'ln_c_gain': 7.894,
     'ln_c_bias': 8.0,
     'xattn_norm': 8.0,
     'mem_norm': 8.0,
     'ffn_norm': 14.043,
     'final_norm': 8.431}
    for name, (base, spread) in spreads.items():
        noise = np.random.default_rng([zlib.crc32(name.encode()), seed]).standard_normal(out[name].shape)
        drawn = base * np.exp(spread * noise) if base else spread * noise
        out[name] = __import__('jax').numpy.asarray(drawn.astype(out[name].dtype))
    for name, factor in factors.items():
        out[name] = (out[name] * factor).astype(out[name].dtype)
    return out
```

```python
from contextlib import ExitStack

import numpy as np

import concourse.bass as bass
from concourse import mybir

P = 128
F32 = mybir.dt.float32
R32 = mybir.dt.float32r
ALU = mybir.AluOpType
ACT = mybir.ActivationFunctionType
AX = mybir.AxisListType
EPS = 1e-6
MASKED = -1e30
HI, LO = 0, 1

D = 1024
T = 1024
KD = D // P
TB = T // P
HALF = 512
NH, DH = 16, 64
QK_ROWS = DH + 2
KA, KC = 3, 31
N_MEM = 256
MB = N_MEM // P
XH, XD = 4, 128
FF = 2816
NF = FF // P

T_FORGET = 0
T_BRANCH = T_FORGET + 1
T_GATE = T_BRANCH + 8 * KD
T_MERGE = T_GATE + 3 * KD
T_O = T_MERGE + 3 * KD
T_XQ = T_O + 2 * KD
T_XK = T_XQ + 2
T_XV = T_XK + XH
T_XQ2 = T_XV + KD // 2
T_XO = T_XQ2 + 2
T_FF = T_XO + 2 * XH
T_END = T_FF + 3 * NF

C_CONVC = 0
C_CBIAS = C_CONVC + KD * KC
C_CONVA = C_CBIAS + KD
C_BGATE = C_CONVA + KD * KA
C_LNG = C_BGATE + 3 * KD
C_LNB = C_LNG + KD
C_BF = C_LNB + KD
N_PARAM = C_BF + 1


class Chain:

    def __init__(self, sem):
        self.sem, self.n, self.i, self.per, self.start = sem, 0, None, 0, 0

    def enter(self, i, per):
        self.i, self.per, self.start = i, per, self.n

    def leave(self, iterations):
        assert self.n - self.start == self.per, (self.n - self.start, self.per)
        self.n = self.start + self.per * iterations
        self.i = None

    def link(self, eng, ins):
        ins.then_inc(self.sem, 1)
        self.n += 1
        eng.wait_ge(self.sem, self.n if self.i is None else self.i * self.per + self.n)


def build(nc, x, mem, w_in, w_out, w_o, w_xq, w_xk, w_xv, w_xo, w_gu, w_down, params, norms, out):
    def scratch(name, shape, dt):
        return nc.dram_tensor(name, shape, dt).ap()

    q_s = scratch("q_s", (NH, QK_ROWS, 2 * T), F32)
    k_s = scratch("k_s", (NH, QK_ROWS, 2 * T), F32)
    v_s = scratch("v_s", (NH // 2, P, 2 * T), F32)
    a_s = scratch("a_s", (KD, P, 2 * T), F32)
    b_s = scratch("b_s", (KD, P, 2 * T), F32)
    u_s = scratch("u_s", (KD, P, T), F32)
    g_s = scratch("g_s", (3 * KD, P, T), F32)
    m_s = scratch("m_s", (KD, P, T), F32)

    with ExitStack() as ctx:
        def sem(name):
            return ctx.enter_context(nc.semaphore(name))

        def sb(name, shape, dt=F32, scope=ctx):
            return scope.enter_context(nc.sbuf_tensor(name, shape, dt))

        ident = sb("ident", [P, P])
        ident_r = sb("ident_r", [P, P], R32)
        mask_r = sb("mask_r", [P, P], R32)
        ones = sb("ones", [P, P])
        eps = sb("eps", [P, 1])
        par = sb("par", [P, N_PARAM])
        xstat = sb("xstat", [P, 4, 2])
        stat = sb("stat", [P, 3, 2])
        w_raw = sb("w_raw", [P, 2, T])
        w_hi = sb("w_hi", [P, 2, T], R32)
        w_lo = sb("w_lo", [P, 2, T], R32)
        row = sb("row", [P, D])
        act0 = sb("act0", [P, KD, 2, T], R32)
        with ExitStack() as s1:
            mask_f = sb("mask_f", [P, P], scope=s1)
            xin = sb("xin", [P, 2, D], scope=s1)
            xn = sb("xn", [P, 2, D], scope=s1)
            t_f = sb("t_f", [P, 2, T], scope=s1)
            u_pad = sb("u_pad", [P, KC - 1 + T], scope=s1)
            sig = sb("sig", [P, T], scope=s1)
            u_acc = sb("u_acc", [P, T], scope=s1)
            a_c = sb("a_c", [P, T], scope=s1)
            a_pad = sb("a_pad", [P, KA - 1 + T], scope=s1)
            a_acc = sb("a_acc", [P, T], scope=s1)
            a_y = sb("a_y", [P, T], scope=s1)
            v_t = sb("v_t", [P, T], scope=s1)
            q_st = sb("q_st", [P, 2, T], R32, scope=s1)
            k_st = sb("k_st", [P, 2, T], R32, scope=s1)
            v_st = sb("v_st", [P, 2, T], R32, scope=s1)
            a_st = sb("a_st", [P, 2, T], R32, scope=s1)
            u_sum = sb("u_sum", [P, T], scope=s1)
            g_st = sb("g_st", [P, 2, T], scope=s1)
        with ExitStack() as s2:
            qh = [sb(f"qh{h}", [QK_ROWS, 2, T], R32, scope=s2) for h in range(2)]
            kh = [sb(f"kh{h}", [QK_ROWS, 2, T], R32, scope=s2) for h in range(2)]
            vh = [sb(f"vh{h}", [P, 2, TB, P], R32, scope=s2) for h in range(2)]
            prob = sb("prob", [P, 2, T], scope=s2)
            pt = [sb(f"pt{u}", [P, 2, TB, 2 * P], R32, scope=s2) for u in range(2)]
            nmax = sb("nmax", [P, 2], scope=s2)
            psum_p = sb("psum_p", [P, 2], scope=s2)
            rsum = sb("rsum", [P, 2], scope=s2)
            o_st = sb("o_st", [P, 2, T], R32, scope=s2)
        act1 = sb("act1", [P, KD, 2, T], R32)
        with ExitStack() as s3:
            rstd = sb("rstd", [P, T], scope=s3)
            sq_sum = sb("sq_sum", [P, T], scope=s3)
            gin = sb("gin", [P, 2, T], scope=s3)
            part = sb("part", [P, 2, T], scope=s3)
            m_in = sb("m_in", [P, 2, T], scope=s3)
            uin = sb("uin", [P, 2, T], scope=s3)
            xc = sb("xc", [P, T], scope=s3)
            sq = sb("sq", [P, T], scope=s3)
        res = sb("res", [P, TB, D])
        xn2 = sb("xn2", [P, 2, D])
        flat1 = act1[:, :, :, :].rearrange("p k s t -> p k (s t)")
        mem_t = flat1[:, 0:2, :].rearrange("p k n -> p (k n)").rearrange("p (k s m) -> p k s m", k=KD, s=2)
        k_x = flat1[:, 2, :].rearrange("p (h s m) -> p h s m", h=XH, s=2)
        v_x = flat1[:, 3, :].rearrange("p (b s n) -> p b s n", b=MB, s=2)
        o_x = act1[:, 4:8, :, :]
        q_x = [act1[:, c, :, :] for c in (6, 7, 0, 1)]
        pt_x = sb("pt_x", [P, 2, MB, HALF], R32)

        psum = [ctx.enter_context(nc.psum_tensor(f"ps{i}", [P, 2 * HALF], F32)) for i in range(4)]

        credit = []

        def sem1(name):
            s = sem(name)
            credit.append(s)
            return s

        def done(k):
            return k + 2

        def before(k):
            return k + 1

        const_done, params_in, gain_in = sem("const_done"), sem("params_in"), sem("gain_in")
        w_loaded = [sem(f"w_loaded{s}") for s in range(2)]
        w_hi_done, w_split = sem("w_hi_done"), sem("w_split")
        gemm_done = sem("gemm_done")
        dve = Chain(sem("dve_chain"))
        const_r, pads, f_cum, r_ready, gated = (sem(n) for n in ("const_r", "pads", "f_cum", "r_ready", "gated"))
        usum_stored, pool_step = sem("usum_stored"), sem("pool_step")
        CONV_TAPS = {2: 5, 3: 6, 4: 6, 5: 7, 6: 6, 7: 1}
        assert sum(CONV_TAPS.values()) == KC
        x_loaded = [sem(f"x_loaded{s}") for s in range(2)]
        n_sq, n_root, n_rstd, n_ready = sem("n_sq"), sem("n_root"), sem("n_rstd"), sem("n_ready")
        n_trans, n_hi, n_lo = sem("n_trans"), sem("n_hi"), sem("n_lo")
        f_abs, f_exp, f_ln, f_min = sem("f_abs"), sem("f_exp"), sem("f_ln"), sem("f_min")
        f_hi, f_rows, rows_stored = sem("f_hi"), sem("f_rows"), sem("rows_stored")
        sig_ready, u_ready, u_summed = sem1("sig_ready"), sem1("u_ready"), sem1("u_summed")
        q_hi, q_lo, k_hi, k_lo = sem1("q_hi"), sem1("q_lo"), sem1("k_hi"), sem1("k_lo")
        v_copied, v_trans, v_hi, v_lo = sem1("v_copied"), sem1("v_trans"), sem1("v_hi"), sem1("v_lo")
        ac_ready, au_ready = sem1("ac_ready"), sem1("au_ready")
        y_ready, y_hi, y_lo = sem1("y_ready"), sem1("y_hi"), sem1("y_lo")
        q_stored, k_stored, v_stored = sem("q_stored"), sem("k_stored"), sem("v_stored")
        u_stored, y_stored = sem("u_stored"), sem("y_stored")
        stage_free = sem1("stage_free")
        gate_done = [sem1(f"gate_done{s}") for s in range(2)]
        gate_stored = [sem(f"gate_stored{s}") for s in range(2)]
        gate_free = [sem1(f"gate_free{s}") for s in range(2)]
        qkv_loaded = [sem(f"qkv_loaded{h}") for h in range(2)]
        v_ones = sem("v_ones")
        s_ready, m_ready = sem("s_ready"), sem("m_ready")
        p_ready = [sem1(f"p_ready{s}") for s in range(2)]
        t_done, pt_hi = sem("t_done"), sem("pt_hi")
        pt_lo = [sem1(f"pt_lo{s}") for s in range(2)]
        pv_done = [sem1(f"pv_done{s}") for s in range(2)]
        o_free = [sem1(f"o_free{s}") for s in range(2)]
        e_ready = sem("e_ready")
        o_hi, o_stored = sem1("o_hi"), sem("o_stored")
        o_stage_free = sem1("o_stage_free")
        act0_loaded, act1_loaded = sem("act0_loaded"), sem("act1_loaded")
        usum_loaded, mean_ps, mean_done = sem("usum_loaded"), sem("mean_ps"), sem("mean_done")
        g_loaded = [sem(f"g_loaded{s}") for s in range(2)]
        m_loaded = [sem(f"m_loaded{s}") for s in range(2)]
        u_loaded = [sem(f"u_loaded{s}") for s in range(2)]
        merged = [sem1(f"merged{s}") for s in range(2)]
        m_stored = [sem(f"m_stored{s}") for s in range(2)]
        part_free = [sem1(f"part_free{s}") for s in range(2)]
        xc_ready, sq_ready, sq_added = sem1("xc_ready"), sem("sq_ready"), sem("sq_added")
        var_ps, root_done, rstd_done = sem("var_ps"), sem("root_done"), sem("rstd_done")
        xc_done = sem("xc_done")
        ln_ready, zs_ready, zz_ready = sem("ln_ready"), sem("zs_ready"), sem("zz_ready")
        z_hi, z_lo = sem("z_hi"), sem("z_lo")
        mg_hi, mg_lo = sem1("mg_hi"), sem1("mg_lo")
        res_loaded, tok_done, res_added = sem("res_loaded"), sem("tok_done"), sem("res_added")
        mem_loaded = sem("mem_loaded")
        x_hi, x_lo = sem("x_hi"), sem("x_lo")
        xs_ready, xm_ready, xe_ready, xr_ready, xp_ready = (
            sem(n) for n in ("xs_ready", "xm_ready", "xe_ready", "xr_ready", "xp_ready"))
        xt_done, xpt_hi, xpt_lo, xpv_done, xo_hi, xo_lo = (
            sem(n) for n in ("xt_done", "xpt_hi", "xpt_lo", "xpv_done", "xo_hi", "xo_lo"))
        ff_sig, ff_gate, ff_prod, ff_hi, ff_lo = (sem1(n) for n in ("ff_sig", "ff_gate", "ff_prod", "ff_hi", "ff_lo"))
        d_ready = sem("d_ready")
        d_added = [sem1(f"d_added{s}") for s in range(2)]
        out_stored = [sem(f"out_stored{s}") for s in range(2)]

        def load_tile(sp, n, slot, src):
            if not isinstance(n, int) or n >= 2:
                sp.wait_ge(w_split, n - 1)
            sp.dma_start(w_raw[:, slot, :], src).then_inc(w_loaded[slot], 16)

        def split_hi(act, n, slot, loads):
            act.wait_ge(w_loaded[slot], loads * 16)
            if not isinstance(n, int) or n >= 2:
                act.wait_ge(gemm_done, n - 1)
            act.activation(w_hi[:, slot, :], w_raw[:, slot, :], ACT.Copy).then_inc(w_hi_done, 1)

        def split_lo(v, n, slot):
            v.wait_ge(w_hi_done, n + 1)
            v.tensor_tensor(w_lo[:, slot, :], w_raw[:, slot, :], w_hi[:, slot, :].bitcast(F32),
                            ALU.subtract).then_inc(w_split, 1)

        def hi_next(act, base, i=0, per=0):
            split_hi(act, base + per * i, base % 2, base // 2 + 1 + (per // 2) * i)

        def lo_next(v, base, i=0, per=0):
            split_lo(v, base + per * i, base % 2)

        def weights(slot):
            return [w[:, slot, :] for w in (w_hi, w_lo)]

        def tile_products(pe, out, act, slot, n_tok=HALF, halves=2):
            w = [t.rearrange("p (k e) -> p k e", k=KD) for t in weights(slot)]
            for kd in range(KD):
                for half in range(halves):
                    t0 = half * HALF
                    for a, b in ((HI, HI), (HI, LO), (LO, HI)):
                        last = pe.matmul(out[:, t0:t0 + n_tok], w[a][:, kd, :], act[:, kd, b, t0:t0 + n_tok],
                                         start=(kd == 0 and a == b), stop=(kd == KD - 1 and a == LO))
            return last

        def row_products(pe, out, stat_hl, slot, start, stop):
            w = weights(slot)
            for half in range(2):
                c = slice(half * HALF, (half + 1) * HALF)
                for a, b in ((HI, HI), (HI, LO), (LO, HI)):
                    last = pe.matmul(out[:, c], stat_hl[a], w[b][:, c],
                                     start=(start and a == b), stop=(stop and a == LO))
            return last

        def norm_stats(act, b, src):
            s = b % 2
            if b >= 2:
                act.wait_ge(n_lo, b - 1)
                act.wait_ge(n_rstd, b - 1)
            act.activation(psum[2 + s][:, :], src, ACT.Square, accum_out=stat[:, 0, s:s + 1]).then_inc(n_sq, 1)
            act.wait_ge(n_sq, b + 1)
            act.activation(stat[:, 1, s:s + 1], stat[:, 0, s:s + 1], ACT.Sqrt, bias=eps[:, 0:1],
                           scale=1.0 / D).then_inc(n_root, 1)

        def norm_scale(v, b, src, dst, g):
            s = b % 2
            v.wait_ge(n_root, b + 1)
            v.reciprocal(stat[:, 2, s:s + 1], stat[:, 1, s:s + 1]).then_inc(n_rstd, 1)
            v.wait_ge(n_rstd, b + 1)
            if b >= 2:
                v.wait_ge(n_trans, b - 1)
            v.scalar_tensor_tensor(dst[:, s, :], src, stat[:, 2, s:s + 1], g[:, :], ALU.mult, ALU.mult)\
             .then_inc(n_ready, 1)

        def norm_transpose(pe, b, src):
            pe.wait_ge(n_ready, b + 1)
            for kd in range(KD):
                last = pe.transpose(psum[2 + b % 2][:, kd * P:(kd + 1) * P], src[:, b % 2, kd * P:(kd + 1) * P],
                                    ident[:, :])
            last.then_inc(n_trans, 1)

        def norm_hi(act, b, dst):
            act.wait_ge(n_trans, b + 1)
            act.activation(dst[HI], psum[2 + b % 2][:, :].rearrange("p (k t) -> p k t", k=KD), ACT.Copy)\
               .then_inc(n_hi, 1)

        def norm_lo(v, b, dst):
            v.wait_ge(n_hi, b + 1)
            v.tensor_tensor(dst[LO], psum[2 + b % 2][:, :].rearrange("p (k t) -> p k t", k=KD),
                            dst[HI].bitcast(F32), ALU.subtract).then_inc(n_lo, 1)

        def token_block(act, t):
            return [act[:, :, s, t * P:(t + 1) * P] for s in (HI, LO)]

        B_X, B_X1, B_MEM, B_X2, B_OUT = 0, TB, 2 * TB, 2 * TB + MB, 3 * TB + MB

        def norm_blocks_act(act, b0, n, src, dst, ready=lambda t: None):
            for t in range(n + 1):
                if t < n:
                    ready(t)
                    norm_stats(act, b0 + t, src(t))
                if t >= 1 and dst:
                    norm_hi(act, b0 + t - 1, dst(t - 1))

        def norm_blocks_dve(v, b0, n, src, buf, g, dst):
            for t in range(n + 1):
                if t < n:
                    norm_scale(v, b0 + t, src(t), buf, g)
                if t >= 1:
                    norm_lo(v, b0 + t - 1, dst(t - 1))

        def chunks(s):
            n = s % TB + 1
            return [(0, min(4, n))] + ([(4, n)] if n > 4 else [])

        first_chunk = [sum(len(chunks(r)) for r in range(s)) for s in range(2 * TB + 1)]
        N_STEP = 2 * TB
        N_CHUNK = first_chunk[N_STEP]

        def attention_pairs(eng, body):
            with eng.Fori(0, NH // 2 - 1) as i:
                body(i, False)
            body(NH // 2 - 1, True)

        N_IT = KD // 2

        block = ctx.enter_context(nc.Block())

        @block.sync
        def _(sp):
            sp.dma_start(row[:, :], norms[0:1, :].to_broadcast([P, D])).then_inc(gain_in, 16)
            for b in range(TB):
                if b >= 2:
                    sp.wait_ge(n_ready, b - 1)
                sp.dma_start(xin[:, b % 2, :], x[b * P:(b + 1) * P, :]).then_inc(x_loaded[b % 2], 16)
                if b == 0:
                    sp.dma_start(par[:, :], params).then_inc(params_in, 16)
                if b == 1:
                    load_tile(sp, 0, 0, w_in[0])
                    load_tile(sp, 1, 1, w_in[1])
            load_tile(sp, 2, 0, w_in[2])
            with sp.Fori(0, (T_MERGE - 3) // 2) as i:
                load_tile(sp, 2 * i + 3, 1, w_in[2 * i + 3])
                load_tile(sp, 2 * i + 4, 0, w_in[2 * i + 4])
            load_tile(sp, T_MERGE, T_MERGE % 2, w_out[0])
            load_tile(sp, T_MERGE + 1, (T_MERGE + 1) % 2, w_out[1])

            for s in (q_stored, k_stored):
                sp.wait_ge(s, 32 * KD)
            for s in (v_stored, u_stored, y_stored):
                sp.wait_ge(s, 16 * KD)
            sp.wait_ge(rows_stored, 64)

            def load_head(h, head, pair):
                sp.dma_start(qh[h][:, :, :].bitcast(F32), q_s[head].rearrange("p (s t) -> p s t", s=2)).then_inc(qkv_loaded[h], 16)
                sp.dma_start(kh[h][:, :, :].bitcast(F32), k_s[head].rearrange("p (s t) -> p s t", s=2)).then_inc(qkv_loaded[h], 16)
                sp.dma_start(vh[h][:, :, :, :].bitcast(F32), v_s[pair].rearrange("p (s j c) -> p s j c", s=2, c=P))\
                  .then_inc(qkv_loaded[h], 16)

            load_head(0, 0, 0)
            load_head(1, 1, 0)
            with sp.Fori(0, NH // 2 - 1) as i:
                sp.wait_ge(pv_done[1], done(4 * i + 1))
                load_head(0, 2 * i + 2, i + 1)
                sp.wait_ge(pv_done[1], done(4 * i + 3))
                load_head(1, 2 * i + 3, i + 1)

            sp.wait_ge(o_stored, 16 * (NH // 2))

            def load_act1(kd):
                sp.dma_start(act1[:, kd, :, :].bitcast(F32), b_s[kd].rearrange("p (s t) -> p s t", s=2))\
                  .then_inc(act1_loaded, 16)

            def load_chunk(br, e, j):
                if br < 2:
                    sp.dma_start(uin[:, j, :], u_s[e]).then_inc(u_loaded[j], 16)
                sp.dma_start(gin[:, j, :], g_s[e + KD * br]).then_inc(g_loaded[j], 16)
                if br:
                    sp.dma_start(m_in[:, j, :], m_s[e]).then_inc(m_loaded[j], 16)

            def merge_step(br, i, j):
                n = T_MERGE + KD * br + j + 2
                at_end = br == 2 and isinstance(i, int)
                load_tile(sp, 2 * i + n, n % 2, w_o[j] if at_end else w_out[2 * i + KD * br + j + 2])
                if br == 0:
                    load_act1(2 * i + j)
                sp.wait_ge(merged[j], done(N_IT * br + i))
                if not isinstance(i, int):
                    load_chunk(br, 2 * i + j + 2, j)
                elif br < 2:
                    sp.wait_ge(m_stored[j], 16 * N_IT * (br + 1))
                    load_chunk(br + 1, j, j)

            for j in range(2):
                load_chunk(0, j, j)
            for br in range(3):
                with sp.Fori(0, N_IT - 1) as i:
                    for j in range(2):
                        merge_step(br, i, j)
                for j in range(2):
                    merge_step(br, N_IT - 1, j)
            sp.wait_ge(mg_lo, done(KD - 1))
            for t in range(TB):
                sp.dma_start(res[:, t, :], x[t * P:(t + 1) * P, :]).then_inc(res_loaded, 16)
            sp.dma_start(row[:, :], norms[1:2, :].to_broadcast([P, D])).then_inc(gain_in, 16)
            tiles = [w_o[kd] for _ in range(2) for kd in range(KD)]
            tiles += [w_xq[0], w_xq[1]] + [w_xk[h] for h in range(XH)] + [w_xv[c] for c in range(KD // 2)]
            tiles += [w_xq[2], w_xq[3]] + [w_xo[kd] for _ in range(2) for kd in range(XH)]
            tiles += [w_gu[0], w_gu[1]]
            assert T_O + len(tiles) == T_FF + 2
            for n in range(T_O + 2, T_FF + 2):
                if n == T_XQ + 2:
                    sp.wait_ge(n_trans, B_X1 + TB)
                    for b in range(MB):
                        sp.dma_start(xn2[:, b, :], mem[b * P:(b + 1) * P, :]).then_inc(mem_loaded, 16)
                    sp.wait_ge(n_ready, B_MEM)
                    sp.dma_start(row[:, :], norms[2:3, :].to_broadcast([P, D])).then_inc(gain_in, 16)
                if n == T_XO:
                    sp.wait_ge(n_ready, B_X2)
                    sp.dma_start(row[:, :], norms[3:4, :].to_broadcast([P, D])).then_inc(gain_in, 16)
                load_tile(sp, n, n % 2, tiles[n - T_O])
            with sp.Fori(0, (NF - 2) // 2) as i:
                for j in range(6):
                    n = T_FF + 2 + j
                    src = (w_gu[4 * i + 2 + j] if j < 2 else w_down[2 * i] if j == 2 else
                           w_gu[4 * i + 1 + j] if j < 5 else w_down[2 * i + 1])
                    load_tile(sp, 6 * i + n, n % 2, src)
            for j, src in enumerate((w_gu[2 * NF - 2], w_gu[2 * NF - 1], w_down[NF - 2], w_down[NF - 1])):
                n = T_END - 4 + j
                load_tile(sp, n, n % 2, src)
            sp.wait_ge(n_ready, B_OUT)
            sp.dma_start(row[:, :], norms[4:5, :].to_broadcast([P, D])).then_inc(gain_in, 16)
            for t in range(TB):
                sp.wait_ge(n_ready, B_OUT + t + 1)
                sp.dma_start(out[t * P:(t + 1) * P, :], xn2[:, t % 2, :]).then_inc(out_stored[t % 2], 16)
            for s in range(2):
                sp.wait_ge(out_stored[s], 16 * TB // 2)

        @block.gpsimd
        def _(pool):
            def wait(s, value):
                pool.wait_ge(s, value)
                pool.sem_inc(pool_step, 1)

            for s in credit:
                pool.sem_inc(s, 1)
            pool.memset(ident[:, :], 0.0).then_inc(const_done, 1)
            pool.memset(mask_f[:, :], 0.0).then_inc(const_done, 1)
            pool.memset(ones[:, :], 1.0).then_inc(const_done, 1)
            pool.memset(eps[:, :], EPS).then_inc(const_done, 1)
            pool.wait_ge(const_done, 4)
            pool.affine_select(out=ident[:, :], in_=ident[:, :], compare_op=ALU.not_equal, fill=1.0, base=0,
                               pattern=[[-1, P]], channel_multiplier=1).then_inc(const_done, 1)
            pool.affine_select(out=mask_f[:, :], in_=mask_f[:, :], compare_op=ALU.is_ge, fill=MASKED, base=0,
                               pattern=[[-1, P]], channel_multiplier=1).then_inc(const_done, 1)

            pool.wait_ge(f_rows, 3)
            r = slice(0, NH)
            for dst, src, at in ((q_s, a_st, DH), (q_s, q_st, DH + 1), (k_s, k_st, DH), (k_s, a_st, DH + 1)):
                pool.dma_start(dst[:, at, :], src[r, :, :].rearrange("p s t -> p (s t)").bitcast(F32)).then_inc(rows_stored, 16)

            with pool.Fori(0, KD) as i:
                for lo_sem, st, dst, stored in ((q_lo, q_st, q_s, q_stored), (k_lo, k_st, k_s, k_stored)):
                    wait(lo_sem, done(i))
                    for h in range(2):
                        pool.dma_start(dst[2 * i + h, 0:DH, :].rearrange("p (s t) -> p s t", s=2),
                                       st[h * DH:(h + 1) * DH, :, :].bitcast(F32)).then_inc(stored, 16)
                wait(v_lo, done(i))
                pool.dma_start(v_s[i].rearrange("p (s t) -> p s t", s=2), v_st[:, :, :].bitcast(F32)).then_inc(v_stored, 16)
                wait(u_summed, done(i))
                pool.dma_start(u_s[i], u_acc[:, :]).then_inc(u_stored, 16)
                wait(y_lo, done(i))
                pool.dma_start(a_s[i].rearrange("p (s t) -> p s t", s=2), a_st[:, :, :].bitcast(F32)).then_inc(y_stored, 16)
                for s, by in ((q_stored, 32), (k_stored, 32), (v_stored, 16), (u_stored, 16), (y_stored, 16)):
                    wait(s, by * i + by)
                pool.sem_inc(stage_free, 1)
            with pool.Fori(0, 3 * KD // 2) as i:
                for j in range(2):
                    wait(gate_done[j], done(i))
                    pool.dma_start(g_s[2 * i + j], g_st[:, j, :]).then_inc(gate_stored[j], 16)
                for j in range(2):
                    wait(gate_stored[j], 16 * i + 16)
                    pool.sem_inc(gate_free[j], 1)

            wait(gemm_done, T_MERGE)
            wait(y_stored, 16 * KD)
            wait(qkv_loaded[1], 48)
            for kd in range(KD):
                pool.dma_start(act0[:, kd, :, :].bitcast(F32), a_s[kd].rearrange("p (s t) -> p s t", s=2)).then_inc(act0_loaded, 16)

            with pool.Fori(0, NH // 2) as i:
                wait(o_free[1], done(2 * i + 1))
                pool.dma_start(b_s[i].rearrange("p (s t) -> p s t", s=2), o_st[:, :, :].bitcast(F32)).then_inc(o_stored, 16)
                wait(o_stored, 16 * i + 16)
                pool.sem_inc(o_stage_free, 1)

            for br in range(2):
                if br == 1:
                    pool.wait_ge(rstd_done, 1)
                with pool.Fori(0, N_IT) as i:
                    for j in range(2):
                        if br == 1:
                            wait(u_loaded[j], 16 * i + 16 * N_IT + 16)
                            pool.tensor_tensor(uin[:, j, :], uin[:, j, :], row[:, :], ALU.subtract).then_inc(xc_done, 1)
                            wait(xc_done, 2 * i + j + 1)
                            pool.tensor_tensor(uin[:, j, :], uin[:, j, :], rstd[:, :], ALU.mult).then_inc(ln_ready, 1)
                    for j in range(2):
                        wait(merged[j], done(N_IT * br + i))
                        pool.dma_start(m_s[2 * i + j], part[:, j, :]).then_inc(m_stored[j], 16)
                    for j in range(2):
                        wait(m_stored[j], 16 * i + 16 * N_IT * br + 16)
                        pool.sem_inc(part_free[j], 1)

        @block.tensor
        def _(pe):
            pe.wait_ge(const_done, 6)
            for t in range(TB):
                norm_transpose(pe, B_X + t, xn)
            pe.wait_ge(n_lo, B_X + TB)

            pe.wait_ge(w_split, T_FORGET + 1)
            tile_products(pe, psum[0], act0, T_FORGET % 2).then_inc(gemm_done, 1)
            pe.wait_ge(f_min, 1)
            pe.wait_ge(f_abs, 1)

            pair_free = [(au_ready, before), (y_ready, before), (ac_ready, before), (u_ready, done),
                         (sig_ready, done), (q_lo, done), (k_lo, done), (v_copied, done)]
            with pe.Fori(0, KD) as i:
                for j in range(8):
                    pe.wait_ge(w_split, 8 * i + T_BRANCH + j + 1)
                    s, when = pair_free[j]
                    pe.wait_ge(s, when(i))
                    tile_products(pe, psum[j % 3], act0, (T_BRANCH + j) % 2).then_inc(gemm_done, 1)
                    if j == 5:
                        pe.wait_ge(v_copied, done(i))
                        pe.wait_ge(v_lo, before(i))
                        for b in range(TB):
                            last = pe.transpose(psum[3][:, b * P:(b + 1) * P], v_t[:, b * P:(b + 1) * P], ident[:, :])
                        last.then_inc(v_trans, 1)

            pe.wait_ge(ac_ready, done(KD - 1))
            pe.wait_ge(v_lo, done(KD - 1))
            with pe.Fori(0, 3 * KD // 2) as i:
                for j in range(2):
                    pe.wait_ge(w_split, 2 * i + T_GATE + j + 1)
                    pe.wait_ge(gate_done[j], before(i))
                    tile_products(pe, psum[2 + j], act0, (T_GATE + j) % 2).then_inc(gemm_done, 1)

            def scores(s):
                h, qb, ps = s // TB % 2, s % TB, psum[s % 2]
                n = (qb + 1) * P
                q = slice(qb * P, n)
                for c in range(0, n, HALF):
                    k = slice(c, min(n, c + HALF))
                    for a, b in ((HI, HI), (HI, LO), (LO, HI)):
                        last = pe.matmul(ps[:, k], qh[h][:, a, q], kh[h][:, b, k], start=(a == b),
                                         stop=(a == LO and k.stop < n))
                last = pe.matmul(ps[:, q], ident_r[:, :], mask_r[:, :], start=False, stop=True)
                last.then_inc(s_ready, 1)

            def transposes(i, s):
                for c, (j0, j1) in enumerate(chunks(s), first_chunk[s]):
                    pe.wait_ge(pt_lo[c % 2], before(N_CHUNK // 2 * i + c // 2))
                    for j in range(j0, j1):
                        last = pe.transpose(psum[2][:, c % 2 * HALF + (j - j0) * P:c % 2 * HALF + (j - j0 + 1) * P],
                                            prob[:, s % 2, j * P:(j + 1) * P], ident[:, :])
                    last.then_inc(t_done, 1)

            def outputs(i, u):
                h, c, g = u // 4, first_chunk[2 * u + 2] - 1, u // 2
                pe.wait_ge(pt_lo[c % 2], done(N_CHUNK // 2 * i + c // 2))
                if u % 2 == 0:
                    pe.wait_ge(o_free[g % 2], before(2 * i + g // 2))
                o0 = g % 2 * HALF + u % 2 * 2 * P
                last_j = 2 * (u % 4) + 1
                for j in range(last_j + 1):
                    c0 = P if j == last_j else 0
                    for a, b in ((HI, HI), (HI, LO), (LO, HI)):
                        last = pe.matmul(psum[3][:, o0 + c0:o0 + 2 * P], vh[h][:, a, j, :],
                                         pt[u % 2][:, b, j, c0:2 * P], start=(j == 0 and a == b),
                                         stop=(j == last_j and a == LO))
                last.then_inc(pv_done[u % 2], 1)

            pe.wait_ge(au_ready, done(KD - 1))
            pe.wait_ge(y_ready, done(KD - 1))
            pe.wait_ge(u_summed, done(KD - 1))
            for half in range(2):
                c = slice(half * HALF, (half + 1) * HALF)
                last = pe.matmul(psum[0][:, c], ones[:, :], u_sum[:, c], start=True, stop=True)
            last.then_inc(mean_ps, 1)
            pe.wait_ge(mean_done, 1)
            for s in gate_done:
                pe.wait_ge(s, done(3 * KD // 2 - 1))
            pe.wait_ge(qkv_loaded[0], 48)
            scores(0)
            scores(1)

            def pair(i, last):
                for s in range(N_STEP):
                    pe.wait_ge(p_ready[s % 2], done(N_STEP // 2 * i + s // 2))
                    transposes(i, s)
                    if not (last and s + 2 >= N_STEP):
                        if s + 2 == TB:
                            pe.wait_ge(qkv_loaded[1], 48 * i + 48)
                        if s + 2 == N_STEP:
                            pe.wait_ge(qkv_loaded[0], 48 * i + 96)
                        scores(s + 2)
                    if s % 2:
                        outputs(i, s // 2)

            attention_pairs(pe, pair)

            for s in o_free:
                pe.wait_ge(s, done(2 * (NH // 2) - 1))
            for br, act in enumerate((act0, act1, act0)):
                if br == 0:
                    pe.wait_ge(act0_loaded, 16 * KD)
                if br == 1:
                    pe.wait_ge(sq_added, KD + 1)
                    for half in range(2):
                        c = slice(half * HALF, (half + 1) * HALF)
                        last = pe.matmul(psum[3][:, c], ones[:, :], sq_sum[:, c], start=True, stop=True)
                    last.then_inc(var_ps, 1)
                    pe.wait_ge(act1_loaded, 16 * KD)
                if br == 2:
                    pe.wait_ge(z_lo, KD)
                with pe.Fori(0, N_IT) as i:
                    for j in range(2):
                        n = T_MERGE + KD * br + j
                        pe.wait_ge(w_split, 2 * i + n + 1)
                        pe.wait_ge(merged[j], before(N_IT * br + i))
                        tile_products(pe, psum[j], act, n % 2).then_inc(gemm_done, 1)

            def token_gemm(n0, n_kd, stationary, free, first):
                for h in range(2):
                    for kd in range(n_kd):
                        n = n0 + n_kd * h + kd
                        pe.wait_ge(w_split, n + 1)
                        for t in range(4):
                            if kd == 0 and h == 0:
                                free(t)
                            if kd == 0 and h == 1:
                                pe.wait_ge(res_added, first + t + 1)
                            last = row_products(pe, psum[t], stationary(kd, 4 * h + t), n % 2,
                                                kd == 0, kd == n_kd - 1)
                            if kd == n_kd - 1 and t < 3:
                                last.then_inc(tok_done, 1)
                        last.then_inc(gemm_done, 1)

            def blocks_of(act, kd, t):
                return [act[:, kd, s, t * P:(t + 1) * P] for s in (HI, LO)]

            def free_o(t):
                if t < 2:
                    pe.wait_ge(merged[t], done(3 * N_IT - 1))
                if t == 3:
                    pe.wait_ge(root_done, 1)
                if t == 0:
                    pe.wait_ge(mg_lo, done(KD - 1))

            token_gemm(T_O, KD, lambda kd, t: blocks_of(act1, kd, t), free_o, 0)
            for t in range(TB):
                norm_transpose(pe, B_X1 + t, xn2)
            pe.wait_ge(n_lo, B_X1 + TB)

            def x_project(n, k, act, n_tok, halves):
                pe.wait_ge(w_split, n + 1)
                pe.wait_ge(x_lo, k - 1) if k >= 2 else pe.wait_ge(res_added, TB)
                tile_products(pe, psum[k % 2], act, n % 2, n_tok, halves).then_inc(gemm_done, 1)

            x_project(T_XQ, 0, act0, HALF, 2)
            x_project(T_XQ + 1, 1, act0, HALF, 2)
            for b in range(MB):
                norm_transpose(pe, B_MEM + b, xn2)
            pe.wait_ge(n_lo, B_MEM + MB)
            for h in range(XH):
                x_project(T_XK + h, 2 + h, mem_t, N_MEM, 1)
            for c in range(KD // 2):
                pe.wait_ge(w_split, T_XV + c + 1)
                w = [t.rearrange("p (k e) -> p k e", k=2) for t in weights((T_XV + c) % 2)]
                for b in range(MB):
                    for k in range(2):
                        for a, p in ((HI, HI), (HI, LO), (LO, HI)):
                            last = pe.matmul(psum[2][:, b * HALF:(b + 1) * HALF],
                                             mem_t[:, 2 * c + k, a, b * P:(b + 1) * P], w[p][:, k, :],
                                             start=(c == 0 and k == 0 and a == p),
                                             stop=(c == KD // 2 - 1 and k == 1 and a == LO))
                last.then_inc(gemm_done, 1)
            pe.wait_ge(x_lo, 2 + XH + 1)
            x_project(T_XQ2, 2 + XH + 1, act0, HALF, 2)
            x_project(T_XQ2 + 1, 2 + XH + 2, act0, HALF, 2)

            def x_scores(m):
                h, t = m // TB, m % TB
                for a, b in ((HI, HI), (HI, LO), (LO, HI)):
                    last = pe.matmul(psum[0][:, m % 2 * HALF:m % 2 * HALF + N_MEM], q_x[h][:, a, t * P:(t + 1) * P],
                                     k_x[:, h, b, :], start=(a == b), stop=(a == LO))
                last.then_inc(xs_ready, 1)

            def x_outputs(g):
                h = g // 2
                pe.wait_ge(xpt_lo, 4 * g + 4)
                if g >= 2:
                    pe.wait_ge(xo_lo, g - 1)
                for b in range(MB):
                    for a, p in ((HI, HI), (HI, LO), (LO, HI)):
                        last = pe.matmul(psum[3][:, g % 2 * HALF:(g % 2 + 1) * HALF], v_x[:, b, a, h * XD:(h + 1) * XD],
                                         pt_x[:, p, b, :], start=(b == 0 and a == p), stop=(b == MB - 1 and a == LO))
                last.then_inc(xpv_done, 1)

            pe.wait_ge(x_lo, 2 + XH + 1 + 2)
            x_scores(0)
            x_scores(1)
            for m in range(XH * TB):
                pe.wait_ge(xp_ready, m + 1)
                if m >= 2:
                    pe.wait_ge(xpt_lo, m - 1)
                for b in range(MB):
                    last = pe.transpose(psum[1][:, m % 2 * HALF + b * P:m % 2 * HALF + (b + 1) * P],
                                        xn2[:, m % 2, b * P:(b + 1) * P], ident[:, :])
                last.then_inc(xt_done, 1)
                if m + 2 < XH * TB:
                    x_scores(m + 2)
                if m % 4 == 3:
                    x_outputs(m // 4)

            def free_xo(t):
                if t == 0:
                    pe.wait_ge(xo_lo, 2 * XH)

            token_gemm(T_XO, XH, lambda kd, t: blocks_of(o_x, kd, t), free_xo, TB)
            for t in range(TB):
                norm_transpose(pe, B_X2 + t, xn2)
            pe.wait_ge(n_lo, B_X2 + TB)

            def ff_up(f, n, slot, wait=True):
                pe.wait_ge(w_split, n + 1)
                pe.wait_ge(ff_gate, before(f))
                tile_products(pe, psum[0], act0, slot).then_inc(gemm_done, 1)
                pe.wait_ge(w_split, n + 2)
                pe.wait_ge(ff_prod, before(f))
                tile_products(pe, psum[1], act0, 1 - slot).then_inc(gemm_done, 1)

            def ff_down(f, fs, n, slot):
                pe.wait_ge(w_split, n + 1)
                pe.wait_ge(ff_lo, done(f))
                for t in range(TB):
                    pe.wait_ge(d_added[t % 2], before(4 * f + t // 2))
                    last = row_products(pe, psum[2 + t % 2], blocks_of(act1, fs, t), slot, True, True)
                    if t < TB - 1:
                        last.then_inc(d_ready, 1)
                last.then_inc(gemm_done, 1)

            ff_up(0, T_FF, T_FF % 2)
            with pe.Fori(0, (NF - 2) // 2) as i:
                for r in range(2):
                    n = T_FF + 2 + 3 * r
                    ff_up(2 * i + 1 + r, 6 * i + n, n % 2)
                    ff_down(2 * i + r, r, 6 * i + n + 2, n % 2)
            ff_up(NF - 1, T_END - 4, T_END % 2)
            ff_down(NF - 2, (NF - 2) % 2, T_END - 2, T_END % 2)
            ff_down(NF - 1, (NF - 1) % 2, T_END - 1, (T_END - 1) % 2)

        @block.scalar
        def _(act):
            act.wait_ge(const_done, 6)
            act.activation(ident_r[:, :], ident[:, :], ACT.Copy).then_inc(const_r, 1)
            act.activation(mask_r[:, :], mask_f[:, :], ACT.Copy).then_inc(const_r, 1)

            def x_ready(t):
                act.wait_ge(x_loaded[t % 2], 16 * (t // 2 + 1))
            norm_blocks_act(act, B_X, TB, lambda t: xin[:, t % 2, :], lambda t: token_block(act0, t), x_ready)

            hi_next(act, T_FORGET)
            hi_next(act, T_FORGET + 1)
            r = slice(0, NH)
            act.wait_ge(gemm_done, T_FORGET + 1)
            act.wait_ge(params_in, 16)
            act.activation(t_f[r, 0, :], psum[0][r, :], ACT.Abs, bias=par[r, C_BF:C_BF + 1]).then_inc(f_abs, 1)
            act.wait_ge(f_abs, 1)
            act.activation(t_f[r, 1, :], t_f[r, 0, :], ACT.Exp, scale=-1.0).then_inc(f_exp, 1)
            act.wait_ge(f_exp, 1)
            act.activation(t_f[r, 0, :], t_f[r, 1, :], ACT.Ln, bias=ones[r, 0:1]).then_inc(f_ln, 1)
            act.wait_ge(f_cum, 1)
            act.activation(q_st[r, HI, :], a_y[r, :], ACT.Copy).then_inc(f_hi, 1)
            act.activation(k_st[r, HI, :], a_y[r, :], ACT.Copy, scale=-1.0).then_inc(f_hi, 1)
            act.wait_ge(rows_stored, 64)

            with act.Fori(0, KD) as i:
                for j in range(8):
                    hi_next(act, T_BRANCH + j + 1, i, 8)
                    if j >= 2:
                        act.wait_ge(gemm_done, 8 * i + T_BRANCH + j)
                    if j == 2:
                        act.wait_ge(u_ready, before(i))
                        act.activation(sig[:, :], psum[1][:, :], ACT.Sigmoid).then_inc(sig_ready, 1)
                    if j == 3:
                        act.wait_ge(stage_free, before(i))
                        act.activation(q_st[:, HI, :], psum[2][:, :], ACT.Copy, scale=DH ** -0.5).then_inc(q_hi, 1)
                    if j == 4:
                        act.wait_ge(stage_free, before(i))
                        act.activation(k_st[:, HI, :], psum[0][:, :], ACT.Copy).then_inc(k_hi, 1)
                    if j == 5:
                        act.wait_ge(v_trans, before(i))
                        act.activation(v_t[:, :], psum[1][:, :], ACT.Copy).then_inc(v_copied, 1)
                    if j == 6:
                        act.wait_ge(au_ready, before(i))
                        act.activation(a_c[:, :], psum[2][:, :], ACT.Copy).then_inc(ac_ready, 1)
                        act.wait_ge(v_trans, done(i))
                        act.wait_ge(stage_free, before(i))
                        act.activation(v_st[:, HI, :], psum[3][:, :], ACT.Copy).then_inc(v_hi, 1)
                act.wait_ge(y_ready, done(i))
                act.wait_ge(stage_free, before(i))
                act.activation(a_st[:, HI, :], a_y[:, :], ACT.Copy).then_inc(y_hi, 1)

            with act.Fori(0, 3 * KD // 2) as i:
                for j in range(2):
                    hi_next(act, T_GATE + j + 1, i, 2)
                    act.wait_ge(gemm_done, 2 * i + T_GATE + j + 1)
                    act.wait_ge(gate_free[j], before(i))
                    act.activation(g_st[:, j, :], psum[2 + j][:, :], ACT.Sigmoid,
                                   bias=par[:, bass.ds(2 * i + (C_BGATE + j), 1)]).then_inc(gate_done[j], 1)

            def exps(i, s):
                n = (s % TB + 1) * P
                act.wait_ge(m_ready, N_STEP * i + s + 1)
                act.activation(prob[:, s % 2, 0:n], psum[s % 2][:, 0:n], ACT.Exp, bias=nmax[:, s % 2:s % 2 + 1],
                               accum_out=psum_p[:, s % 2:s % 2 + 1]).then_inc(e_ready, 1)

            act.wait_ge(mean_ps, 1)
            act.activation(row[:, :], psum[0][:, :], ACT.Copy, scale=1.0 / D).then_inc(mean_done, 1)
            exps(0, 0)
            for stored in gate_stored:
                act.wait_ge(stored, 16 * (3 * KD // 2))

            def outputs_hi(i, g):
                act.wait_ge(pv_done[1], done(4 * i + g))
                r, c = slice(g // 2 * DH, (g // 2 + 1) * DH), slice(g % 2 * HALF, (g % 2 + 1) * HALF)
                act.activation(o_st[r, HI, c], psum[3][r, c], ACT.Copy).then_inc(o_hi, 1)

            def pair(i, last):
                for s in range(N_STEP):
                    if not (last and s == N_STEP - 1):
                        exps(i, s + 1)
                    if s == 4:
                        act.wait_ge(o_stage_free, before(i))
                    if s % 4 == 0 and s:
                        outputs_hi(i, s // 4 - 1)
                    u, q0 = s // 2, s % 2 * P
                    act.wait_ge(pv_done[u % 2], before(4 * i + u // 2))
                    for c, (j0, j1) in enumerate(chunks(s), first_chunk[s]):
                        act.wait_ge(t_done, N_CHUNK * i + c + 1)
                        act.activation(pt[u % 2][:, HI, j0:j1, q0:q0 + P],
                                       psum[2][:, c % 2 * HALF:c % 2 * HALF + (j1 - j0) * P]
                                       .rearrange("p (j q) -> p j q", q=P), ACT.Copy).then_inc(pt_hi, 1)
                outputs_hi(i, 3)

            attention_pairs(act, pair)

            for br in range(3):
                if br == 1:
                    act.wait_ge(var_ps, 1)
                    act.activation(rstd[:, :], psum[3][:, :], ACT.Sqrt, bias=eps[:, 0:1], scale=1.0 / D)\
                       .then_inc(root_done, 1)
                with act.Fori(0, N_IT) as i:
                    for j in range(2):
                        hi_next(act, T_MERGE + KD * br + j + 1, i, 2)
                        if br == 0:
                            act.wait_ge(xc_ready, done(2 * i + j))
                            act.activation(sq[:, :], xc[:, :], ACT.Square).then_inc(sq_ready, 1)
                        if br == 1:
                            act.wait_ge(ln_ready, 2 * i + j + 1)
                            act.activation(xc[:, :], uin[:, j, :], ACT.Sigmoid,
                                           bias=par[:, bass.ds(2 * i + (C_LNB + j), 1)],
                                           scale=par[:, bass.ds(2 * i + (C_LNG + j), 1)]).then_inc(zs_ready, 1)
                            act.wait_ge(zz_ready, 2 * i + j + 1)
                            act.activation(act0[:, 2 * i + j, HI, :], sq[:, :], ACT.Copy).then_inc(z_hi, 1)
                        if br == 2:
                            act.wait_ge(merged[j], done(2 * N_IT + i))
                            act.activation(act1[:, 2 * i + j, HI, :], part[:, j, :], ACT.Copy).then_inc(mg_hi, 1)

            for n in range(T_O + 1, T_XQ + 1):
                hi_next(act, n)

            def res_done(first):
                return lambda t: act.wait_ge(res_added, first + max(t + 1, TB - 1 + t % 2))
            norm_blocks_act(act, B_X1, TB, lambda t: res[:, t, :], lambda t: token_block(act0, t), res_done(0))

            def mem_ready(t):
                act.wait_ge(mem_loaded, 16 * MB)
            mem_parts = [[mem_t[:, :, s, b * P:(b + 1) * P] for s in (HI, LO)] for b in range(MB)]

            def x_evacuate(k, gemms, dst, src):
                act.wait_ge(gemm_done, gemms)
                act.activation(dst[HI], src, ACT.Copy).then_inc(x_hi, 1)

            hi_next(act, T_XQ + 1)
            norm_blocks_act(act, B_MEM, MB, lambda t: xn2[:, t, :], None, mem_ready)
            hi_next(act, T_XQ + 2)
            x_evacuate(0, T_XQ + 1, [q_x[0][:, HI, :]], psum[0][:, :])
            hi_next(act, T_XQ + 3)
            x_evacuate(1, T_XQ + 2, [q_x[1][:, HI, :]], psum[1][:, :])
            for b in range(MB):
                norm_hi(act, B_MEM + b, mem_parts[b])
            for h in range(XH):
                x_evacuate(2 + h, T_XK + h + 1, [k_x[:, h, HI, :]], psum[h % 2][:, 0:N_MEM])
                hi_next(act, T_XK + h + 2)
            for c in range(KD // 2):
                if c < KD // 2 - 1:
                    hi_next(act, T_XV + c + 2)
            x_evacuate(6, T_XV + KD // 2, [v_x[:, :, HI, :]], psum[2][:, :].rearrange("p (b n) -> p b n", b=MB))
            hi_next(act, T_XQ2 + 1)
            act.wait_ge(x_lo, 7)
            x_evacuate(7, T_XQ2 + 1, [q_x[2][:, HI, :]], psum[(2 + XH + 1) % 2][:, :])
            hi_next(act, T_XO)
            x_evacuate(8, T_XQ2 + 2, [q_x[3][:, HI, :]], psum[(2 + XH + 2) % 2][:, :])
            hi_next(act, T_XO + 1)

            def x_exp(m):
                act.wait_ge(xm_ready, m + 1)
                if m >= 2:
                    act.wait_ge(xt_done, m - 1)
                act.activation(xn2[:, m % 2, 0:N_MEM], psum[0][:, m % 2 * HALF:m % 2 * HALF + N_MEM], ACT.Exp,
                               bias=xstat[:, 1, m % 2:m % 2 + 1], scale=XD ** -0.5,
                               accum_out=xstat[:, 2, m % 2:m % 2 + 1]).then_inc(xe_ready, 1)

            x_exp(0)
            for m in range(XH * TB):
                if m + 1 < XH * TB:
                    x_exp(m + 1)
                act.wait_ge(xt_done, m + 1)
                if m >= 4:
                    act.wait_ge(xpv_done, m // 4)
                c0 = m % 4 * P
                act.activation(pt_x[:, HI, :, c0:c0 + P],
                               psum[1][:, m % 2 * HALF:m % 2 * HALF + N_MEM].rearrange("p (b t) -> p b t", b=MB),
                               ACT.Copy).then_inc(xpt_hi, 1)
                if m % 4 == 3:
                    g = m // 4
                    act.wait_ge(xpv_done, g + 1)
                    act.activation(o_x[:, g // 2, HI, g % 2 * HALF:(g % 2 + 1) * HALF],
                                   psum[3][:, g % 2 * HALF:(g % 2 + 1) * HALF], ACT.Copy).then_inc(xo_hi, 1)

            for n in range(T_XO + 2, T_FF + 1):
                hi_next(act, n)
            norm_blocks_act(act, B_X2, TB, lambda t: res[:, t, :], lambda t: token_block(act0, t), res_done(TB))

            def ff_sigmoid(f, gemms):
                act.wait_ge(gemm_done, gemms)
                act.wait_ge(ff_lo, before(f))
                act.activation(xn2[:, 0, :], psum[0][:, :], ACT.Sigmoid).then_inc(ff_sig, 1)

            def ff_high(f, fs):
                act.wait_ge(ff_prod, done(f))
                act.activation(act1[:, fs, HI, :], xn2[:, 0, :], ACT.Copy).then_inc(ff_hi, 1)

            hi_next(act, T_FF + 1)
            ff_sigmoid(0, T_FF + 1)
            hi_next(act, T_FF + 2)
            with act.Fori(0, (NF - 2) // 2) as i:
                for r in range(2):
                    n = T_FF + 2 + 3 * r
                    hi_next(act, n + 1, i, 6)
                    ff_high(2 * i + r, r)
                    hi_next(act, n + 2, i, 6)
                    ff_sigmoid(2 * i + 1 + r, 6 * i + n + 1)
                    hi_next(act, n + 3, i, 6)
            n = T_END - 4
            hi_next(act, n + 1)
            ff_high(NF - 2, (NF - 2) % 2)
            hi_next(act, n + 2)
            ff_sigmoid(NF - 1, n + 1)
            hi_next(act, n + 3)
            ff_high(NF - 1, (NF - 1) % 2)

            def block_done(t):
                act.wait_ge(d_added[t % 2], done(4 * (NF - 1) + t // 2))
            for t in range(TB):
                block_done(t)
                s = t % 2
                if t >= 2:
                    act.wait_ge(n_rstd, B_OUT + t - 1)
                act.activation(psum[s][:, :], res[:, t, :], ACT.Square, accum_out=stat[:, 0, s:s + 1]).then_inc(n_sq, 1)
                act.wait_ge(n_sq, B_OUT + t + 1)
                act.activation(stat[:, 1, s:s + 1], stat[:, 0, s:s + 1], ACT.Sqrt, bias=eps[:, 0:1], scale=1.0 / D)\
                   .then_inc(n_root, 1)

        @block.vector
        def _(v):
            v.wait_ge(gain_in, 16)
            norm_blocks_dve(v, B_X, TB, lambda t: xin[:, t % 2, :], xn, row, lambda t: token_block(act0, t))
            v.memset(u_pad[:, 0:KC - 1], 0.0).then_inc(pads, 1)
            v.memset(a_pad[:, 0:KA - 1], 0.0).then_inc(pads, 1)
            v.memset(u_sum[:, :], 0.0).then_inc(pads, 1)

            r = slice(0, NH)
            lo_next(v, T_FORGET)
            lo_next(v, T_FORGET + 1)
            v.memset(v_t[r, :], 1.0).then_inc(pads, 1)
            v.memset(a_st[r, HI, :].bitcast(F32), 1.0).then_inc(f_rows, 1)
            v.memset(a_st[r, LO, :].bitcast(F32), 0.0).then_inc(f_rows, 1)
            v.wait_ge(gemm_done, T_FORGET + 1)
            v.wait_ge(params_in, 16)
            v.wait_ge(f_abs, 1)
            v.tensor_scalar(a_c[r, :], psum[0][r, :], par[r, C_BF:C_BF + 1], 0.0, ALU.add, ALU.min).then_inc(f_min, 1)
            v.wait_ge(f_min, 1)
            v.wait_ge(f_ln, 1)
            dve.link(v, v.tensor_tensor(a_acc[r, :], a_c[r, :], t_f[r, 0, :], ALU.subtract))
            v.wait_ge(pads, 4)
            v.tensor_tensor_scan(a_y[r, :], v_t[r, :], a_acc[r, :], 0.0, ALU.mult, ALU.add).then_inc(f_cum, 1)
            v.wait_ge(f_cum, 1)
            v.wait_ge(f_hi, 2)
            dve.link(v, v.tensor_tensor(q_st[r, LO, :], a_y[r, :], q_st[r, HI, :].bitcast(F32), ALU.subtract))
            v.scalar_tensor_tensor(k_st[r, LO, :], a_y[r, :], -1.0, k_st[r, HI, :].bitcast(F32), ALU.mult,
                                   ALU.subtract).then_inc(f_rows, 1)

            with v.Fori(0, KD) as i:
                dve.enter(i, KC + KA)

                def conv_taps(count, k0, pad, out, width, col, bias_col):
                    for k in range(k0, k0 + count):
                        w = par[:, bass.ds(width * i + (col + k), 1)]
                        if k == 0 and bias_col is not None:
                            ins = v.tensor_scalar(out[:, :], pad[:, 0:T], w, par[:, bass.ds(i + bias_col, 1)],
                                                  ALU.mult, ALU.add)
                        elif k == 0:
                            ins = v.tensor_scalar(out[:, :], pad[:, 0:T], w, None, ALU.mult)
                        else:
                            ins = v.scalar_tensor_tensor(out[:, :], pad[:, k:k + T], w, out[:, :], ALU.mult, ALU.add)
                        dve.link(v, ins)

                taps = 0
                for j in range(8):
                    lo_next(v, T_BRANCH + j + 1, i, 8)
                    if j == 2:
                        v.wait_ge(sig_ready, done(i))
                        v.tensor_tensor(u_pad[:, KC - 1:], psum[0][:, :], sig[:, :], ALU.mult).then_inc(u_ready, 1)
                        v.wait_ge(u_ready, done(i))
                        v.wait_ge(stage_free, before(i))
                    if j == 3:
                        v.wait_ge(q_hi, done(i))
                        v.scalar_tensor_tensor(q_st[:, LO, :], psum[2][:, :], DH ** -0.5, q_st[:, HI, :].bitcast(F32),
                                               ALU.mult, ALU.subtract).then_inc(q_lo, 1)
                    if j == 4:
                        v.wait_ge(k_hi, done(i))
                        v.tensor_tensor(k_st[:, LO, :], psum[0][:, :], k_st[:, HI, :].bitcast(F32), ALU.subtract)\
                         .then_inc(k_lo, 1)
                    if j == 7:
                        v.wait_ge(v_hi, done(i))
                        v.tensor_tensor(v_st[:, LO, :], psum[3][:, :], v_st[:, HI, :].bitcast(F32), ALU.subtract)\
                         .then_inc(v_lo, 1)
                    if j == 7:
                        v.wait_ge(ac_ready, done(i))
                        v.wait_ge(gemm_done, 8 * i + T_BRANCH + 7)
                        v.tensor_tensor(a_pad[:, KA - 1:], psum[0][:, :], a_c[:, :], ALU.mult).then_inc(au_ready, 1)
                        v.wait_ge(au_ready, done(i))
                        conv_taps(KA, 0, a_pad, a_acc, KA, C_CONVA, None)
                    if j in CONV_TAPS:
                        conv_taps(CONV_TAPS[j], taps, u_pad, u_acc, KC, C_CONVC, C_CBIAS)
                        taps += CONV_TAPS[j]
                    if j == 7:
                        v.tensor_tensor(u_sum[:, :], u_sum[:, :], u_acc[:, :], ALU.add).then_inc(u_summed, 1)
                v.wait_ge(gemm_done, 8 * i + T_BRANCH + 8)
                v.tensor_tensor(a_y[:, :], psum[1][:, :], a_acc[:, :], ALU.mult).then_inc(y_ready, 1)
                v.wait_ge(y_hi, done(i))
                v.tensor_tensor(a_st[:, LO, :], a_y[:, :], a_st[:, HI, :].bitcast(F32), ALU.subtract).then_inc(y_lo, 1)
            dve.leave(KD)

            with v.Fori(0, 3 * KD // 2) as i:
                for j in range(2):
                    lo_next(v, T_GATE + j + 1, i, 2)

            def maxima(i, s):
                n = (s % TB + 1) * P
                v.wait_ge(s_ready, N_STEP * i + s + 1)
                v.tensor_reduce(nmax[:, s % 2:s % 2 + 1], psum[s % 2][:, 0:n], AX.X, ALU.max, negate=True)\
                 .then_inc(m_ready, 1)

            def normalise(i, s):
                k, n = s % 2, (s % TB + 1) * P
                v.wait_ge(e_ready, N_STEP * i + s + 1)
                v.reciprocal(rsum[:, k:k + 1], psum_p[:, k:k + 1]).then_inc(r_ready, 1)
                v.wait_ge(r_ready, N_STEP * i + s + 1)
                v.tensor_scalar(prob[:, k, 0:n], prob[:, k, 0:n], rsum[:, k:k + 1], None, ALU.mult)\
                 .then_inc(p_ready[k], 1)

            def outputs_lo(i, g):
                v.wait_ge(o_hi, done(4 * i + g))
                r, c = slice(g // 2 * DH, (g // 2 + 1) * DH), slice(g % 2 * HALF, (g % 2 + 1) * HALF)
                v.tensor_tensor(o_st[r, LO, c], psum[3][r, c], o_st[r, HI, c].bitcast(F32), ALU.subtract)\
                 .then_inc(o_free[g % 2], 1)

            maxima(0, 0)
            maxima(0, 1)
            normalise(0, 0)

            def pair(i, last):
                for s in range(N_STEP):
                    u, q0 = s // 2, s % 2 * P
                    if not (last and s == N_STEP - 1):
                        normalise(i, s + 1)
                    if s % 4 == 0 and s:
                        outputs_lo(i, s // 4 - 1)
                    for c, (j0, j1) in enumerate(chunks(s), first_chunk[s]):
                        v.wait_ge(pt_hi, N_CHUNK * i + c + 1)
                        v.tensor_tensor(pt[u % 2][:, LO, j0:j1, q0:q0 + P],
                                        psum[2][:, c % 2 * HALF:c % 2 * HALF + (j1 - j0) * P]
                                        .rearrange("p (j q) -> p j q", q=P),
                                        pt[u % 2][:, HI, j0:j1, q0:q0 + P].bitcast(F32), ALU.subtract)\
                         .then_inc(pt_lo[c % 2], 1)
                    if not (last and s + 2 >= N_STEP):
                        maxima(i, s + 2)
                outputs_lo(i, 3)

            attention_pairs(v, pair)

            v.wait_ge(o_stored, 16 * (NH // 2))
            v.wait_ge(mean_done, 1)
            v.memset(sq_sum[:, :], 0.0).then_inc(sq_added, 1)
            for br in range(3):
                if br == 1:
                    v.wait_ge(root_done, 1)
                    v.reciprocal(rstd[:, :], rstd[:, :]).then_inc(rstd_done, 1)
                with v.Fori(0, N_IT) as i:
                    if br == 1:
                        dve.enter(i, 2)
                    for j in range(2):
                        n = T_MERGE + KD * br + j
                        e = 2 * i + j
                        lo_next(v, n + 1, i, 2)
                        if br == 0:
                            v.wait_ge(u_loaded[j], 16 * i + 16)
                            v.tensor_tensor(xc[:, :], uin[:, j, :], row[:, :], ALU.subtract).then_inc(xc_ready, 1)
                            v.wait_ge(sq_ready, e + 1)
                            v.wait_ge(sq_added, e + 1)
                            v.tensor_tensor(sq_sum[:, :], sq_sum[:, :], sq[:, :], ALU.add).then_inc(sq_added, 1)
                        if br == 1:
                            v.wait_ge(ln_ready, e + 1)
                            dve.link(v, v.tensor_scalar(sq[:, :], uin[:, j, :], par[:, bass.ds(2 * i + (C_LNG + j), 1)],
                                                        par[:, bass.ds(2 * i + (C_LNB + j), 1)], ALU.mult, ALU.add))
                            v.wait_ge(zs_ready, e + 1)
                            v.tensor_tensor(sq[:, :], sq[:, :], xc[:, :], ALU.mult).then_inc(zz_ready, 1)
                            v.wait_ge(z_hi, e + 1)
                            v.tensor_tensor(act0[:, e, LO, :], sq[:, :], act0[:, e, HI, :].bitcast(F32), ALU.subtract)\
                             .then_inc(z_lo, 1)
                        v.wait_ge(gemm_done, 2 * i + n + 1)
                        v.wait_ge(g_loaded[j], 16 * i + 16 * N_IT * br + 16)
                        if br < 2:
                            v.wait_ge(part_free[j], before(N_IT * br + i))
                        else:
                            v.wait_ge(part_free[j], done(2 * N_IT - 1))
                        if br == 0:
                            v.tensor_tensor(part[:, j, :], psum[j][:, :], gin[:, j, :], ALU.mult).then_inc(merged[j], 1)
                        else:
                            v.tensor_tensor(part[:, j, :], psum[j][:, :], gin[:, j, :], ALU.mult).then_inc(gated, 1)
                            v.wait_ge(gated, e + KD * (br - 1) + 1)
                            v.wait_ge(m_loaded[j], 16 * i + 16 * N_IT * (br - 1) + 16)
                            v.tensor_tensor(part[:, j, :], part[:, j, :], m_in[:, j, :], ALU.add).then_inc(merged[j], 1)
                        if br == 2:
                            v.wait_ge(mg_hi, done(e))
                            v.tensor_tensor(act1[:, e, LO, :], part[:, j, :], act1[:, e, HI, :].bitcast(F32),
                                            ALU.subtract).then_inc(mg_lo, 1)
                if br == 1:
                    dve.leave(N_IT)

            def add_residual(n0, n_kd, next_splits, first):
                for h in range(2):
                    for kd in range(n_kd):
                        n = n0 + n_kd * h + kd
                        if n + 1 < next_splits:
                            lo_next(v, n + 1)
                    for t in range(4):
                        if t < 3:
                            v.wait_ge(tok_done, 3 * (first // 4 + h) + t + 1)
                        else:
                            v.wait_ge(gemm_done, n0 + n_kd * (h + 1))
                        v.tensor_tensor(res[:, 4 * h + t, :], res[:, 4 * h + t, :], psum[t][:, :], ALU.add)\
                         .then_inc(res_added, 1)

            v.wait_ge(res_loaded, 16 * TB)
            add_residual(T_O, KD, T_END, 0)
            v.wait_ge(gain_in, 32)
            v.wait_ge(res_added, TB)
            norm_blocks_dve(v, B_X1, TB, lambda t: res[:, t, :], xn2, row, lambda t: token_block(act0, t))

            def x_split(k, dst_hi, dst_lo, src):
                v.wait_ge(x_hi, k + 1)
                v.tensor_tensor(dst_lo, src, dst_hi.bitcast(F32), ALU.subtract).then_inc(x_lo, 1)

            lo_next(v, T_XQ + 1)
            v.wait_ge(gain_in, 48)
            for b in range(MB):
                norm_scale(v, B_MEM + b, xn2[:, b, :], xn2, row)
            lo_next(v, T_XQ + 2)
            x_split(0, q_x[0][:, HI, :], q_x[0][:, LO, :], psum[0][:, :])
            lo_next(v, T_XQ + 3)
            x_split(1, q_x[1][:, HI, :], q_x[1][:, LO, :], psum[1][:, :])
            for b in range(MB):
                norm_lo(v, B_MEM + b, [mem_t[:, :, s, b * P:(b + 1) * P] for s in (HI, LO)])
            for h in range(XH):
                x_split(2 + h, k_x[:, h, HI, :], k_x[:, h, LO, :], psum[h % 2][:, 0:N_MEM])
                lo_next(v, T_XK + h + 2)
            for c in range(KD // 2 - 1):
                lo_next(v, T_XV + c + 2)
            x_split(6, v_x[:, :, HI, :], v_x[:, :, LO, :], psum[2][:, :].rearrange("p (b n) -> p b n", b=MB))
            lo_next(v, T_XQ2 + 1)
            x_split(7, q_x[2][:, HI, :], q_x[2][:, LO, :], psum[1][:, :])
            lo_next(v, T_XO)
            x_split(8, q_x[3][:, HI, :], q_x[3][:, LO, :], psum[0][:, :])
            lo_next(v, T_XO + 1)

            def x_max(m):
                s = m % 2
                v.wait_ge(xs_ready, m + 1)
                dve.link(v, v.tensor_reduce(xstat[:, 0, s:s + 1], psum[0][:, s * HALF:s * HALF + N_MEM], AX.X, ALU.max))
                v.tensor_scalar(xstat[:, 1, s:s + 1], xstat[:, 0, s:s + 1], -XD ** -0.5, None, ALU.mult)\
                 .then_inc(xm_ready, 1)

            def x_normalise(m):
                s = m % 2
                v.wait_ge(xe_ready, m + 1)
                dve.link(v, v.reciprocal(xstat[:, 3, s:s + 1], xstat[:, 2, s:s + 1]))
                v.tensor_scalar(xn2[:, s, 0:N_MEM], xn2[:, s, 0:N_MEM], xstat[:, 3, s:s + 1], None, ALU.mult)\
                 .then_inc(xp_ready, 1)

            x_max(0)
            x_max(1)
            x_normalise(0)
            for m in range(XH * TB):
                if m + 1 < XH * TB:
                    x_normalise(m + 1)
                v.wait_ge(xpt_hi, m + 1)
                c0 = m % 4 * P
                v.tensor_tensor(pt_x[:, LO, :, c0:c0 + P],
                                psum[1][:, m % 2 * HALF:m % 2 * HALF + N_MEM].rearrange("p (b t) -> p b t", b=MB),
                                pt_x[:, HI, :, c0:c0 + P].bitcast(F32), ALU.subtract).then_inc(xpt_lo, 1)
                if m + 2 < XH * TB:
                    x_max(m + 2)
                if m % 4 == 3:
                    g = m // 4
                    c = slice(g % 2 * HALF, (g % 2 + 1) * HALF)
                    v.wait_ge(xo_hi, g + 1)
                    v.tensor_tensor(o_x[:, g // 2, LO, c], psum[3][:, c], o_x[:, g // 2, HI, c].bitcast(F32),
                                    ALU.subtract).then_inc(xo_lo, 1)

            for h in range(2):
                for kd in range(XH):
                    n = T_XO + XH * h + kd
                    if T_XO + 2 <= n + 1 <= T_FF:
                        lo_next(v, n + 1)
                for t in range(4):
                    if t < 3:
                        v.wait_ge(tok_done, 3 * (2 + h) + t + 1)
                    else:
                        v.wait_ge(gemm_done, T_XO + XH * (h + 1))
                    v.tensor_tensor(res[:, 4 * h + t, :], res[:, 4 * h + t, :], psum[t][:, :], ALU.add)\
                     .then_inc(res_added, 1)
            v.wait_ge(gain_in, 64)
            v.wait_ge(res_added, 2 * TB)
            norm_blocks_dve(v, B_X2, TB, lambda t: res[:, t, :], xn2, row, lambda t: token_block(act0, t))

            def ff_gated(f):
                v.wait_ge(ff_sig, done(f))
                v.tensor_tensor(xn2[:, 1, :], psum[0][:, :], xn2[:, 0, :], ALU.mult).then_inc(ff_gate, 1)

            def ff_product(f, fs, gemms):
                v.wait_ge(ff_gate, done(f))
                v.wait_ge(gemm_done, gemms)
                v.tensor_tensor(xn2[:, 0, :], psum[1][:, :], xn2[:, 1, :], ALU.mult).then_inc(ff_prod, 1)
                v.wait_ge(ff_hi, done(f))
                v.tensor_tensor(act1[:, fs, LO, :], xn2[:, 0, :], act1[:, fs, HI, :].bitcast(F32), ALU.subtract)\
                 .then_inc(ff_lo, 1)

            def ff_add(f, gemms):
                for t in range(TB):
                    if t < TB - 1:
                        v.wait_ge(d_ready, (TB - 1) * f + t + 1)
                    else:
                        v.wait_ge(gemm_done, gemms)
                    v.tensor_tensor(res[:, t, :], res[:, t, :], psum[2 + t % 2][:, :], ALU.add).then_inc(d_added[t % 2], 1)

            lo_next(v, T_FF + 1)
            ff_gated(0)
            lo_next(v, T_FF + 2)
            with v.Fori(0, (NF - 2) // 2) as i:
                for r_ in range(2):
                    n = T_FF + 2 + 3 * r_
                    lo_next(v, n + 1, i, 6)
                    ff_product(2 * i + r_, r_, 6 * i + n)
                    lo_next(v, n + 2, i, 6)
                    ff_gated(2 * i + 1 + r_)
                    lo_next(v, n + 3, i, 6)
                    ff_add(2 * i + r_, 6 * i + n + 3)
            n = T_END - 4
            lo_next(v, n + 1)
            ff_product(NF - 2, (NF - 2) % 2, n)
            lo_next(v, n + 2)
            ff_gated(NF - 1)
            lo_next(v, n + 3)
            ff_product(NF - 1, (NF - 1) % 2, n + 2)
            ff_add(NF - 2, n + 3)
            ff_add(NF - 1, n + 4)

            v.wait_ge(gain_in, 80)
            for t in range(TB):
                s = t % 2
                v.wait_ge(n_root, B_OUT + t + 1)
                v.reciprocal(stat[:, 2, s:s + 1], stat[:, 1, s:s + 1]).then_inc(n_rstd, 1)
                v.wait_ge(n_rstd, B_OUT + t + 1)
                if t >= 2:
                    v.wait_ge(out_stored[s], 16 * (t // 2))
                v.scalar_tensor_tensor(xn2[:, s, :], res[:, t, :], stat[:, 2, s:s + 1], row[:, :], ALU.mult, ALU.mult)\
                 .then_inc(n_ready, 1)


def row_tiles(w):
    return np.ascontiguousarray(w.reshape(-1, P, T))


def column_tiles(w, starts):
    return np.ascontiguousarray(
        np.stack([w[:, c:c + P].reshape(KD, P, P).transpose(1, 0, 2).reshape(P, T) for c in starts]))


def kernel(**inputs):
    import concourse.bacc as bacc
    from concourse.bass_utils import run_bass_kernel_spmd

    a = {k: np.asarray(v) for k, v in inputs.items()}
    w_in = a["w_in"][0]
    a_b, a_c, a_u, q, k, v, f = (D * n for n in range(7))
    c_val = f + NH
    c_gate, g = c_val + D, c_val + 2 * D
    order = [f] + [start + e * P for e in range(KD) for start in (c_val, c_gate, q, k, v, a_c, a_u, a_b)]
    order += [g + n * P for n in range(3 * KD)]
    w_xkv = a["w_xkv"][0]
    XW = XH * XD

    def per_channel(m):
        return m.reshape(m.shape[0], -1, P).transpose(2, 1, 0).reshape(P, -1)

    params = np.concatenate([
        per_channel(a["conv_c"][0]), per_channel(a["conv_c_bias"]), per_channel(a["conv_a"][0]),
        per_channel(a["b_gate"]), per_channel(a["ln_c_gain"]), per_channel(a["ln_c_bias"]),
        np.pad(a["b_forget"][0], (0, P - NH))[:, None]], axis=1)
    arrays = {
        "x": a["x"][0],
        "mem": a["mem"][0],
        "w_in": column_tiles(w_in, order),
        "w_out": np.concatenate([column_tiles(a[n][0], range(0, D, P)) for n in ("w_out_a", "w_out_b", "w_out_c")]),
        "w_o": row_tiles(a["w_o"][0]),
        "w_xq": column_tiles(a["w_xq"][0], range(0, XW, P)),
        "w_xk": column_tiles(w_xkv, range(0, XW, P)),
        "w_xv": w_xkv[:, XW:].reshape(KD // 2, 2, P, XW).transpose(0, 2, 1, 3).reshape(KD // 2, P, T),
        "w_xo": row_tiles(a["w_xo"][0]),
        "w_gu": column_tiles(a["w_gate_up"][0], [h * FF + n * P for n in range(NF) for h in range(2)]),
        "w_down": row_tiles(a["w_down"][0]),
        "params": params,
        "norms": np.stack([a["mix_norm"][0], a["xattn_norm"][0], a["mem_norm"], a["ffn_norm"][0], a["final_norm"]]),
    }
    nc = bacc.Bacc("TRN2", target_bir_lowering=False, num_devices=1)
    arrays = {n: np.ascontiguousarray(m) for n, m in arrays.items()}
    args = [nc.dram_tensor(n, m.shape, F32, kind="ExternalInput").ap() for n, m in arrays.items()]
    out = nc.dram_tensor("out", (T, D), F32, kind="ExternalOutput").ap()
    build(nc, *args, out)
    r = run_bass_kernel_spmd(nc, [arrays], core_ids=[0])
    return r.results[0]["out"].reshape(1, T, D)
```

```python
from contextlib import ExitStack

import numpy as np

import concourse.bass as bass
from concourse import mybir

P = 128
F32 = mybir.dt.float32
R32 = mybir.dt.float32r
ALU = mybir.AluOpType
ACT = mybir.ActivationFunctionType
AX = mybir.AxisListType
EPS = 1e-6
MASKED = -1e30
HI, LO = 0, 1

D = 1024
T = 1024
KD = D // P
TB = T // P
HALF = 512
NH, DH = 16, 64
QK_ROWS = DH + 2
KA, KC = 3, 31
N_MEM = 256
MB = N_MEM // P
XH, XD = 4, 128
X_STEPS = TB // 2
FF = 2816
NF = FF // P

T_FORGET = 0
T_BRANCH = T_FORGET + 1
T_GATE = T_BRANCH + 8 * KD
T_MERGE = T_GATE + 3 * KD
T_O = T_MERGE + 3 * KD
T_XQ = T_O + 2 * KD
T_XK = T_XQ + 2
T_XV = T_XK + XH
T_XQ2 = T_XV + KD // 2
T_XO = T_XQ2 + 2
T_FF = T_XO + 2 * XH
T_END = T_FF + 3 * NF

C_CONVC = 0
C_CBIAS = C_CONVC + KD * KC
C_CONVA = C_CBIAS + KD
C_BGATE = C_CONVA + KD * KA
C_LNG = C_BGATE + 3 * KD
C_LNB = C_LNG + KD
C_BF = C_LNB + KD
N_PARAM = C_BF + 1


class Chain:

    def __init__(self, sem):
        self.sem, self.n, self.i, self.per, self.start = sem, 0, None, 0, 0

    def enter(self, i, per):
        self.i, self.per, self.start = i, per, self.n

    def leave(self, iterations):
        assert self.n - self.start == self.per, (self.n - self.start, self.per)
        self.n = self.start + self.per * iterations
        self.i = None

    def link(self, eng, ins):
        ins.then_inc(self.sem, 1)
        self.n += 1
        eng.wait_ge(self.sem, self.n if self.i is None else self.i * self.per + self.n)


def build(nc, x, mem, w_in, w_out, w_o, w_xq, w_xk, w_xv, w_xo, w_gu, w_down, params, norms, out):
    def scratch(name, shape, dt):
        return nc.dram_tensor(name, shape, dt).ap()

    q_s = scratch("q_s", (NH, QK_ROWS, 2 * T), F32)
    k_s = scratch("k_s", (NH, QK_ROWS, 2 * T), F32)
    v_s = scratch("v_s", (NH // 2, P, 2 * T), F32)
    a_s = scratch("a_s", (KD, P, 2 * T), F32)
    b_s = scratch("b_s", (KD, P, 2 * T), F32)
    u_s = scratch("u_s", (KD, P, T), F32)
    g_s = scratch("g_s", (3 * KD, P, T), F32)
    m_s = scratch("m_s", (KD, P, T), F32)

    with ExitStack() as ctx:
        def sem(name):
            return ctx.enter_context(nc.semaphore(name))

        def sb(name, shape, dt=F32, scope=ctx):
            return scope.enter_context(nc.sbuf_tensor(name, shape, dt))

        ident = sb("ident", [P, P])
        ident_r = sb("ident_r", [P, P], R32)
        mask_r = sb("mask_r", [P, P], R32)
        ones = sb("ones", [P, P])
        eps = sb("eps", [P, 1])
        par = sb("par", [P, N_PARAM])
        xstat = sb("xstat", [P, 4, 2, 2])
        stat = sb("stat", [P, 3, 4])
        w_raw = sb("w_raw", [P, 2, T])
        w_hi = sb("w_hi", [P, 2, T], R32)
        w_lo = sb("w_lo", [P, 2, T], R32)
        row = sb("row", [P, D])
        act0 = sb("act0", [P, KD, 2, T], R32)
        with ExitStack() as s1:
            mask_f = sb("mask_f", [P, P], scope=s1)
            xin = sb("xin", [P, 4, D], scope=s1)
            xn = sb("xn", [P, 2, D], scope=s1)
            t_f = sb("t_f", [P, 2, T], scope=s1)
            u_pad = sb("u_pad", [P, KC - 1 + T], scope=s1)
            sig = sb("sig", [P, T], scope=s1)
            u_acc = sb("u_acc", [P, T], scope=s1)
            a_c = sb("a_c", [P, T], scope=s1)
            a_pad = sb("a_pad", [P, KA - 1 + T], scope=s1)
            a_acc = sb("a_acc", [P, T], scope=s1)
            a_y = sb("a_y", [P, T], scope=s1)
            v_t = sb("v_t", [P, T], scope=s1)
            q_st = sb("q_st", [P, 2, T], R32, scope=s1)
            k_st = sb("k_st", [P, 2, T], R32, scope=s1)
            v_st = sb("v_st", [P, 2, T], R32, scope=s1)
            a_st = sb("a_st", [P, 2, T], R32, scope=s1)
            u_sum = sb("u_sum", [P, T], scope=s1)
            g_st = sb("g_st", [P, 2, T], scope=s1)
        with ExitStack() as s2:
            qh = [sb(f"qh{h}", [QK_ROWS, 2, T], R32, scope=s2) for h in range(2)]
            kh = [sb(f"kh{h}", [QK_ROWS, 2, T], R32, scope=s2) for h in range(2)]
            vh = [sb(f"vh{h}", [P, 2, TB, P], R32, scope=s2) for h in range(2)]
            prob = sb("prob", [P, 2, T], scope=s2)
            pt = [sb(f"pt{u}", [P, 2, TB, 2 * P], R32, scope=s2) for u in range(2)]
            nmax = sb("nmax", [P, 2], scope=s2)
            prob_sum = sb("prob_sum", [P, 2], scope=s2)
            rsum = sb("rsum", [P, 2], scope=s2)
            o_st = sb("o_st", [P, 2, T], R32, scope=s2)
        act1 = sb("act1", [P, KD, 2, T], R32)
        with ExitStack() as s3:
            rstd = sb("rstd", [P, T], scope=s3)
            sq_sum = sb("sq_sum", [P, T], scope=s3)
            gin = sb("gin", [P, 2, T], scope=s3)
            part = sb("part", [P, 2, T], scope=s3)
            m_in = sb("m_in", [P, 2, T], scope=s3)
            uin = sb("uin", [P, 2, T], scope=s3)
            xc = sb("xc", [P, T], scope=s3)
            sq = sb("sq", [P, T], scope=s3)
        res = sb("res", [P, TB, D])
        xn2 = sb("xn2", [P, 2, D])
        flat1 = act1[:, :, :, :].rearrange("p k s t -> p k (s t)")
        mem_t = flat1[:, 0:2, :].rearrange("p k n -> p (k n)").rearrange("p (k s m) -> p k s m", k=KD, s=2)
        k_x = flat1[:, 2, :].rearrange("p (h s m) -> p h s m", h=XH, s=2)
        v_x = flat1[:, 3, :].rearrange("p (b s n) -> p b s n", b=MB, s=2)
        o_x = act1[:, 4:8, :, :]
        q_x = [act1[:, c, :, :] for c in (6, 7, 0, 1)]
        pt_x = sb("pt_x", [P, 2, MB, HALF], R32)
        junk = pt_x[:, 0, :, :].rearrange("p b t -> p (b t)")

        psum = [ctx.enter_context(nc.psum_tensor(f"ps{i}", [P, 2 * HALF], F32)) for i in range(4)]

        credit = []

        def sem1(name):
            s = sem(name)
            credit.append(s)
            return s

        def done(k):
            return k + 2

        def before(k):
            return k + 1

        const_done, params_in, gain_in = sem("const_done"), sem("params_in"), sem("gain_in")
        w_loaded = [sem(f"w_loaded{s}") for s in range(2)]
        w_hi_done, w_split = sem("w_hi_done"), sem("w_split")
        gemm_done = sem("gemm_done")
        dve = Chain(sem("dve_chain"))
        const_r, pads, f_cum, r_ready, gated = (sem(n) for n in ("const_r", "pads", "f_cum", "r_ready", "gated"))
        usum_stored, pool_step = sem("usum_stored"), sem("pool_step")
        CONV_TAPS = {2: 5, 3: 6, 4: 6, 5: 7, 6: 6, 7: 1}
        assert sum(CONV_TAPS.values()) == KC
        x_loaded = [sem(f"x_loaded{s}") for s in range(4)]
        n_sq, n_root, n_rstd, n_ready = sem("n_sq"), sem("n_root"), sem("n_rstd"), sem("n_ready")
        n_trans, n_hi, n_lo = sem("n_trans"), sem("n_hi"), sem("n_lo")
        f_abs, f_exp, f_ln, f_min = sem("f_abs"), sem("f_exp"), sem("f_ln"), sem("f_min")
        f_hi, f_rows, rows_stored = sem("f_hi"), sem("f_rows"), sem("rows_stored")
        sig_ready, u_ready, u_summed = sem1("sig_ready"), sem1("u_ready"), sem1("u_summed")
        q_hi, q_lo, k_hi, k_lo = sem1("q_hi"), sem1("q_lo"), sem1("k_hi"), sem1("k_lo")
        v_copied, v_trans, v_hi, v_lo = sem1("v_copied"), sem1("v_trans"), sem1("v_hi"), sem1("v_lo")
        ac_ready, au_ready = sem1("ac_ready"), sem1("au_ready")
        y_ready, y_hi, y_lo = sem1("y_ready"), sem1("y_hi"), sem1("y_lo")
        q_stored, k_stored, v_stored = sem("q_stored"), sem("k_stored"), sem("v_stored")
        u_stored, y_stored = sem("u_stored"), sem("y_stored")
        stage_free = sem("stage_free")
        gate_done = [sem1(f"gate_done{s}") for s in range(2)]
        gate_stored = [sem(f"gate_stored{s}") for s in range(2)]
        gate_free = [sem1(f"gate_free{s}") for s in range(2)]
        qkv_loaded = [sem(f"qkv_loaded{h}") for h in range(2)]
        v_ones = sem("v_ones")
        s_ready, m_ready = sem("s_ready"), sem("m_ready")
        p_ready = sem("p_ready")
        t_done, pt_hi = sem("t_done"), sem("pt_hi")
        pt_lo = sem1("pt_lo")
        pv_done = [sem1(f"pv_done{s}") for s in range(2)]
        o_free = [sem1(f"o_free{s}") for s in range(2)]
        e_ready = sem("e_ready")
        o_hi, o_stored = sem1("o_hi"), sem("o_stored")
        o_stage_free = sem1("o_stage_free")
        act0_loaded, act1_loaded = sem("act0_loaded"), sem("act1_loaded")
        usum_loaded, mean_ps, mean_done = sem("usum_loaded"), sem("mean_ps"), sem("mean_done")
        g_loaded = [sem(f"g_loaded{s}") for s in range(2)]
        m_loaded = [sem(f"m_loaded{s}") for s in range(2)]
        u_loaded = [sem(f"u_loaded{s}") for s in range(2)]
        merged = [sem1(f"merged{s}") for s in range(2)]
        m_stored = [sem(f"m_stored{s}") for s in range(2)]
        part_free = [sem1(f"part_free{s}") for s in range(2)]
        xc_ready, sq_ready, sq_added = sem1("xc_ready"), sem("sq_ready"), sem("sq_added")
        var_ps, root_done, rstd_done = sem("var_ps"), sem("root_done"), sem("rstd_done")
        xc_done = sem("xc_done")
        ln_ready, zs_ready, zz_ready = sem("ln_ready"), sem("zs_ready"), sem("zz_ready")
        z_hi, z_lo = sem("z_hi"), sem("z_lo")
        mg_hi, mg_lo = sem1("mg_hi"), sem1("mg_lo")
        res_loaded, tok_done, res_added = sem("res_loaded"), sem("tok_done"), sem("res_added")
        mem_loaded = sem("mem_loaded")
        x_hi, x_lo = sem("x_hi"), sem("x_lo")
        xs_ready, xm_ready, xe_ready, xr_ready, xp_ready = (
            sem(n) for n in ("xs_ready", "xm_ready", "xe_ready", "xr_ready", "xp_ready"))
        xt_done, xpt_hi, xpt_lo, xpv_done, xo_hi, xo_lo = (
            sem(n) for n in ("xt_done", "xpt_hi", "xpt_lo", "xpv_done", "xo_hi", "xo_lo"))
        ff_sig, ff_gate, ff_prod, ff_hi, ff_lo = (sem1(n) for n in ("ff_sig", "ff_gate", "ff_prod", "ff_hi", "ff_lo"))
        d_ready = sem("d_ready")
        d_added = [sem1(f"d_added{s}") for s in range(2)]
        out_stored = [sem(f"out_stored{s}") for s in range(2)]

        def load_tile(sp, n, slot, src):
            if not isinstance(n, int) or n >= 2:
                sp.wait_ge(w_split, n - 1)
            sp.dma_start(w_raw[:, slot, :], src).then_inc(w_loaded[slot], 16)

        def split_hi(act, n, slot, loads):
            act.wait_ge(w_loaded[slot], loads * 16)
            if not isinstance(n, int) or n >= 2:
                act.wait_ge(gemm_done, n - 1)
            act.activation(w_hi[:, slot, :], w_raw[:, slot, :], ACT.Copy).then_inc(w_hi_done, 1)

        def split_lo(v, n, slot):
            v.wait_ge(w_hi_done, n + 1)
            v.tensor_tensor(w_lo[:, slot, :], w_raw[:, slot, :], w_hi[:, slot, :].bitcast(F32),
                            ALU.subtract).then_inc(w_split, 1)

        def hi_next(act, base, i=0, per=0):
            split_hi(act, base + per * i, base % 2, base // 2 + 1 + (per // 2) * i)

        def lo_next(v, base, i=0, per=0):
            split_lo(v, base + per * i, base % 2)

        def weights(slot):
            return [w[:, slot, :] for w in (w_hi, w_lo)]

        def tile_products(pe, out, act, slot, halves=range(2), n_tok=HALF):
            w = [t.rearrange("p (k e) -> p k e", k=KD) for t in weights(slot)]
            for kd in range(KD):
                for half in halves:
                    t0 = half * HALF
                    for a, b in ((HI, HI), (HI, LO), (LO, HI)):
                        last = pe.matmul(out[:, t0:t0 + n_tok], w[a][:, kd, :], act[:, kd, b, t0:t0 + n_tok],
                                         start=(kd == 0 and a == b), stop=(kd == KD - 1 and a == LO))
            return last

        def row_products(pe, out, stat_hl, slot, start, stop):
            w = weights(slot)
            for half in range(2):
                c = slice(half * HALF, (half + 1) * HALF)
                for a, b in ((HI, HI), (HI, LO), (LO, HI)):
                    last = pe.matmul(out[:, c], stat_hl[a], w[b][:, c],
                                     start=(start and a == b), stop=(stop and a == LO))
            return last

        def norm_stats(act, b, src, junk):
            s = b % 4
            if b >= 4:
                act.wait_ge(n_rstd, b - 3)
            act.activation(junk, src, ACT.Square, accum_out=stat[:, 0, s:s + 1]).then_inc(n_sq, 1)
            act.wait_ge(n_sq, b + 1)
            act.activation(stat[:, 1, s:s + 1], stat[:, 0, s:s + 1], ACT.Sqrt, bias=eps[:, 0:1],
                           scale=1.0 / D).then_inc(n_root, 1)

        def norm_scale(v, b, src, dst, g):
            s = b % 4
            v.wait_ge(n_root, b + 1)
            v.reciprocal(stat[:, 2, s:s + 1], stat[:, 1, s:s + 1]).then_inc(n_rstd, 1)
            v.wait_ge(n_rstd, b + 1)
            if b >= 2:
                v.wait_ge(n_trans, b - 1)
            v.scalar_tensor_tensor(dst[:, b % 2, :], src, stat[:, 2, s:s + 1], g[:, :], ALU.mult, ALU.mult)\
             .then_inc(n_ready, 1)

        def norm_transpose(pe, b, src):
            pe.wait_ge(n_ready, b + 1)
            if b >= 2:
                pe.wait_ge(n_lo, b - 1)
            for kd in range(KD):
                last = pe.transpose(psum[2 + b % 2][:, kd * P:(kd + 1) * P], src[:, b % 2, kd * P:(kd + 1) * P],
                                    ident[:, :])
            last.then_inc(n_trans, 1)

        def norm_hi(act, b, dst):
            act.wait_ge(n_trans, b + 1)
            act.activation(dst[HI], psum[2 + b % 2][:, :].rearrange("p (k t) -> p k t", k=KD), ACT.Copy)\
               .then_inc(n_hi, 1)

        def norm_lo(v, b, dst):
            v.wait_ge(n_hi, b + 1)
            v.tensor_tensor(dst[LO], psum[2 + b % 2][:, :].rearrange("p (k t) -> p k t", k=KD),
                            dst[HI].bitcast(F32), ALU.subtract).then_inc(n_lo, 1)

        def token_block(act, t):
            return [act[:, :, s, t * P:(t + 1) * P] for s in (HI, LO)]

        B_X, B_X1, B_MEM, B_X2, B_OUT = 0, TB, 2 * TB, 2 * TB + MB, 3 * TB + MB

        def norm_blocks_act(act, b0, src, dst, junk, ready, midway, started=0):
            for t in range(TB + 2):
                if started <= t < TB:
                    ready(t)
                    norm_stats(act, b0 + t, src(t), junk)
                if t >= 2:
                    norm_hi(act, b0 + t - 2, token_block(dst, t - 2))
                if t == TB // 2 + 1:
                    midway()

        def norm_blocks_dve(v, b0, src, buf, dst, midway, started=0):
            for t in range(TB + 2):
                if started <= t < TB:
                    norm_scale(v, b0 + t, src(t), buf, row)
                if t >= 2:
                    norm_lo(v, b0 + t - 2, token_block(dst, t - 2))
                if t == TB // 2 + 1:
                    midway()

        def norm_then_gemm(pe, b0, src, dst, tiles, ready=lambda t: None):
            for t in range(TB - 2):
                ready(t)
                norm_transpose(pe, b0 + t, src)
            for k, (out, n, slot) in enumerate(tiles):
                pe.wait_ge(w_split, n + 1)
                tile_products(pe, out, dst, slot, range(1))
                for t in ((TB - 2, TB - 1) if k == 0 else ()):
                    norm_transpose(pe, b0 + t, src)
            pe.wait_ge(n_lo, b0 + TB)
            for out, n, slot in tiles:
                tile_products(pe, out, dst, slot, range(1, 2)).then_inc(gemm_done, 1)

        ORDER = [q for n in range(TB // 2) for q in (TB - 1 - n, n)]
        N_STEP = 2 * TB

        def query(s):
            return ORDER[s % TB]

        def chunks(s):
            n = query(s) + 1
            return [(0, 4, psum[2][:, 0:HALF]), (4, n, psum[2][:, HALF:])] if n > 4 else [(0, n, psum[1][:, HALF:])]

        first_chunk = [sum(len(chunks(r)) for r in range(s)) for s in range(N_STEP + 1)]
        N_CHUNK = first_chunk[N_STEP]

        def quarter(k):
            last = k // 2 * 4 + 2 + k % 2
            return k // 4, query(last) // 2, last

        def half_head(g):
            return slice(g // 2 * DH, (g // 2 + 1) * DH), slice((1 - g % 2) * HALF, (2 - g % 2) * HALF)

        def attention_pairs(eng, body):
            with eng.Fori(0, NH // 2 - 1) as i:
                body(i, False)
            body(NH // 2 - 1, True)

        LAST_PAIRS = (2, 3, 0, 1)
        N_IT = KD // 2

        block = ctx.enter_context(nc.Block())

        @block.sync
        def _(sp):
            for b in range(TB):
                if b >= 4:
                    sp.wait_ge(n_ready, b - 3)
                sp.dma_start(xin[:, b % 4, :], x[b * P:(b + 1) * P, :]).then_inc(x_loaded[b % 4], 16)
                if b == 0:
                    sp.dma_start(row[:, :], norms[0:1, :].to_broadcast([P, D])).then_inc(gain_in, 16)
                if b == 3:
                    sp.dma_start(par[:, :], params).then_inc(params_in, 16)
                    load_tile(sp, 0, 0, w_in[0])
                    load_tile(sp, 1, 1, w_in[1])
            load_tile(sp, 2, 0, w_in[2])
            with sp.Fori(0, (T_MERGE - 3) // 2) as i:
                load_tile(sp, 2 * i + 3, 1, w_in[2 * i + 3])
                load_tile(sp, 2 * i + 4, 0, w_in[2 * i + 4])
            load_tile(sp, T_MERGE, T_MERGE % 2, w_out[0])
            load_tile(sp, T_MERGE + 1, (T_MERGE + 1) % 2, w_out[1])

            for s in (q_stored, k_stored):
                sp.wait_ge(s, 32 * KD)
            for s in (v_stored, u_stored, y_stored):
                sp.wait_ge(s, 16 * KD)
            sp.wait_ge(rows_stored, 64)

            def load_head(h, head, pair):
                sp.dma_start(qh[h][:, :, :].bitcast(F32), q_s[head].rearrange("p (s t) -> p s t", s=2)).then_inc(qkv_loaded[h], 16)
                sp.dma_start(kh[h][:, :, :].bitcast(F32), k_s[head].rearrange("p (s t) -> p s t", s=2)).then_inc(qkv_loaded[h], 16)
                sp.dma_start(vh[h][:, :, :, :].bitcast(F32), v_s[pair].rearrange("p (s j c) -> p s j c", s=2, c=P))\
                  .then_inc(qkv_loaded[h], 16)

            load_head(0, 0, 0)
            load_head(1, 1, 0)
            with sp.Fori(0, NH // 2 - 1) as i:
                sp.wait_ge(pv_done[1], done(4 * i + 1))
                load_head(0, 2 * i + 2, i + 1)
                sp.wait_ge(pv_done[1], done(4 * i + 3))
                load_head(1, 2 * i + 3, i + 1)

            sp.wait_ge(o_stored, 16 * (NH // 2))

            def load_act1(kd):
                sp.dma_start(act1[:, kd, :, :].bitcast(F32), b_s[kd].rearrange("p (s t) -> p s t", s=2))\
                  .then_inc(act1_loaded, 16)

            def load_chunk(br, e, j):
                if br < 2:
                    sp.dma_start(uin[:, j, :], u_s[e]).then_inc(u_loaded[j], 16)
                sp.dma_start(gin[:, j, :], g_s[e + KD * br]).then_inc(g_loaded[j], 16)
                if br:
                    sp.dma_start(m_in[:, j, :], m_s[e]).then_inc(m_loaded[j], 16)

            def merge_step(br, i, j):
                n = T_MERGE + KD * br + j + 2
                at_end = br == 2 and isinstance(i, int)
                load_tile(sp, 2 * i + n, n % 2, w_o[j] if at_end else w_out[2 * i + KD * br + j + 2])
                if br == 0:
                    load_act1(2 * i + j)
                sp.wait_ge(merged[j], done(N_IT * br + i))
                if not isinstance(i, int):
                    load_chunk(br, 2 * i + j + 2, j)
                elif br < 2:
                    sp.wait_ge(m_stored[j], 16 * N_IT * (br + 1))
                    load_chunk(br + 1, j, j)

            for j in range(2):
                load_chunk(0, j, j)
            for br in range(3):
                with sp.Fori(0, N_IT - 1) as i:
                    for j in range(2):
                        merge_step(br, i, j)
                for j in range(2):
                    merge_step(br, N_IT - 1, j)
            sp.wait_ge(mg_lo, done(KD - 1))
            for t in range(TB):
                sp.dma_start(res[:, t, :], x[t * P:(t + 1) * P, :]).then_inc(res_loaded, 16)
            sp.dma_start(row[:, :], norms[1:2, :].to_broadcast([P, D])).then_inc(gain_in, 16)
            tiles = [w_o[kd] for _ in range(2) for kd in range(KD)]
            tiles += [w_xq[0], w_xq[1]] + [w_xk[h] for h in range(XH)] + [w_xv[c] for c in range(KD // 2)]
            tiles += [w_xq[2], w_xq[3]] + [w_xo[kd] for _ in range(2) for kd in range(XH)]
            tiles += [w_gu[0], w_gu[1]]
            assert T_O + len(tiles) == T_FF + 2
            for n in range(T_O + 2, T_FF + 2):
                if n == T_XQ + 2:
                    sp.wait_ge(n_trans, B_X1 + TB)
                    for b in range(MB):
                        sp.dma_start(xn2[:, b, :], mem[b * P:(b + 1) * P, :]).then_inc(mem_loaded, 16)
                    sp.wait_ge(n_ready, B_MEM)
                    sp.dma_start(row[:, :], norms[2:3, :].to_broadcast([P, D])).then_inc(gain_in, 16)
                if n == T_XO:
                    sp.wait_ge(n_ready, B_X2)
                    sp.dma_start(row[:, :], norms[3:4, :].to_broadcast([P, D])).then_inc(gain_in, 16)
                load_tile(sp, n, n % 2, tiles[n - T_O])
            with sp.Fori(0, (NF - 2) // 2) as i:
                for j in range(6):
                    n = T_FF + 2 + j
                    src = (w_gu[4 * i + 2 + j] if j < 2 else w_down[2 * i] if j == 2 else
                           w_gu[4 * i + 1 + j] if j < 5 else w_down[2 * i + 1])
                    load_tile(sp, 6 * i + n, n % 2, src)
            for j, src in enumerate((w_gu[2 * NF - 2], w_gu[2 * NF - 1], w_down[NF - 2], w_down[NF - 1])):
                n = T_END - 4 + j
                load_tile(sp, n, n % 2, src)
            sp.wait_ge(n_ready, B_OUT)
            sp.dma_start(row[:, :], norms[4:5, :].to_broadcast([P, D])).then_inc(gain_in, 16)
            for t in range(TB):
                sp.wait_ge(n_ready, B_OUT + t + 1)
                sp.dma_start(out[t * P:(t + 1) * P, :], xn2[:, t % 2, :]).then_inc(out_stored[t % 2], 16)
            for s in range(2):
                sp.wait_ge(out_stored[s], 16 * TB // 2)

        @block.gpsimd
        def _(pool):
            def wait(s, value):
                pool.wait_ge(s, value)
                pool.sem_inc(pool_step, 1)

            for s in credit:
                pool.sem_inc(s, 1)
            pool.memset(ident[:, :], 0.0).then_inc(const_done, 1)
            pool.memset(mask_f[:, :], 0.0).then_inc(const_done, 1)
            pool.memset(ones[:, :], 1.0).then_inc(const_done, 1)
            pool.memset(eps[:, :], EPS).then_inc(const_done, 1)
            pool.wait_ge(const_done, 4)
            pool.affine_select(out=ident[:, :], in_=ident[:, :], compare_op=ALU.not_equal, fill=1.0, base=0,
                               pattern=[[-1, P]], channel_multiplier=1).then_inc(const_done, 1)
            pool.affine_select(out=mask_f[:, :], in_=mask_f[:, :], compare_op=ALU.is_ge, fill=MASKED, base=0,
                               pattern=[[-1, P]], channel_multiplier=1).then_inc(const_done, 1)

            pool.wait_ge(f_rows, 3)
            r = slice(0, NH)
            for dst, src, at in ((q_s, a_st, DH), (q_s, q_st, DH + 1), (k_s, k_st, DH), (k_s, a_st, DH + 1)):
                pool.dma_start(dst[:, at, :], src[r, :, :].rearrange("p s t -> p (s t)").bitcast(F32)).then_inc(rows_stored, 16)
            pool.wait_ge(rows_stored, 64)
            pool.sem_inc(stage_free, 1)

            with pool.Fori(0, KD) as i:
                for lo_sem, st, dst, stored in ((q_lo, q_st, q_s, q_stored), (k_lo, k_st, k_s, k_stored)):
                    wait(lo_sem, done(i))
                    for h in range(2):
                        pool.dma_start(dst[2 * i + h, 0:DH, :].rearrange("p (s t) -> p s t", s=2),
                                       st[h * DH:(h + 1) * DH, :, :].bitcast(F32)).then_inc(stored, 16)
                wait(v_lo, done(i))
                pool.dma_start(v_s[i].rearrange("p (s t) -> p s t", s=2), v_st[:, :, :].bitcast(F32)).then_inc(v_stored, 16)
                wait(u_summed, done(i))
                pool.dma_start(u_s[i], u_acc[:, :]).then_inc(u_stored, 16)
                wait(y_lo, done(i))
                pool.dma_start(a_s[i].rearrange("p (s t) -> p s t", s=2), a_st[:, :, :].bitcast(F32)).then_inc(y_stored, 16)
                for s, by in ((q_stored, 32), (k_stored, 32), (v_stored, 16), (u_stored, 16), (y_stored, 16)):
                    wait(s, by * i + by)
                pool.sem_inc(stage_free, 1)
            with pool.Fori(0, 3 * KD // 2) as i:
                for j in range(2):
                    wait(gate_done[j], done(i))
                    pool.dma_start(g_s[2 * i + j], g_st[:, j, :]).then_inc(gate_stored[j], 16)
                for j in range(2):
                    wait(gate_stored[j], 16 * i + 16)
                    pool.sem_inc(gate_free[j], 1)

            wait(gemm_done, T_MERGE)
            wait(y_stored, 16 * KD)
            wait(qkv_loaded[1], 48)
            for kd in range(KD):
                pool.dma_start(act0[:, kd, :, :].bitcast(F32), a_s[kd].rearrange("p (s t) -> p s t", s=2)).then_inc(act0_loaded, 16)

            with pool.Fori(0, NH // 2) as i:
                wait(o_free[0], done(2 * i + 1))
                pool.dma_start(b_s[i].rearrange("p (s t) -> p s t", s=2), o_st[:, :, :].bitcast(F32)).then_inc(o_stored, 16)
                wait(o_stored, 16 * i + 16)
                pool.sem_inc(o_stage_free, 1)

            for br in range(2):
                if br == 1:
                    pool.wait_ge(rstd_done, 1)
                with pool.Fori(0, N_IT) as i:
                    for j in range(2):
                        if br == 1:
                            wait(u_loaded[j], 16 * i + 16 * N_IT + 16)
                            pool.tensor_tensor(uin[:, j, :], uin[:, j, :], row[:, :], ALU.subtract).then_inc(xc_done, 1)
                            wait(xc_done, 2 * i + j + 1)
                            pool.tensor_tensor(uin[:, j, :], uin[:, j, :], rstd[:, :], ALU.mult).then_inc(ln_ready, 1)
                    for j in range(2):
                        wait(merged[j], done(N_IT * br + i))
                        pool.dma_start(m_s[2 * i + j], part[:, j, :]).then_inc(m_stored[j], 16)
                    for j in range(2):
                        wait(m_stored[j], 16 * i + 16 * N_IT * br + 16)
                        pool.sem_inc(part_free[j], 1)

        @block.tensor
        def _(pe):
            pe.wait_ge(const_done, 6)
            norm_then_gemm(pe, B_X, xn, act0, [(psum[1], T_FORGET, T_FORGET % 2)])

            pair_free = [(au_ready, before), (y_ready, before), (ac_ready, before), (u_ready, done),
                         (sig_ready, done), (q_lo, done), (k_lo, done), (v_copied, done)]
            with pe.Fori(0, KD) as i:
                for j in range(8):
                    pe.wait_ge(w_split, 8 * i + T_BRANCH + j + 1)
                    s, when = pair_free[j]
                    pe.wait_ge(s, when(i))
                    tile_products(pe, psum[j % 3], act0, (T_BRANCH + j) % 2).then_inc(gemm_done, 1)
                    if j == 5:
                        pe.wait_ge(v_copied, done(i))
                        pe.wait_ge(v_lo, before(i))
                        for b in range(TB):
                            last = pe.transpose(psum[3][:, b * P:(b + 1) * P], v_t[:, b * P:(b + 1) * P], ident[:, :])
                        last.then_inc(v_trans, 1)

            pe.wait_ge(ac_ready, done(KD - 1))
            pe.wait_ge(v_lo, done(KD - 1))
            with pe.Fori(0, 3 * KD // 2) as i:
                for j in range(2):
                    pe.wait_ge(w_split, 2 * i + T_GATE + j + 1)
                    pe.wait_ge(gate_done[j], before(i))
                    tile_products(pe, psum[2 + j], act0, (T_GATE + j) % 2).then_inc(gemm_done, 1)

            def scores(s):
                h, qb, ps = s // TB % 2, query(s), psum[s % 2]
                n = (qb + 1) * P
                q = slice(qb * P, n)
                for c in range(0, n, HALF):
                    k = slice(c, min(n, c + HALF))
                    for a, b in ((HI, HI), (HI, LO), (LO, HI)):
                        last = pe.matmul(ps[:, k], qh[h][:, a, q], kh[h][:, b, k], start=(a == b),
                                         stop=(a == LO and k.stop < n))
                last = pe.matmul(ps[:, q], ident_r[:, :], mask_r[:, :], start=False, stop=True)
                last.then_inc(s_ready, 1)

            def transposes(i, s):
                pe.wait_ge(pt_lo, done(N_CHUNK * i + (first_chunk[s - 1] if s >= 2 else 0) - 1))
                for j0, j1, bank in chunks(s):
                    for j in range(j0, j1):
                        last = pe.transpose(bank[:, (j - j0) * P:(j - j0 + 1) * P],
                                            prob[:, s % 2, j * P:(j + 1) * P], ident[:, :])
                    last.then_inc(t_done, 1)

            def outputs(i, k):
                h, u, s = quarter(k)
                half = u // 2
                pe.wait_ge(pt_lo, done(N_CHUNK * i + first_chunk[s + 1] - 1))
                if k % 4 < 2:
                    pe.wait_ge(o_free[half], before(2 * i + h))
                o0 = half * HALF + u % 2 * 2 * P
                last_j = 2 * u + 1
                for j in range(last_j + 1):
                    c0 = P if j == last_j else 0
                    for a, b in ((HI, HI), (HI, LO), (LO, HI)):
                        last = pe.matmul(psum[3][:, o0 + c0:o0 + 2 * P], vh[h][:, a, j, :],
                                         pt[k % 2][:, b, j, c0:2 * P], start=(j == 0 and a == b),
                                         stop=(j == last_j and a == LO))
                last.then_inc(pv_done[k % 2], 1)

            pe.wait_ge(au_ready, done(KD - 1))
            pe.wait_ge(y_ready, done(KD - 1))
            pe.wait_ge(u_summed, done(KD - 1))
            for half in range(2):
                c = slice(half * HALF, (half + 1) * HALF)
                last = pe.matmul(psum[0][:, c], ones[:, :], u_sum[:, c], start=True, stop=True)
            last.then_inc(mean_ps, 1)
            pe.wait_ge(mean_done, 1)
            for s in gate_done:
                pe.wait_ge(s, done(3 * KD // 2 - 1))
            pe.wait_ge(qkv_loaded[0], 48)
            scores(0)
            scores(1)

            def pair(i, last):
                for s in range(N_STEP):
                    if not (last and s + 2 >= N_STEP):
                        if s + 2 == TB:
                            pe.wait_ge(qkv_loaded[1], 48 * i + 48)
                        if s + 2 == N_STEP:
                            pe.wait_ge(qkv_loaded[0], 48 * i + 96)
                        pe.wait_ge(e_ready, N_STEP * i + s + 1)
                        scores(s + 2)
                    pe.wait_ge(p_ready, N_STEP * i + s + 1)
                    transposes(i, s)
                    for k in range(8):
                        if quarter(k)[2] == s - 1:
                            outputs(i, k)
                outputs(i, 7)

            attention_pairs(pe, pair)

            for s in o_free:
                pe.wait_ge(s, done(2 * (NH // 2) - 1))
            for br, act in enumerate((act0, act1, act0)):
                if br == 0:
                    pe.wait_ge(act0_loaded, 16 * KD)
                if br == 1:
                    pe.wait_ge(sq_added, KD + 1)
                    for half in range(2):
                        c = slice(half * HALF, (half + 1) * HALF)
                        last = pe.matmul(psum[3][:, c], ones[:, :], sq_sum[:, c], start=True, stop=True)
                    last.then_inc(var_ps, 1)
                    pe.wait_ge(act1_loaded, 16 * KD)
                if br == 2:
                    pe.wait_ge(z_lo, KD)
                with pe.Fori(0, N_IT) as i:
                    for j in range(2):
                        n = T_MERGE + KD * br + j
                        pe.wait_ge(w_split, 2 * i + n + 1)
                        pe.wait_ge(merged[j], before(N_IT * br + i))
                        tile_products(pe, psum[j], act, n % 2).then_inc(gemm_done, 1)

            def token_gemm(n0, n_kd, stationary, free, first):
                for h in range(2):
                    for kd in range(n_kd):
                        n = n0 + n_kd * h + kd
                        pe.wait_ge(w_split, n + 1)
                        for t in range(4):
                            if kd == 0 and h == 0:
                                free(t)
                            if kd == 0 and h == 1:
                                pe.wait_ge(res_added, first + t + 1)
                            last = row_products(pe, psum[t], stationary(kd, 4 * h + t), n % 2,
                                                kd == 0, kd == n_kd - 1)
                            if kd == n_kd - 1 and t < 3:
                                last.then_inc(tok_done, 1)
                        last.then_inc(gemm_done, 1)

            def blocks_of(act, kd, t):
                return [act[:, kd, s, t * P:(t + 1) * P] for s in (HI, LO)]

            def free_o(t):
                if t < 2:
                    pe.wait_ge(merged[t], done(3 * N_IT - 1))
                if t == 3:
                    pe.wait_ge(root_done, 1)
                if t == 0:
                    pe.wait_ge(mg_lo, done(KD - 1))

            token_gemm(T_O, KD, lambda kd, t: blocks_of(act1, kd, t), free_o, 0)

            def pair_added(first):
                return lambda t: pe.wait_ge(res_added, first + TB - 1 + min(t, 1))

            norm_then_gemm(pe, B_X1, xn2, act0, [(psum[k], T_XQ + k, (T_XQ + k) % 2) for k in range(2)], pair_added(0))

            def x_project(n, k, act, halves=range(2), n_tok=HALF):
                pe.wait_ge(w_split, n + 1)
                pe.wait_ge(x_lo, k - 1)
                tile_products(pe, psum[k % 2], act, n % 2, halves, n_tok).then_inc(gemm_done, 1)

            for b in range(MB):
                norm_transpose(pe, B_MEM + b, xn2)
            pe.wait_ge(n_lo, B_MEM + MB)
            for h in range(XH):
                x_project(T_XK + h, 2 + h, mem_t, range(1), N_MEM)
            for c in range(KD // 2):
                pe.wait_ge(w_split, T_XV + c + 1)
                w = [t.rearrange("p (k e) -> p k e", k=2) for t in weights((T_XV + c) % 2)]
                for b in range(MB):
                    for k in range(2):
                        for a, p in ((HI, HI), (HI, LO), (LO, HI)):
                            last = pe.matmul(psum[2][:, b * HALF:(b + 1) * HALF],
                                             mem_t[:, 2 * c + k, a, b * P:(b + 1) * P], w[p][:, k, :],
                                             start=(c == 0 and k == 0 and a == p),
                                             stop=(c == KD // 2 - 1 and k == 1 and a == LO))
                last.then_inc(gemm_done, 1)
            pe.wait_ge(x_lo, 2 + XH + 1)
            x_project(T_XQ2, 2 + XH + 1, act0)
            x_project(T_XQ2 + 1, 2 + XH + 2, act0)

            def x_scores(m):
                h = m // X_STEPS
                for k in range(2):
                    t = m % X_STEPS * 2 + k
                    c0 = m % 2 * HALF + k * N_MEM
                    for a, b in ((HI, HI), (HI, LO), (LO, HI)):
                        last = pe.matmul(psum[0][:, c0:c0 + N_MEM], q_x[h][:, a, t * P:(t + 1) * P],
                                         k_x[:, h, b, :], start=(a == b), stop=(a == LO))
                last.then_inc(xs_ready, 1)

            def x_outputs(g):
                h = g // 2
                pe.wait_ge(xpt_lo, 2 * g + 2)
                if g >= 2:
                    pe.wait_ge(xo_lo, g - 1)
                for b in range(MB):
                    for a, p in ((HI, HI), (HI, LO), (LO, HI)):
                        last = pe.matmul(psum[3][:, g % 2 * HALF:(g % 2 + 1) * HALF], v_x[:, b, a, h * XD:(h + 1) * XD],
                                         pt_x[:, p, b, :], start=(b == 0 and a == p), stop=(b == MB - 1 and a == LO))
                last.then_inc(xpv_done, 1)

            pe.wait_ge(x_lo, 2 + XH + 1 + 2)
            x_scores(0)
            x_scores(1)
            for m in range(XH * X_STEPS):
                if m + 2 < XH * X_STEPS:
                    pe.wait_ge(xe_ready, m + 1)
                    x_scores(m + 2)
                if m >= 2 and m % 2 == 0:
                    x_outputs(m // 2 - 1)
                pe.wait_ge(xp_ready, m + 1)
                if m >= 2:
                    pe.wait_ge(xpt_lo, m - 1)
                for k in range(2):
                    for b in range(MB):
                        c0 = m % 2 * HALF + (2 * b + k) * P
                        last = pe.transpose(psum[1][:, c0:c0 + P], xn2[:, m % 2, (2 * k + b) * P:(2 * k + b + 1) * P],
                                            ident[:, :])
                last.then_inc(xt_done, 1)
            x_outputs(2 * XH - 1)

            def free_xo(t):
                if t == 0:
                    pe.wait_ge(xo_lo, 2 * XH)

            token_gemm(T_XO, XH, lambda kd, t: blocks_of(o_x, kd, t), free_xo, TB)
            norm_then_gemm(pe, B_X2, xn2, act0, [(psum[k], T_FF + k, (T_FF + k) % 2) for k in range(2)], pair_added(TB))

            def ff_up(f, n, slot, wait=True):
                pe.wait_ge(w_split, n + 1)
                pe.wait_ge(ff_gate, before(f))
                tile_products(pe, psum[0], act0, slot).then_inc(gemm_done, 1)
                pe.wait_ge(w_split, n + 2)
                pe.wait_ge(ff_prod, before(f))
                tile_products(pe, psum[1], act0, 1 - slot).then_inc(gemm_done, 1)

            def ff_down(f, fs, n, slot):
                pe.wait_ge(w_split, n + 1)
                pe.wait_ge(ff_lo, done(f))
                for t in range(TB):
                    pe.wait_ge(d_added[t % 2], before(4 * f + t // 2))
                    last = row_products(pe, psum[2 + t % 2], blocks_of(act1, fs, t), slot, True, True)
                    if t < TB - 1:
                        last.then_inc(d_ready, 1)
                last.then_inc(gemm_done, 1)

            with pe.Fori(0, (NF - 2) // 2) as i:
                for r in range(2):
                    n = T_FF + 2 + 3 * r
                    ff_up(2 * i + 1 + r, 6 * i + n, n % 2)
                    ff_down(2 * i + r, r, 6 * i + n + 2, n % 2)
            ff_up(NF - 1, T_END - 4, T_END % 2)

            def last_down(f, t, n):
                return row_products(pe, psum[LAST_PAIRS[t % 4]], blocks_of(act1, f % 2, t), n % 2, f == NF - 2, f == NF - 1)

            def last_down_first(t):
                if t < 2:
                    pe.wait_ge(d_added[t], done(4 * (NF - 2) - 1))
                elif t == 2:
                    pe.wait_ge(ff_gate, done(NF - 1))
                elif t == 3:
                    pe.wait_ge(ff_prod, done(NF - 1))
                else:
                    pe.wait_ge(d_added[t % 2], done(4 * (NF - 2) + t // 2 - 2))
                return last_down(NF - 2, t, T_END - 2)

            pe.wait_ge(w_split, T_END - 1)
            pe.wait_ge(ff_lo, done(NF - 2))
            for t in range(4):
                last_down_first(t)
            pe.wait_ge(w_split, T_END)
            pe.wait_ge(ff_lo, done(NF - 1))
            for t in range(TB):
                last = last_down(NF - 1, t, T_END - 1)
                last.then_inc(*((d_ready, 1) if t < TB - 1 else (gemm_done, 1)))
                if 1 <= t < TB - 3:
                    last = last_down_first(t + 3)
                    if t + 3 == TB - 1:
                        last.then_inc(gemm_done, 1)

        @block.scalar
        def _(act):
            act.wait_ge(const_done, 6)
            act.activation(ident_r[:, :], ident[:, :], ACT.Copy).then_inc(const_r, 1)
            act.activation(mask_r[:, :], mask_f[:, :], ACT.Copy).then_inc(const_r, 1)

            def x_ready(t):
                act.wait_ge(x_loaded[t % 4], 16 * (t // 4 + 1))
            norm_blocks_act(act, B_X, lambda t: xin[:, t % 4, :], act0, u_acc[:, :], x_ready,
                            lambda: hi_next(act, T_FORGET))

            hi_next(act, T_FORGET + 1)
            r = slice(0, NH)
            act.wait_ge(gemm_done, T_FORGET + 1)
            act.wait_ge(params_in, 16)
            act.activation(t_f[r, 0, :], psum[1][r, :], ACT.Abs, bias=par[r, C_BF:C_BF + 1]).then_inc(f_abs, 1)
            act.wait_ge(f_abs, 1)
            act.activation(t_f[r, 1, :], t_f[r, 0, :], ACT.Exp, scale=-1.0).then_inc(f_exp, 1)
            act.wait_ge(f_exp, 1)
            act.activation(t_f[r, 0, :], t_f[r, 1, :], ACT.Ln, bias=ones[r, 0:1]).then_inc(f_ln, 1)
            act.wait_ge(f_cum, 1)
            act.activation(q_st[r, HI, :], a_y[r, :], ACT.Copy).then_inc(f_hi, 1)
            act.activation(k_st[r, HI, :], a_y[r, :], ACT.Copy, scale=-1.0).then_inc(f_hi, 1)

            with act.Fori(0, KD) as i:
                for j in range(8):
                    hi_next(act, T_BRANCH + j + 1, i, 8)
                    if j >= 2:
                        act.wait_ge(gemm_done, 8 * i + T_BRANCH + j)
                    if j == 2:
                        act.wait_ge(u_ready, before(i))
                        act.activation(sig[:, :], psum[1][:, :], ACT.Sigmoid).then_inc(sig_ready, 1)
                    if j == 3:
                        act.wait_ge(stage_free, before(i))
                        act.activation(q_st[:, HI, :], psum[2][:, :], ACT.Copy, scale=DH ** -0.5).then_inc(q_hi, 1)
                    if j == 4:
                        act.wait_ge(stage_free, before(i))
                        act.activation(k_st[:, HI, :], psum[0][:, :], ACT.Copy).then_inc(k_hi, 1)
                    if j == 5:
                        act.wait_ge(v_trans, before(i))
                        act.activation(v_t[:, :], psum[1][:, :], ACT.Copy).then_inc(v_copied, 1)
                    if j == 6:
                        act.wait_ge(au_ready, before(i))
                        act.activation(a_c[:, :], psum[2][:, :], ACT.Copy).then_inc(ac_ready, 1)
                        act.wait_ge(v_trans, done(i))
                        act.wait_ge(stage_free, before(i))
                        act.activation(v_st[:, HI, :], psum[3][:, :], ACT.Copy).then_inc(v_hi, 1)
                act.wait_ge(y_ready, done(i))
                act.wait_ge(stage_free, before(i))
                act.activation(a_st[:, HI, :], a_y[:, :], ACT.Copy).then_inc(y_hi, 1)

            with act.Fori(0, 3 * KD // 2) as i:
                for j in range(2):
                    hi_next(act, T_GATE + j + 1, i, 2)
                    act.wait_ge(gemm_done, 2 * i + T_GATE + j + 1)
                    act.wait_ge(gate_free[j], before(i))
                    act.activation(g_st[:, j, :], psum[2 + j][:, :], ACT.Sigmoid,
                                   bias=par[:, bass.ds(2 * i + (C_BGATE + j), 1)]).then_inc(gate_done[j], 1)

            def exps(i, s):
                n = (query(s) + 1) * P
                act.wait_ge(m_ready, N_STEP * i + s + 1)
                act.activation(prob[:, s % 2, 0:n], psum[s % 2][:, 0:n], ACT.Exp, bias=nmax[:, s % 2:s % 2 + 1],
                               accum_out=prob_sum[:, s % 2:s % 2 + 1]).then_inc(e_ready, 1)

            act.wait_ge(mean_ps, 1)
            act.activation(row[:, :], psum[0][:, :], ACT.Copy, scale=1.0 / D).then_inc(mean_done, 1)
            exps(0, 0)
            for stored in gate_stored:
                act.wait_ge(stored, 16 * (3 * KD // 2))

            def outputs_hi(i, g):
                act.wait_ge(pv_done[g % 2], done(4 * i + g // 2 * 2 + 1))
                r, c = half_head(g)
                act.activation(o_st[r, HI, c], psum[3][r, c], ACT.Copy).then_inc(o_hi, 1)

            def pair(i, last):
                for s in range(N_STEP):
                    if not (last and s == N_STEP - 1):
                        exps(i, s + 1)
                    if s == TB:
                        act.wait_ge(o_stage_free, before(i))
                    if s in (TB, TB + 1):
                        outputs_hi(i, s - TB)
                    if s % 4 < 2:
                        act.wait_ge(pv_done[s % 2], before(4 * i + s // 4))
                    q0 = query(s) % 2 * P
                    for c, (j0, j1, bank) in enumerate(chunks(s), first_chunk[s]):
                        act.wait_ge(t_done, N_CHUNK * i + c + 1)
                        act.activation(pt[s % 2][:, HI, j0:j1, q0:q0 + P],
                                       bank[:, 0:(j1 - j0) * P].rearrange("p (j q) -> p j q", q=P),
                                       ACT.Copy).then_inc(pt_hi, 1)
                outputs_hi(i, 2)
                outputs_hi(i, 3)

            attention_pairs(act, pair)

            for br in range(3):
                if br == 1:
                    act.wait_ge(var_ps, 1)
                    act.activation(rstd[:, :], psum[3][:, :], ACT.Sqrt, bias=eps[:, 0:1], scale=1.0 / D)\
                       .then_inc(root_done, 1)
                with act.Fori(0, N_IT) as i:
                    for j in range(2):
                        hi_next(act, T_MERGE + KD * br + j + 1, i, 2)
                        if br == 0:
                            act.wait_ge(xc_ready, done(2 * i + j))
                            act.activation(sq[:, :], xc[:, :], ACT.Square).then_inc(sq_ready, 1)
                        if br == 1:
                            act.wait_ge(ln_ready, 2 * i + j + 1)
                            act.activation(xc[:, :], uin[:, j, :], ACT.Sigmoid,
                                           bias=par[:, bass.ds(2 * i + (C_LNB + j), 1)],
                                           scale=par[:, bass.ds(2 * i + (C_LNG + j), 1)]).then_inc(zs_ready, 1)
                            act.wait_ge(zz_ready, 2 * i + j + 1)
                            act.activation(act0[:, 2 * i + j, HI, :], sq[:, :], ACT.Copy).then_inc(z_hi, 1)
                        if br == 2:
                            act.wait_ge(merged[j], done(2 * N_IT + i))
                            act.activation(act1[:, 2 * i + j, HI, :], part[:, j, :], ACT.Copy).then_inc(mg_hi, 1)

            def residual_norm(b0, first, n0, n1, middle):
                def added(t):
                    act.wait_ge(res_added, first + t + 1)
                for n in range(n0, n1 + 1):
                    if n == middle:
                        for t in range(TB // 2):
                            added(t)
                            norm_stats(act, b0 + t, res[:, t, :], junk)
                    hi_next(act, n)
                norm_blocks_act(act, b0, lambda t: res[:, t, :], act0, junk, added, lambda: hi_next(act, n1 + 1), TB // 2)

            residual_norm(B_X1, 0, T_O + 1, T_XQ, T_O + KD + 3)

            mem_parts = [[mem_t[:, :, s, b * P:(b + 1) * P] for s in (HI, LO)] for b in range(MB)]

            def x_evacuate(k, gemms, dst, src):
                act.wait_ge(gemm_done, gemms)
                act.activation(dst[HI], src, ACT.Copy).then_inc(x_hi, 1)

            act.wait_ge(mem_loaded, 16 * MB)
            for b in range(MB):
                norm_stats(act, B_MEM + b, xn2[:, b, :], junk)
            hi_next(act, T_XQ + 2)
            x_evacuate(0, T_XQ + 1, [q_x[0][:, HI, :]], psum[0][:, :])
            hi_next(act, T_XQ + 3)
            x_evacuate(1, T_XQ + 2, [q_x[1][:, HI, :]], psum[1][:, :])
            for b in range(MB):
                norm_hi(act, B_MEM + b, mem_parts[b])
            for h in range(XH):
                x_evacuate(2 + h, T_XK + h + 1, [k_x[:, h, HI, :]], psum[h % 2][:, 0:N_MEM])
                hi_next(act, T_XK + h + 2)
            for c in range(KD // 2):
                if c < KD // 2 - 1:
                    hi_next(act, T_XV + c + 2)
            x_evacuate(6, T_XV + KD // 2, [v_x[:, :, HI, :]], psum[2][:, :].rearrange("p (b n) -> p b n", b=MB))
            hi_next(act, T_XQ2 + 1)
            act.wait_ge(x_lo, 7)
            x_evacuate(7, T_XQ2 + 1, [q_x[2][:, HI, :]], psum[(2 + XH + 1) % 2][:, :])
            hi_next(act, T_XO)
            x_evacuate(8, T_XQ2 + 2, [q_x[3][:, HI, :]], psum[(2 + XH + 2) % 2][:, :])
            hi_next(act, T_XO + 1)

            def x_exp(m):
                s = m % 2
                act.wait_ge(xm_ready, m + 1)
                if m >= 2:
                    act.wait_ge(xt_done, m - 1)
                for k in range(2):
                    c0 = s * HALF + k * N_MEM
                    ins = act.activation(xn2[:, s, k * N_MEM:(k + 1) * N_MEM], psum[0][:, c0:c0 + N_MEM], ACT.Exp,
                                         bias=xstat[:, 1, s, k:k + 1], scale=XD ** -0.5,
                                         accum_out=xstat[:, 2, s, k:k + 1])
                ins.then_inc(xe_ready, 1)

            def x_outputs_hi(g):
                act.wait_ge(xpv_done, g + 1)
                act.activation(o_x[:, g // 2, HI, g % 2 * HALF:(g % 2 + 1) * HALF],
                               psum[3][:, g % 2 * HALF:(g % 2 + 1) * HALF], ACT.Copy).then_inc(xo_hi, 1)

            x_exp(0)
            for m in range(XH * X_STEPS):
                if m + 1 < XH * X_STEPS:
                    x_exp(m + 1)
                if m >= 3 and m % 2:
                    x_outputs_hi((m - 3) // 2)
                act.wait_ge(xt_done, m + 1)
                if m >= 2 and m % 2 == 0:
                    act.wait_ge(xpv_done, m // 2)
                act.activation(pt_x[:, HI, :, m % 2 * 2 * P:(m % 2 + 1) * 2 * P],
                               psum[1][:, m % 2 * HALF:(m % 2 + 1) * HALF].rearrange("p (b t) -> p b t", b=MB),
                               ACT.Copy).then_inc(xpt_hi, 1)
            x_outputs_hi(2 * XH - 1)

            residual_norm(B_X2, TB, T_XO + 2, T_FF, T_XO + XH + 2)

            def ff_sigmoid(f, gemms):
                act.wait_ge(gemm_done, gemms)
                act.wait_ge(ff_lo, before(f))
                act.activation(xn2[:, 0, :], psum[0][:, :], ACT.Sigmoid).then_inc(ff_sig, 1)

            def ff_high(f, fs):
                act.wait_ge(ff_prod, done(f))
                act.activation(act1[:, fs, HI, :], xn2[:, 0, :], ACT.Copy).then_inc(ff_hi, 1)

            ff_sigmoid(0, T_FF + 1)
            hi_next(act, T_FF + 2)
            with act.Fori(0, (NF - 2) // 2) as i:
                for r in range(2):
                    n = T_FF + 2 + 3 * r
                    hi_next(act, n + 1, i, 6)
                    ff_high(2 * i + r, r)
                    hi_next(act, n + 2, i, 6)
                    ff_sigmoid(2 * i + 1 + r, 6 * i + n + 1)
                    hi_next(act, n + 3, i, 6)
            n = T_END - 4
            hi_next(act, n + 1)
            ff_high(NF - 2, (NF - 2) % 2)
            hi_next(act, n + 2)
            ff_sigmoid(NF - 1, n + 1)
            hi_next(act, n + 3)
            ff_high(NF - 1, (NF - 1) % 2)

            def block_done(t):
                act.wait_ge(d_added[t % 2], done(4 * (NF - 2) + t // 2))
            for t in range(TB):
                block_done(t)
                norm_stats(act, B_OUT + t, res[:, t, :], junk)

        @block.vector
        def _(v):
            v.wait_ge(gain_in, 16)
            norm_blocks_dve(v, B_X, lambda t: xin[:, t % 4, :], xn, act0, lambda: lo_next(v, T_FORGET))
            v.memset(u_pad[:, 0:KC - 1], 0.0).then_inc(pads, 1)
            v.memset(a_pad[:, 0:KA - 1], 0.0).then_inc(pads, 1)
            v.memset(u_sum[:, :], 0.0).then_inc(pads, 1)

            r = slice(0, NH)
            lo_next(v, T_FORGET + 1)
            v.memset(v_t[r, :], 1.0).then_inc(pads, 1)
            v.memset(a_st[r, HI, :].bitcast(F32), 1.0).then_inc(f_rows, 1)
            v.memset(a_st[r, LO, :].bitcast(F32), 0.0).then_inc(f_rows, 1)
            v.wait_ge(gemm_done, T_FORGET + 1)
            v.wait_ge(params_in, 16)
            v.wait_ge(f_abs, 1)
            v.tensor_scalar(a_c[r, :], psum[1][r, :], par[r, C_BF:C_BF + 1], 0.0, ALU.add, ALU.min).then_inc(f_min, 1)
            v.wait_ge(f_min, 1)
            v.wait_ge(f_ln, 1)
            dve.link(v, v.tensor_tensor(a_acc[r, :], a_c[r, :], t_f[r, 0, :], ALU.subtract))
            v.wait_ge(pads, 4)
            v.tensor_tensor_scan(a_y[r, :], v_t[r, :], a_acc[r, :], 0.0, ALU.mult, ALU.add).then_inc(f_cum, 1)
            v.wait_ge(f_cum, 1)
            v.wait_ge(f_hi, 2)
            dve.link(v, v.tensor_tensor(q_st[r, LO, :], a_y[r, :], q_st[r, HI, :].bitcast(F32), ALU.subtract))
            v.scalar_tensor_tensor(k_st[r, LO, :], a_y[r, :], -1.0, k_st[r, HI, :].bitcast(F32), ALU.mult,
                                   ALU.subtract).then_inc(f_rows, 1)

            with v.Fori(0, KD) as i:
                dve.enter(i, KC + KA)

                def conv_taps(count, k0, pad, out, width, col, bias_col):
                    for k in range(k0, k0 + count):
                        w = par[:, bass.ds(width * i + (col + k), 1)]
                        if k == 0 and bias_col is not None:
                            ins = v.tensor_scalar(out[:, :], pad[:, 0:T], w, par[:, bass.ds(i + bias_col, 1)],
                                                  ALU.mult, ALU.add)
                        elif k == 0:
                            ins = v.tensor_scalar(out[:, :], pad[:, 0:T], w, None, ALU.mult)
                        else:
                            ins = v.scalar_tensor_tensor(out[:, :], pad[:, k:k + T], w, out[:, :], ALU.mult, ALU.add)
                        dve.link(v, ins)

                taps = 0
                for j in range(8):
                    lo_next(v, T_BRANCH + j + 1, i, 8)
                    if j == 2:
                        v.wait_ge(sig_ready, done(i))
                        v.tensor_tensor(u_pad[:, KC - 1:], psum[0][:, :], sig[:, :], ALU.mult).then_inc(u_ready, 1)
                        v.wait_ge(u_ready, done(i))
                        v.wait_ge(stage_free, before(i))
                    if j == 3:
                        v.wait_ge(q_hi, done(i))
                        v.scalar_tensor_tensor(q_st[:, LO, :], psum[2][:, :], DH ** -0.5, q_st[:, HI, :].bitcast(F32),
                                               ALU.mult, ALU.subtract).then_inc(q_lo, 1)
                    if j == 4:
                        v.wait_ge(k_hi, done(i))
                        v.tensor_tensor(k_st[:, LO, :], psum[0][:, :], k_st[:, HI, :].bitcast(F32), ALU.subtract)\
                         .then_inc(k_lo, 1)
                    if j == 7:
                        v.wait_ge(v_hi, done(i))
                        v.tensor_tensor(v_st[:, LO, :], psum[3][:, :], v_st[:, HI, :].bitcast(F32), ALU.subtract)\
                         .then_inc(v_lo, 1)
                    if j == 7:
                        v.wait_ge(ac_ready, done(i))
                        v.wait_ge(gemm_done, 8 * i + T_BRANCH + 7)
                        v.tensor_tensor(a_pad[:, KA - 1:], psum[0][:, :], a_c[:, :], ALU.mult).then_inc(au_ready, 1)
                        v.wait_ge(au_ready, done(i))
                        conv_taps(KA, 0, a_pad, a_acc, KA, C_CONVA, None)
                    if j in CONV_TAPS:
                        conv_taps(CONV_TAPS[j], taps, u_pad, u_acc, KC, C_CONVC, C_CBIAS)
                        taps += CONV_TAPS[j]
                    if j == 7:
                        v.tensor_tensor(u_sum[:, :], u_sum[:, :], u_acc[:, :], ALU.add).then_inc(u_summed, 1)
                v.wait_ge(gemm_done, 8 * i + T_BRANCH + 8)
                v.tensor_tensor(a_y[:, :], psum[1][:, :], a_acc[:, :], ALU.mult).then_inc(y_ready, 1)
                v.wait_ge(y_hi, done(i))
                v.tensor_tensor(a_st[:, LO, :], a_y[:, :], a_st[:, HI, :].bitcast(F32), ALU.subtract).then_inc(y_lo, 1)
            dve.leave(KD)

            with v.Fori(0, 3 * KD // 2) as i:
                for j in range(2):
                    lo_next(v, T_GATE + j + 1, i, 2)

            def maxima(i, s):
                n = (query(s) + 1) * P
                v.wait_ge(s_ready, N_STEP * i + s + 1)
                v.tensor_reduce(nmax[:, s % 2:s % 2 + 1], psum[s % 2][:, 0:n], AX.X, ALU.max, negate=True)\
                 .then_inc(m_ready, 1)

            def normalise(i, s):
                k, n = s % 2, (query(s) + 1) * P
                v.wait_ge(e_ready, N_STEP * i + s + 1)
                v.reciprocal(rsum[:, k:k + 1], prob_sum[:, k:k + 1]).then_inc(r_ready, 1)
                v.wait_ge(r_ready, N_STEP * i + s + 1)
                v.tensor_scalar(prob[:, k, 0:n], prob[:, k, 0:n], rsum[:, k:k + 1], None, ALU.mult)\
                 .then_inc(p_ready, 1)

            def probabilities_lo(i, s):
                q0 = query(s) % 2 * P
                for c, (j0, j1, bank) in enumerate(chunks(s), first_chunk[s]):
                    v.wait_ge(pt_hi, N_CHUNK * i + c + 1)
                    v.tensor_tensor(pt[s % 2][:, LO, j0:j1, q0:q0 + P],
                                    bank[:, 0:(j1 - j0) * P].rearrange("p (j q) -> p j q", q=P),
                                    pt[s % 2][:, HI, j0:j1, q0:q0 + P].bitcast(F32), ALU.subtract)\
                     .then_inc(pt_lo, 1)

            def outputs_lo(i, g):
                v.wait_ge(o_hi, done(4 * i + g))
                r, c = half_head(g)
                v.tensor_tensor(o_st[r, LO, c], psum[3][r, c], o_st[r, HI, c].bitcast(F32), ALU.subtract)\
                 .then_inc(o_free[1 - g % 2], 1)

            maxima(0, 0)
            maxima(0, 1)

            def pair(i, last):
                for s in range(N_STEP):
                    normalise(i, s)
                    if s:
                        probabilities_lo(i, s - 1)
                    if s in (TB, TB + 1):
                        outputs_lo(i, s - TB)
                    if not (last and s + 2 >= N_STEP):
                        maxima(i, s + 2)
                probabilities_lo(i, N_STEP - 1)
                outputs_lo(i, 2)
                outputs_lo(i, 3)

            attention_pairs(v, pair)

            v.wait_ge(o_stored, 16 * (NH // 2))
            v.wait_ge(mean_done, 1)
            v.memset(sq_sum[:, :], 0.0).then_inc(sq_added, 1)
            for br in range(3):
                if br == 1:
                    v.wait_ge(root_done, 1)
                    v.reciprocal(rstd[:, :], rstd[:, :]).then_inc(rstd_done, 1)
                with v.Fori(0, N_IT) as i:
                    if br == 1:
                        dve.enter(i, 2)
                    for j in range(2):
                        n = T_MERGE + KD * br + j
                        e = 2 * i + j
                        lo_next(v, n + 1, i, 2)
                        if br == 0:
                            v.wait_ge(u_loaded[j], 16 * i + 16)
                            v.tensor_tensor(xc[:, :], uin[:, j, :], row[:, :], ALU.subtract).then_inc(xc_ready, 1)
                            v.wait_ge(sq_ready, e + 1)
                            v.wait_ge(sq_added, e + 1)
                            v.tensor_tensor(sq_sum[:, :], sq_sum[:, :], sq[:, :], ALU.add).then_inc(sq_added, 1)
                        if br == 1:
                            v.wait_ge(ln_ready, e + 1)
                            dve.link(v, v.tensor_scalar(sq[:, :], uin[:, j, :], par[:, bass.ds(2 * i + (C_LNG + j), 1)],
                                                        par[:, bass.ds(2 * i + (C_LNB + j), 1)], ALU.mult, ALU.add))
                            v.wait_ge(zs_ready, e + 1)
                            v.tensor_tensor(sq[:, :], sq[:, :], xc[:, :], ALU.mult).then_inc(zz_ready, 1)
                            v.wait_ge(z_hi, e + 1)
                            v.tensor_tensor(act0[:, e, LO, :], sq[:, :], act0[:, e, HI, :].bitcast(F32), ALU.subtract)\
                             .then_inc(z_lo, 1)
                        v.wait_ge(gemm_done, 2 * i + n + 1)
                        v.wait_ge(g_loaded[j], 16 * i + 16 * N_IT * br + 16)
                        if br < 2:
                            v.wait_ge(part_free[j], before(N_IT * br + i))
                        else:
                            v.wait_ge(part_free[j], done(2 * N_IT - 1))
                        if br == 0:
                            v.tensor_tensor(part[:, j, :], psum[j][:, :], gin[:, j, :], ALU.mult).then_inc(merged[j], 1)
                        else:
                            v.tensor_tensor(part[:, j, :], psum[j][:, :], gin[:, j, :], ALU.mult).then_inc(gated, 1)
                            v.wait_ge(gated, e + KD * (br - 1) + 1)
                            v.wait_ge(m_loaded[j], 16 * i + 16 * N_IT * (br - 1) + 16)
                            v.tensor_tensor(part[:, j, :], part[:, j, :], m_in[:, j, :], ALU.add).then_inc(merged[j], 1)
                        if br == 2:
                            v.wait_ge(mg_hi, done(e))
                            v.tensor_tensor(act1[:, e, LO, :], part[:, j, :], act1[:, e, HI, :].bitcast(F32),
                                            ALU.subtract).then_inc(mg_lo, 1)
                if br == 1:
                    dve.leave(N_IT)

            def residual_norm(b0, first, n0, n_kd, already_split, middle, gain):
                for h in range(2):
                    for kd in range(n_kd):
                        n = n0 + n_kd * h + kd
                        if n + 1 == middle:
                            v.wait_ge(gain_in, gain)
                            for t in range(2):
                                norm_scale(v, b0 + t, res[:, t, :], xn2, row)
                        if n + 1 >= already_split:
                            lo_next(v, n + 1)
                    for t in range(4):
                        if t < 3:
                            v.wait_ge(tok_done, 3 * (first // 4 + h) + t + 1)
                        else:
                            v.wait_ge(gemm_done, n0 + n_kd * (h + 1))
                        v.tensor_tensor(res[:, 4 * h + t, :], res[:, 4 * h + t, :], psum[t][:, :], ALU.add)\
                         .then_inc(res_added, 1)
                v.wait_ge(res_added, first + TB)
                norm_blocks_dve(v, b0, lambda t: res[:, t, :], xn2, act0, lambda: lo_next(v, n0 + 2 * n_kd + 1), 2)

            v.wait_ge(res_loaded, 16 * TB)
            residual_norm(B_X1, 0, T_O, KD, 0, T_O + KD + 4, 32)

            def x_split(k, dst_hi, dst_lo, src):
                v.wait_ge(x_hi, k + 1)
                v.tensor_tensor(dst_lo, src, dst_hi.bitcast(F32), ALU.subtract).then_inc(x_lo, 1)

            v.wait_ge(gain_in, 48)
            for b in range(MB):
                norm_scale(v, B_MEM + b, xn2[:, b, :], xn2, row)
            lo_next(v, T_XQ + 2)
            x_split(0, q_x[0][:, HI, :], q_x[0][:, LO, :], psum[0][:, :])
            lo_next(v, T_XQ + 3)
            x_split(1, q_x[1][:, HI, :], q_x[1][:, LO, :], psum[1][:, :])
            for b in range(MB):
                norm_lo(v, B_MEM + b, [mem_t[:, :, s, b * P:(b + 1) * P] for s in (HI, LO)])
            for h in range(XH):
                x_split(2 + h, k_x[:, h, HI, :], k_x[:, h, LO, :], psum[h % 2][:, 0:N_MEM])
                lo_next(v, T_XK + h + 2)
            for c in range(KD // 2 - 1):
                lo_next(v, T_XV + c + 2)
            x_split(6, v_x[:, :, HI, :], v_x[:, :, LO, :], psum[2][:, :].rearrange("p (b n) -> p b n", b=MB))
            lo_next(v, T_XQ2 + 1)
            x_split(7, q_x[2][:, HI, :], q_x[2][:, LO, :], psum[1][:, :])
            lo_next(v, T_XO)
            x_split(8, q_x[3][:, HI, :], q_x[3][:, LO, :], psum[0][:, :])
            lo_next(v, T_XO + 1)

            def x_max(m):
                s = m % 2
                v.wait_ge(xs_ready, m + 1)
                dve.link(v, v.tensor_reduce(xstat[:, 0, s, :], psum[0][:, s * HALF:(s + 1) * HALF]
                                            .rearrange("p (k n) -> p k n", k=2), AX.X, ALU.max, negate=True))
                v.tensor_scalar(xstat[:, 1, s, :], xstat[:, 0, s, :], XD ** -0.5, None, ALU.mult).then_inc(xm_ready, 1)

            def x_normalise(m):
                s = m % 2
                v.wait_ge(xe_ready, m + 1)
                dve.link(v, v.reciprocal(xstat[:, 3, s, :], xstat[:, 2, s, :]))
                for k in range(2):
                    c = slice(k * N_MEM, (k + 1) * N_MEM)
                    ins = v.tensor_scalar(xn2[:, s, c], xn2[:, s, c], xstat[:, 3, s, k:k + 1], None, ALU.mult)
                ins.then_inc(xp_ready, 1)

            def x_probabilities_lo(m):
                v.wait_ge(xpt_hi, m + 1)
                c = slice(m % 2 * 2 * P, (m % 2 + 1) * 2 * P)
                v.tensor_tensor(pt_x[:, LO, :, c],
                                psum[1][:, m % 2 * HALF:(m % 2 + 1) * HALF].rearrange("p (b t) -> p b t", b=MB),
                                pt_x[:, HI, :, c].bitcast(F32), ALU.subtract).then_inc(xpt_lo, 1)

            def x_outputs_lo(g):
                c = slice(g % 2 * HALF, (g % 2 + 1) * HALF)
                v.wait_ge(xo_hi, g + 1)
                v.tensor_tensor(o_x[:, g // 2, LO, c], psum[3][:, c], o_x[:, g // 2, HI, c].bitcast(F32),
                                ALU.subtract).then_inc(xo_lo, 1)

            x_max(0)
            x_max(1)
            for m in range(XH * X_STEPS):
                x_normalise(m)
                if m:
                    x_probabilities_lo(m - 1)
                if m >= 3 and m % 2:
                    x_outputs_lo((m - 3) // 2)
                if m + 2 < XH * X_STEPS:
                    x_max(m + 2)
            x_probabilities_lo(XH * X_STEPS - 1)
            x_outputs_lo(2 * XH - 1)

            residual_norm(B_X2, TB, T_XO, XH, T_XO + 2, T_XO + XH + 3, 64)

            def ff_gated(f):
                v.wait_ge(ff_sig, done(f))
                v.tensor_tensor(xn2[:, 1, :], psum[0][:, :], xn2[:, 0, :], ALU.mult).then_inc(ff_gate, 1)

            def ff_product(f, fs, gemms):
                v.wait_ge(ff_gate, done(f))
                v.wait_ge(gemm_done, gemms)
                v.tensor_tensor(xn2[:, 0, :], psum[1][:, :], xn2[:, 1, :], ALU.mult).then_inc(ff_prod, 1)
                v.wait_ge(ff_hi, done(f))
                v.tensor_tensor(act1[:, fs, LO, :], xn2[:, 0, :], act1[:, fs, HI, :].bitcast(F32), ALU.subtract)\
                 .then_inc(ff_lo, 1)

            def ff_add(f, gemms):
                for t in range(TB):
                    if t < TB - 1:
                        v.wait_ge(d_ready, (TB - 1) * f + t + 1)
                    else:
                        v.wait_ge(gemm_done, gemms)
                    v.tensor_tensor(res[:, t, :], res[:, t, :], psum[2 + t % 2][:, :], ALU.add).then_inc(d_added[t % 2], 1)

            ff_gated(0)
            lo_next(v, T_FF + 2)
            with v.Fori(0, (NF - 2) // 2) as i:
                for r_ in range(2):
                    n = T_FF + 2 + 3 * r_
                    lo_next(v, n + 1, i, 6)
                    ff_product(2 * i + r_, r_, 6 * i + n)
                    lo_next(v, n + 2, i, 6)
                    ff_gated(2 * i + 1 + r_)
                    lo_next(v, n + 3, i, 6)
                    ff_add(2 * i + r_, 6 * i + n + 3)
            n = T_END - 4
            lo_next(v, n + 1)
            ff_product(NF - 2, (NF - 2) % 2, n)
            lo_next(v, n + 2)
            ff_gated(NF - 1)
            lo_next(v, n + 3)
            ff_product(NF - 1, (NF - 1) % 2, n + 2)

            v.wait_ge(gain_in, 80)
            for t in range(TB + 1):
                if t < TB:
                    f = NF - 2
                    if t < TB - 1:
                        v.wait_ge(d_ready, (TB - 1) * f + t + 1)
                    else:
                        v.wait_ge(gemm_done, T_END)
                    v.tensor_tensor(res[:, t, :], res[:, t, :], psum[LAST_PAIRS[t % 4]][:, :], ALU.add)\
                     .then_inc(d_added[t % 2], 1)
                if t:
                    b, s, k = t - 1, (t - 1) % 2, (B_OUT + t - 1) % 4
                    v.wait_ge(n_root, B_OUT + b + 1)
                    v.reciprocal(stat[:, 2, k:k + 1], stat[:, 1, k:k + 1]).then_inc(n_rstd, 1)
                    v.wait_ge(n_rstd, B_OUT + b + 1)
                    if b >= 2:
                        v.wait_ge(out_stored[s], 16 * (b // 2))
                    v.scalar_tensor_tensor(xn2[:, s, :], res[:, b, :], stat[:, 2, k:k + 1], row[:, :], ALU.mult, ALU.mult)\
                     .then_inc(n_ready, 1)


def row_tiles(w):
    return np.ascontiguousarray(w.reshape(-1, P, T))


def column_tiles(w, starts):
    return np.ascontiguousarray(
        np.stack([w[:, c:c + P].reshape(KD, P, P).transpose(1, 0, 2).reshape(P, T) for c in starts]))


def kernel(**inputs):
    import concourse.bacc as bacc
    from concourse.bass_utils import run_bass_kernel_spmd

    a = {k: np.asarray(v) for k, v in inputs.items()}
    w_in = a["w_in"][0]
    a_b, a_c, a_u, q, k, v, f = (D * n for n in range(7))
    c_val = f + NH
    c_gate, g = c_val + D, c_val + 2 * D
    order = [f] + [start + e * P for e in range(KD) for start in (c_val, c_gate, q, k, v, a_c, a_u, a_b)]
    order += [g + n * P for n in range(3 * KD)]
    w_xkv = a["w_xkv"][0]
    XW = XH * XD

    def per_channel(m):
        return m.reshape(m.shape[0], -1, P).transpose(2, 1, 0).reshape(P, -1)

    params = np.concatenate([
        per_channel(a["conv_c"][0]), per_channel(a["conv_c_bias"]), per_channel(a["conv_a"][0]),
        per_channel(a["b_gate"]), per_channel(a["ln_c_gain"]), per_channel(a["ln_c_bias"]),
        np.pad(a["b_forget"][0], (0, P - NH))[:, None]], axis=1)
    arrays = {
        "x": a["x"][0],
        "mem": a["mem"][0],
        "w_in": column_tiles(w_in, order),
        "w_out": np.concatenate([column_tiles(a[n][0], range(0, D, P)) for n in ("w_out_a", "w_out_b", "w_out_c")]),
        "w_o": row_tiles(a["w_o"][0]),
        "w_xq": column_tiles(a["w_xq"][0], range(0, XW, P)),
        "w_xk": column_tiles(w_xkv, range(0, XW, P)),
        "w_xv": w_xkv[:, XW:].reshape(KD // 2, 2, P, XW).transpose(0, 2, 1, 3).reshape(KD // 2, P, T),
        "w_xo": row_tiles(a["w_xo"][0]),
        "w_gu": column_tiles(a["w_gate_up"][0], [h * FF + n * P for n in range(NF) for h in range(2)]),
        "w_down": row_tiles(a["w_down"][0]),
        "params": params,
        "norms": np.stack([a["mix_norm"][0], a["xattn_norm"][0], a["mem_norm"], a["ffn_norm"][0], a["final_norm"]]),
    }
    nc = bacc.Bacc("TRN2", target_bir_lowering=False, num_devices=1)
    arrays = {n: np.ascontiguousarray(m) for n, m in arrays.items()}
    args = [nc.dram_tensor(n, m.shape, F32, kind="ExternalInput").ap() for n, m in arrays.items()]
    out = nc.dram_tensor("out", (T, D), F32, kind="ExternalOutput").ap()
    build(nc, *args, out)
    r = run_bass_kernel_spmd(nc, [arrays], core_ids=[0])
    return r.results[0]["out"].reshape(1, T, D)
```

```python
from contextlib import ExitStack

import numpy as np

import concourse.bass as bass
from concourse import mybir

P = 128
F32 = mybir.dt.float32
R32 = mybir.dt.float32r
ALU = mybir.AluOpType
ACT = mybir.ActivationFunctionType
AX = mybir.AxisListType
EPS = 1e-6
MASKED = -1e30
HI, LO = 0, 1

D = 1024
T = 1024
KD = D // P
TB = T // P
HALF = 512
NH, DH = 16, 64
QK_ROWS = DH + 2
KA, KC = 3, 31
N_MEM = 256
MB = N_MEM // P
XH, XD = 4, 128
X_STEPS = TB // 2
Q2_STEP, Q3_STEP = 0, 5
FF = 2816
NF = FF // P

T_FORGET = 0
T_BRANCH = T_FORGET + 1
T_GATE = T_BRANCH + 8 * KD
T_MERGE = T_GATE + 3 * KD
T_O = T_MERGE + 3 * KD
T_XQ = T_O + 2 * KD
T_XK = T_XQ + 2
T_XV = T_XK + XH
T_XQ2 = T_XV + KD // 2
T_XO = T_XQ2 + 2
T_FF = T_XO + 2 * XH
T_END = T_FF + 3 * NF

C_CONVC = 0
C_CBIAS = C_CONVC + KD * KC
C_CONVA = C_CBIAS + KD
C_BGATE = C_CONVA + KD * KA
C_LNG = C_BGATE + 3 * KD
C_LNB = C_LNG + KD
C_BF = C_LNB + KD
N_PARAM = C_BF + 1


class Chain:

    def __init__(self, sem):
        self.sem, self.n, self.i, self.per, self.start = sem, 0, None, 0, 0

    def enter(self, i, per):
        self.i, self.per, self.start = i, per, self.n

    def leave(self, iterations):
        assert self.n - self.start == self.per, (self.n - self.start, self.per)
        self.n = self.start + self.per * iterations
        self.i = None

    def link(self, eng, ins):
        ins.then_inc(self.sem, 1)
        self.n += 1
        eng.wait_ge(self.sem, self.n if self.i is None else self.i * self.per + self.n)


def build(nc, x, mem, w_in, w_out, w_o, w_xq, w_xk, w_xv, w_xo, w_gu, w_down, params, norms, out):
    def scratch(name, shape, dt):
        return nc.dram_tensor(name, shape, dt).ap()

    q_s = scratch("q_s", (NH, QK_ROWS, 2 * T), F32)
    k_s = scratch("k_s", (NH, QK_ROWS, 2 * T), F32)
    v_s = scratch("v_s", (NH // 2, P, 2 * T), F32)
    a_s = scratch("a_s", (KD, P, 2 * T), F32)
    b_s = scratch("b_s", (KD, P, 2 * T), F32)
    u_s = scratch("u_s", (KD, P, T), F32)
    g_s = scratch("g_s", (3 * KD, P, T), F32)
    m_s = scratch("m_s", (KD, P, T), F32)

    with ExitStack() as ctx:
        def sem(name):
            return ctx.enter_context(nc.semaphore(name))

        def sb(name, shape, dt=F32, scope=ctx):
            return scope.enter_context(nc.sbuf_tensor(name, shape, dt))

        ident = sb("ident", [P, P])
        ident_r = sb("ident_r", [P, P], R32)
        mask_r = sb("mask_r", [P, P], R32)
        ones = sb("ones", [P, P])
        eps = sb("eps", [P, 1])
        par = sb("par", [P, N_PARAM])
        xstat = sb("xstat", [P, 4, 2, 2])
        stat = sb("stat", [P, 3, 4])
        w_raw = sb("w_raw", [P, 2, T])
        w_hi = sb("w_hi", [P, 2, T], R32)
        w_lo = sb("w_lo", [P, 2, T], R32)
        row = sb("row", [P, D])
        act0 = sb("act0", [P, KD, 2, T], R32)
        with ExitStack() as s1:
            mask_f = sb("mask_f", [P, P], scope=s1)
            xin = sb("xin", [P, 4, D], scope=s1)
            xn = sb("xn", [P, 2, D], scope=s1)
            t_f = sb("t_f", [P, 2, T], scope=s1)
            u_pad = sb("u_pad", [P, KC - 1 + T], scope=s1)
            sig = sb("sig", [P, T], scope=s1)
            u_acc = sb("u_acc", [P, T], scope=s1)
            a_c = sb("a_c", [P, T], scope=s1)
            a_pad = sb("a_pad", [P, KA - 1 + T], scope=s1)
            a_acc = sb("a_acc", [P, T], scope=s1)
            a_y = sb("a_y", [P, T], scope=s1)
            v_t = sb("v_t", [P, T], scope=s1)
            q_st = sb("q_st", [P, 2, T], R32, scope=s1)
            k_st = sb("k_st", [P, 2, T], R32, scope=s1)
            v_st = sb("v_st", [P, 2, T], R32, scope=s1)
            a_st = sb("a_st", [P, 2, T], R32, scope=s1)
            u_sum = sb("u_sum", [P, T], scope=s1)
            g_st = sb("g_st", [P, 2, T], scope=s1)
        with ExitStack() as s2:
            qh = [sb(f"qh{h}", [QK_ROWS, 2, T], R32, scope=s2) for h in range(2)]
            kh = [sb(f"kh{h}", [QK_ROWS, 2, T], R32, scope=s2) for h in range(2)]
            vh = [sb(f"vh{h}", [P, 2, TB, P], R32, scope=s2) for h in range(2)]
            prob = sb("prob", [P, 2, T], scope=s2)
            pt = [sb(f"pt{u}", [P, 2, TB, 2 * P], R32, scope=s2) for u in range(2)]
            nmax = sb("nmax", [P, 2], scope=s2)
            prob_sum = sb("prob_sum", [P, 2], scope=s2)
            rsum = sb("rsum", [P, 2], scope=s2)
            o_st = sb("o_st", [P, 2, T], R32, scope=s2)
        act1 = sb("act1", [P, KD, 2, T], R32)
        with ExitStack() as s3:
            rstd = sb("rstd", [P, T], scope=s3)
            sq_sum = sb("sq_sum", [P, T], scope=s3)
            gin = sb("gin", [P, 2, T], scope=s3)
            part = sb("part", [P, 2, T], scope=s3)
            m_in = sb("m_in", [P, 2, T], scope=s3)
            uin = sb("uin", [P, 2, T], scope=s3)
            xc = sb("xc", [P, T], scope=s3)
            sq = sb("sq", [P, T], scope=s3)
        res = sb("res", [P, TB, D])
        xn2 = sb("xn2", [P, 2, D])
        flat1 = act1[:, :, :, :].rearrange("p k s t -> p k (s t)")
        mem_t = flat1[:, 0:2, :].rearrange("p k n -> p (k n)").rearrange("p (k s m) -> p k s m", k=KD, s=2)
        k_x = flat1[:, 2, :].rearrange("p (h s m) -> p h s m", h=XH, s=2)
        v_x = flat1[:, 3, :].rearrange("p (b s n) -> p b s n", b=MB, s=2)
        o_x = act1[:, 4:8, :, :]
        q_x = [act1[:, c, :, :] for c in (6, 7, 0, 1)]
        pt_x = sb("pt_x", [P, 2, MB, HALF], R32)
        junk = pt_x[:, 0, :, :].rearrange("p b t -> p (b t)")

        psum = [ctx.enter_context(nc.psum_tensor(f"ps{i}", [P, 2 * HALF], F32)) for i in range(4)]

        credit = []

        def sem1(name):
            s = sem(name)
            credit.append(s)
            return s

        def done(k):
            return k + 2

        def before(k):
            return k + 1

        const_done, params_in, gain_in = sem("const_done"), sem("params_in"), sem("gain_in")
        w_loaded = [sem(f"w_loaded{s}") for s in range(2)]
        w_hi_done, w_split = sem("w_hi_done"), sem("w_split")
        gemm_done = sem("gemm_done")
        dve = Chain(sem("dve_chain"))
        const_r, pads, f_cum, r_ready, gated = (sem(n) for n in ("const_r", "pads", "f_cum", "r_ready", "gated"))
        pool_step = sem("pool_step")
        CONV_TAPS = {2: 5, 3: 6, 4: 6, 5: 7, 6: 6, 7: 1}
        assert sum(CONV_TAPS.values()) == KC
        x_loaded = [sem(f"x_loaded{s}") for s in range(4)]
        n_sq, n_root, n_rstd, n_ready = sem("n_sq"), sem("n_root"), sem("n_rstd"), sem("n_ready")
        n_trans, n_hi, n_lo = sem("n_trans"), sem("n_hi"), sem("n_lo")
        f_abs, f_exp, f_ln, f_min = sem("f_abs"), sem("f_exp"), sem("f_ln"), sem("f_min")
        f_hi, f_rows, rows_stored = sem("f_hi"), sem("f_rows"), sem("rows_stored")
        sig_ready, u_ready, u_summed = sem1("sig_ready"), sem1("u_ready"), sem1("u_summed")
        q_hi, q_lo, k_hi, k_lo = sem1("q_hi"), sem1("q_lo"), sem1("k_hi"), sem1("k_lo")
        v_copied, v_trans, v_hi, v_lo = sem1("v_copied"), sem1("v_trans"), sem1("v_hi"), sem1("v_lo")
        ac_ready, au_ready = sem1("ac_ready"), sem1("au_ready")
        y_ready, y_hi, y_lo = sem1("y_ready"), sem1("y_hi"), sem1("y_lo")
        q_stored, k_stored, v_stored = sem("q_stored"), sem("k_stored"), sem("v_stored")
        u_stored, y_stored = sem("u_stored"), sem("y_stored")
        stage_free = sem("stage_free")
        gate_done = [sem1(f"gate_done{s}") for s in range(2)]
        gate_stored = [sem(f"gate_stored{s}") for s in range(2)]
        gate_free = [sem1(f"gate_free{s}") for s in range(2)]
        qkv_loaded = [sem(f"qkv_loaded{h}") for h in range(2)]
        s_ready, m_ready = sem("s_ready"), sem("m_ready")
        e_ready, p_ready = sem("e_ready"), sem("p_ready")
        t_done, pt_hi, pt_lo = sem("t_done"), sem("pt_hi"), sem1("pt_lo")
        pv_done = [sem1(f"pv_done{s}") for s in range(2)]
        o_free = [sem1(f"o_free{s}") for s in range(2)]
        o_hi, o_stored = sem1("o_hi"), sem("o_stored")
        o_stage_free = sem1("o_stage_free")
        act0_loaded, act1_loaded = sem("act0_loaded"), sem("act1_loaded")
        mean_ps, mean_done = sem("mean_ps"), sem("mean_done")
        g_loaded = [sem(f"g_loaded{s}") for s in range(2)]
        m_loaded = [sem(f"m_loaded{s}") for s in range(2)]
        u_loaded = [sem(f"u_loaded{s}") for s in range(2)]
        merged = [sem1(f"merged{s}") for s in range(2)]
        m_stored = [sem(f"m_stored{s}") for s in range(2)]
        part_free = [sem1(f"part_free{s}") for s in range(2)]
        xc_ready, sq_ready, sq_added = sem1("xc_ready"), sem("sq_ready"), sem("sq_added")
        var_ps, root_done, rstd_done = sem("var_ps"), sem("root_done"), sem("rstd_done")
        xc_done = sem("xc_done")
        ln_ready, zs_ready, zz_ready = sem("ln_ready"), sem("zs_ready"), sem("zz_ready")
        z_hi, z_lo = sem("z_hi"), sem("z_lo")
        mg_hi, mg_lo = sem1("mg_hi"), sem1("mg_lo")
        res_loaded, tok_done, res_added = sem("res_loaded"), sem("tok_done"), sem("res_added")
        mem_loaded = sem("mem_loaded")
        x_hi, x_lo = sem("x_hi"), sem("x_lo")
        xs_ready, xm_ready, xe_ready, xp_ready = (sem(n) for n in ("xs_ready", "xm_ready", "xe_ready", "xp_ready"))
        xt_done, xpt_hi, xpt_lo, xpv_done, xo_hi, xo_lo = (
            sem(n) for n in ("xt_done", "xpt_hi", "xpt_lo", "xpv_done", "xo_hi", "xo_lo"))
        ff_sig, ff_gate, ff_prod, ff_hi, ff_lo = (sem1(n) for n in ("ff_sig", "ff_gate", "ff_prod", "ff_hi", "ff_lo"))
        d_ready = sem("d_ready")
        d_added = [sem1(f"d_added{s}") for s in range(2)]
        out_stored = [sem(f"out_stored{s}") for s in range(2)]

        def load_tile(sp, n, slot, src):
            if not isinstance(n, int) or n >= 2:
                sp.wait_ge(w_split, n - 1)
            sp.dma_start(w_raw[:, slot, :], src).then_inc(w_loaded[slot], 16)

        def split_hi(act, n, slot, loads):
            act.wait_ge(w_loaded[slot], loads * 16)
            if not isinstance(n, int) or n >= 2:
                act.wait_ge(gemm_done, n - 1)
            act.activation(w_hi[:, slot, :], w_raw[:, slot, :], ACT.Copy).then_inc(w_hi_done, 1)

        def split_lo(v, n, slot):
            v.wait_ge(w_hi_done, n + 1)
            v.tensor_tensor(w_lo[:, slot, :], w_raw[:, slot, :], w_hi[:, slot, :].bitcast(F32),
                            ALU.subtract).then_inc(w_split, 1)

        def hi_next(act, base, i=0, per=0):
            split_hi(act, base + per * i, base % 2, base // 2 + 1 + (per // 2) * i)

        def lo_next(v, base, i=0, per=0):
            split_lo(v, base + per * i, base % 2)

        def weights(slot):
            return [w[:, slot, :] for w in (w_hi, w_lo)]

        def tile_products(pe, out, act, slot, halves=range(2), n_tok=HALF, kds=range(KD)):
            w = [t.rearrange("p (k e) -> p k e", k=KD) for t in weights(slot)]
            for kd in kds:
                for half in halves:
                    t0 = half * HALF
                    for a, b in ((HI, HI), (HI, LO), (LO, HI)):
                        last = pe.matmul(out[:, t0:t0 + n_tok], w[a][:, kd, :], act[:, kd, b, t0:t0 + n_tok],
                                         start=(kd == 0 and a == b), stop=(kd == KD - 1 and a == LO))
            return last

        def row_products(pe, out, stat_hl, slot, start, stop):
            w = weights(slot)
            for half in range(2):
                c = slice(half * HALF, (half + 1) * HALF)
                for a, b in ((HI, HI), (HI, LO), (LO, HI)):
                    last = pe.matmul(out[:, c], stat_hl[a], w[b][:, c],
                                     start=(start and a == b), stop=(stop and a == LO))
            return last

        def norm_stats(act, b, src, junk):
            s = b % 4
            if b >= 4:
                act.wait_ge(n_rstd, b - 3)
            act.activation(junk, src, ACT.Square, accum_out=stat[:, 0, s:s + 1]).then_inc(n_sq, 1)
            act.wait_ge(n_sq, b + 1)
            act.activation(stat[:, 1, s:s + 1], stat[:, 0, s:s + 1], ACT.Sqrt, bias=eps[:, 0:1],
                           scale=1.0 / D).then_inc(n_root, 1)

        def norm_scale(v, b, src, dst, g):
            s = b % 4
            v.wait_ge(n_root, b + 1)
            v.reciprocal(stat[:, 2, s:s + 1], stat[:, 1, s:s + 1]).then_inc(n_rstd, 1)
            v.wait_ge(n_rstd, b + 1)
            if b >= 2:
                v.wait_ge(n_trans, b - 1)
            v.scalar_tensor_tensor(dst[:, b % 2, :], src, stat[:, 2, s:s + 1], g[:, :], ALU.mult, ALU.mult)\
             .then_inc(n_ready, 1)

        def norm_transpose(pe, b, src):
            pe.wait_ge(n_ready, b + 1)
            if b >= 2:
                pe.wait_ge(n_lo, b - 1)
            for kd in range(KD):
                last = pe.transpose(psum[2 + b % 2][:, kd * P:(kd + 1) * P], src[:, b % 2, kd * P:(kd + 1) * P],
                                    ident[:, :])
            last.then_inc(n_trans, 1)

        def norm_hi(act, b, dst):
            act.wait_ge(n_trans, b + 1)
            act.activation(dst[HI], psum[2 + b % 2][:, :].rearrange("p (k t) -> p k t", k=KD), ACT.Copy)\
               .then_inc(n_hi, 1)

        def norm_lo(v, b, dst):
            v.wait_ge(n_hi, b + 1)
            v.tensor_tensor(dst[LO], psum[2 + b % 2][:, :].rearrange("p (k t) -> p k t", k=KD),
                            dst[HI].bitcast(F32), ALU.subtract).then_inc(n_lo, 1)

        def token_block(act, t):
            return [act[:, :, s, t * P:(t + 1) * P] for s in (HI, LO)]

        B_X, B_X1, B_MEM, B_X2, B_OUT = 0, TB, 2 * TB, 2 * TB + MB, 3 * TB + MB

        def norm_blocks_act(act, b0, src, dst, junk, ready, midway, started=0):
            for t in range(TB + 2):
                if started <= t < TB:
                    ready(t)
                    norm_stats(act, b0 + t, src(t), junk)
                if t >= 2:
                    norm_hi(act, b0 + t - 2, token_block(dst, t - 2))
                if t == TB // 2 + 1:
                    midway()

        def norm_blocks_dve(v, b0, src, buf, dst, midway, started=0):
            for t in range(TB + 2):
                if started <= t < TB:
                    norm_scale(v, b0 + t, src(t), buf, row)
                if t >= 2:
                    norm_lo(v, b0 + t - 2, token_block(dst, t - 2))
                if t == TB // 2 + 1:
                    midway()

        def norm_then_gemm(pe, b0, src, dst, tiles, ready=lambda t: None, between=lambda: None):
            for t in range(TB - 2):
                ready(t)
                norm_transpose(pe, b0 + t, src)
            for k, (out, n, slot) in enumerate(tiles):
                pe.wait_ge(w_split, n + 1)
                tile_products(pe, out, dst, slot, range(1))
                for t in ((TB - 2, TB - 1) if k == 0 else ()):
                    norm_transpose(pe, b0 + t, src)
            pe.wait_ge(n_lo, b0 + TB)
            for k, (out, n, slot) in enumerate(tiles):
                tile_products(pe, out, dst, slot, range(1, 2)).then_inc(gemm_done, 1)
                if k == 0:
                    between()

        ORDER = [q for n in range(TB // 2) for q in (TB - 1 - n, n)]
        N_STEP = 2 * TB

        def query(s):
            return ORDER[s % TB]

        def chunks(s):
            n = query(s) + 1
            return [(0, 4, psum[2][:, 0:HALF]), (4, n, psum[2][:, HALF:])] if n > 4 else [(0, n, psum[1][:, HALF:])]

        first_chunk = [sum(len(chunks(r)) for r in range(s)) for s in range(N_STEP + 1)]
        N_CHUNK = first_chunk[N_STEP]

        def quarter(k):
            last = k // 2 * 4 + 2 + k % 2
            return k // 4, query(last) // 2, last

        def half_head(g):
            return slice(g // 2 * DH, (g // 2 + 1) * DH), slice((1 - g % 2) * HALF, (2 - g % 2) * HALF)

        def attention_pairs(eng, body):
            with eng.Fori(0, NH // 2 - 1) as i:
                body(i, False)
            body(NH // 2 - 1, True)

        N_PAIR = NF // 2
        G0, U0, G1, U1, D0, D1 = range(T_FF, T_FF + 6)

        N_IT = KD // 2

        block = ctx.enter_context(nc.Block())

        @block.sync
        def _(sp):
            for b in range(TB):
                if b >= 4:
                    sp.wait_ge(n_ready, b - 3)
                sp.dma_start(xin[:, b % 4, :], x[b * P:(b + 1) * P, :]).then_inc(x_loaded[b % 4], 16)
                if b == 0:
                    sp.dma_start(row[:, :], norms[0:1, :].to_broadcast([P, D])).then_inc(gain_in, 16)
                if b == 3:
                    sp.dma_start(par[:, :], params).then_inc(params_in, 16)
                    load_tile(sp, 0, 0, w_in[0])
                    load_tile(sp, 1, 1, w_in[1])
            load_tile(sp, 2, 0, w_in[2])
            with sp.Fori(0, (T_MERGE - 3) // 2) as i:
                load_tile(sp, 2 * i + 3, 1, w_in[2 * i + 3])
                load_tile(sp, 2 * i + 4, 0, w_in[2 * i + 4])
            load_tile(sp, T_MERGE, T_MERGE % 2, w_out[0])
            load_tile(sp, T_MERGE + 1, (T_MERGE + 1) % 2, w_out[1])

            for s in (q_stored, k_stored):
                sp.wait_ge(s, 32 * KD)
            for s in (v_stored, u_stored, y_stored):
                sp.wait_ge(s, 16 * KD)
            sp.wait_ge(rows_stored, 64)

            def load_head(h, head, pair):
                for dst, src in ((qh[h], q_s), (kh[h], k_s)):
                    sp.dma_start(dst[:, :, :].bitcast(F32), src[head].rearrange("p (s t) -> p s t", s=2))\
                      .then_inc(qkv_loaded[h], 16)
                sp.dma_start(vh[h][:, :, :, :].bitcast(F32), v_s[pair].rearrange("p (s j c) -> p s j c", s=2, c=P))\
                  .then_inc(qkv_loaded[h], 16)

            load_head(0, 0, 0)
            load_head(1, 1, 0)
            with sp.Fori(0, NH // 2 - 1) as i:
                sp.wait_ge(pv_done[1], done(4 * i + 1))
                load_head(0, 2 * i + 2, i + 1)
                sp.wait_ge(pv_done[1], done(4 * i + 3))
                load_head(1, 2 * i + 3, i + 1)

            sp.wait_ge(o_stored, 16 * (NH // 2))

            def load_act1(kd):
                sp.dma_start(act1[:, kd, :, :].bitcast(F32), b_s[kd].rearrange("p (s t) -> p s t", s=2))\
                  .then_inc(act1_loaded, 16)

            def load_chunk(br, e, j):
                if br < 2:
                    sp.dma_start(uin[:, j, :], u_s[e]).then_inc(u_loaded[j], 16)
                sp.dma_start(gin[:, j, :], g_s[e + KD * br]).then_inc(g_loaded[j], 16)
                if br:
                    sp.dma_start(m_in[:, j, :], m_s[e]).then_inc(m_loaded[j], 16)

            def merge_step(br, i, j):
                n = T_MERGE + KD * br + j + 2
                at_end = br == 2 and isinstance(i, int)
                load_tile(sp, 2 * i + n, n % 2, w_o[j] if at_end else w_out[2 * i + KD * br + j + 2])
                if br == 0:
                    load_act1(2 * i + j)
                sp.wait_ge(merged[j], done(N_IT * br + i))
                if not isinstance(i, int):
                    load_chunk(br, 2 * i + j + 2, j)
                elif br < 2:
                    sp.wait_ge(m_stored[j], 16 * N_IT * (br + 1))
                    load_chunk(br + 1, j, j)

            for j in range(2):
                load_chunk(0, j, j)
            for br in range(3):
                with sp.Fori(0, N_IT - 1) as i:
                    for j in range(2):
                        merge_step(br, i, j)
                for j in range(2):
                    merge_step(br, N_IT - 1, j)
            sp.wait_ge(mg_lo, done(KD - 1))
            tiles = [w_o[kd] for _ in range(2) for kd in range(KD)]
            tiles += [w_xq[0], w_xq[1]] + [w_xk[h] for h in range(XH)] + [w_xv[c] for c in range(KD // 2)]
            tiles += [w_xq[2], w_xq[3]] + [w_xo[kd] for _ in range(2) for kd in range(XH)]
            tiles += [w_gu[0], w_gu[1]]
            assert T_O + len(tiles) == T_FF + 2
            for n in range(T_O + 2, T_FF + 2):
                if n == T_XQ + 2:
                    sp.wait_ge(n_trans, B_X1 + TB)
                    for b in range(MB):
                        sp.dma_start(xn2[:, b, :], mem[b * P:(b + 1) * P, :]).then_inc(mem_loaded, 16)
                    sp.wait_ge(n_ready, B_MEM)
                    sp.dma_start(row[:, :], norms[2:3, :].to_broadcast([P, D])).then_inc(gain_in, 16)
                if n == T_XO:
                    sp.wait_ge(n_ready, B_X2)
                    sp.dma_start(row[:, :], norms[3:4, :].to_broadcast([P, D])).then_inc(gain_in, 16)
                load_tile(sp, n, n % 2, tiles[n - T_O])
                t = n - (T_O + 2)
                if t < TB:
                    sp.dma_start(res[:, t, :], x[t * P:(t + 1) * P, :]).then_inc(res_loaded, 16)
                if t == TB // 2 - 1:
                    sp.dma_start(row[:, :], norms[1:2, :].to_broadcast([P, D])).then_inc(gain_in, 16)
            with sp.Fori(0, N_PAIR - 1) as i:
                for j, src in enumerate((w_gu[4 * i + 2], w_gu[4 * i + 3], w_down[2 * i], w_down[2 * i + 1],
                                         w_gu[4 * i + 4], w_gu[4 * i + 5])):
                    load_tile(sp, 6 * i + G1 + j, (G1 + j) % 2, src)
            for j, src in enumerate((w_gu[2 * NF - 2], w_gu[2 * NF - 1], w_down[NF - 2], w_down[NF - 1])):
                n = T_END - 4 + j
                load_tile(sp, n, n % 2, src)
            sp.wait_ge(n_ready, B_OUT)
            sp.dma_start(row[:, :], norms[4:5, :].to_broadcast([P, D])).then_inc(gain_in, 16)
            for t in range(TB):
                sp.wait_ge(n_ready, B_OUT + t + 1)
                sp.dma_start(out[t * P:(t + 1) * P, :], xn2[:, t % 2, :]).then_inc(out_stored[t % 2], 16)
            for s in range(2):
                sp.wait_ge(out_stored[s], 16 * TB // 2)

        @block.gpsimd
        def _(pool):
            def wait(s, value):
                pool.wait_ge(s, value)
                pool.sem_inc(pool_step, 1)

            for s in credit:
                pool.sem_inc(s, 1)
            pool.memset(ident[:, :], 0.0).then_inc(const_done, 1)
            pool.memset(mask_f[:, :], 0.0).then_inc(const_done, 1)
            pool.memset(ones[:, :], 1.0).then_inc(const_done, 1)
            pool.memset(eps[:, :], EPS).then_inc(const_done, 1)
            pool.wait_ge(const_done, 4)
            pool.affine_select(out=ident[:, :], in_=ident[:, :], compare_op=ALU.not_equal, fill=1.0, base=0,
                               pattern=[[-1, P]], channel_multiplier=1).then_inc(const_done, 1)
            pool.affine_select(out=mask_f[:, :], in_=mask_f[:, :], compare_op=ALU.is_ge, fill=MASKED, base=0,
                               pattern=[[-1, P]], channel_multiplier=1).then_inc(const_done, 1)

            pool.wait_ge(f_rows, 3)
            r = slice(0, NH)
            for dst, src, at in ((q_s, a_st, DH), (q_s, q_st, DH + 1), (k_s, k_st, DH), (k_s, a_st, DH + 1)):
                pool.dma_start(dst[:, at, :], src[r, :, :].rearrange("p s t -> p (s t)").bitcast(F32))\
                    .then_inc(rows_stored, 16)
            pool.wait_ge(rows_stored, 64)
            pool.sem_inc(stage_free, 1)

            with pool.Fori(0, KD) as i:
                for lo_sem, st, dst, stored in ((q_lo, q_st, q_s, q_stored), (k_lo, k_st, k_s, k_stored)):
                    wait(lo_sem, done(i))
                    for h in range(2):
                        pool.dma_start(dst[2 * i + h, 0:DH, :].rearrange("p (s t) -> p s t", s=2),
                                       st[h * DH:(h + 1) * DH, :, :].bitcast(F32)).then_inc(stored, 16)
                wait(v_lo, done(i))
                pool.dma_start(v_s[i].rearrange("p (s t) -> p s t", s=2), v_st[:, :, :].bitcast(F32))\
                    .then_inc(v_stored, 16)
                wait(u_summed, done(i))
                pool.dma_start(u_s[i], u_acc[:, :]).then_inc(u_stored, 16)
                wait(y_lo, done(i))
                pool.dma_start(a_s[i].rearrange("p (s t) -> p s t", s=2), a_st[:, :, :].bitcast(F32))\
                    .then_inc(y_stored, 16)
                for s, by in ((q_stored, 32), (k_stored, 32), (v_stored, 16), (u_stored, 16), (y_stored, 16)):
                    wait(s, by * i + by)
                pool.sem_inc(stage_free, 1)
            with pool.Fori(0, 3 * KD // 2) as i:
                for j in range(2):
                    wait(gate_done[j], done(i))
                    pool.dma_start(g_s[2 * i + j], g_st[:, j, :]).then_inc(gate_stored[j], 16)
                for j in range(2):
                    wait(gate_stored[j], 16 * i + 16)
                    pool.sem_inc(gate_free[j], 1)

            wait(gemm_done, T_MERGE)
            wait(y_stored, 16 * KD)
            wait(qkv_loaded[1], 48)
            for kd in range(KD):
                pool.dma_start(act0[:, kd, :, :].bitcast(F32), a_s[kd].rearrange("p (s t) -> p s t", s=2))\
                    .then_inc(act0_loaded, 16)

            with pool.Fori(0, NH // 2) as i:
                wait(o_free[0], done(2 * i + 1))
                pool.dma_start(b_s[i].rearrange("p (s t) -> p s t", s=2), o_st[:, :, :].bitcast(F32))\
                    .then_inc(o_stored, 16)
                wait(o_stored, 16 * i + 16)
                pool.sem_inc(o_stage_free, 1)

            def layer_norm(i, j):
                wait(u_loaded[j], 16 * i + 16 * N_IT + 16)
                pool.tensor_tensor(uin[:, j, :], uin[:, j, :], row[:, :], ALU.subtract).then_inc(xc_done, 1)
                wait(xc_done, 2 * i + j + 1)
                pool.tensor_tensor(uin[:, j, :], uin[:, j, :], rstd[:, :], ALU.mult).then_inc(ln_ready, 1)

            def store_partial(br, i, j):
                wait(merged[j], done(N_IT * br + i))
                pool.dma_start(m_s[2 * i + j], part[:, j, :]).then_inc(m_stored[j], 16)

            def free_partial(br, i, j):
                wait(m_stored[j], 16 * i + 16 * N_IT * br + 16)
                pool.sem_inc(part_free[j], 1)

            with pool.Fori(0, N_IT) as i:
                for j in range(2):
                    store_partial(0, i, j)
                for j in range(2):
                    free_partial(0, i, j)
            pool.wait_ge(rstd_done, 1)
            layer_norm(0, 0)

            def merge_steps(i, last):
                layer_norm(i, 1)
                store_partial(1, i, 0)
                if not last:
                    layer_norm(i + 1, 0)
                free_partial(1, i, 0)
                store_partial(1, i, 1)
                free_partial(1, i, 1)

            with pool.Fori(0, N_IT - 1) as i:
                merge_steps(i, False)
            merge_steps(N_IT - 1, True)

        @block.tensor
        def _(pe):
            pe.wait_ge(const_done, 6)
            norm_then_gemm(pe, B_X, xn, act0, [(psum[1], T_FORGET, T_FORGET % 2)])

            pair_free = [(au_ready, before), (y_ready, before), (ac_ready, before), (u_ready, done),
                         (sig_ready, done), (q_lo, done), (k_lo, done), (v_copied, done)]
            with pe.Fori(0, KD) as i:
                for j in range(8):
                    pe.wait_ge(w_split, 8 * i + T_BRANCH + j + 1)
                    s, when = pair_free[j]
                    pe.wait_ge(s, when(i))
                    tile_products(pe, psum[j % 3], act0, (T_BRANCH + j) % 2).then_inc(gemm_done, 1)
                    if j == 5:
                        pe.wait_ge(v_copied, done(i))
                        pe.wait_ge(v_lo, before(i))
                        for b in range(TB):
                            last = pe.transpose(psum[3][:, b * P:(b + 1) * P], v_t[:, b * P:(b + 1) * P], ident[:, :])
                        last.then_inc(v_trans, 1)

            pe.wait_ge(ac_ready, done(KD - 1))
            pe.wait_ge(v_lo, done(KD - 1))
            with pe.Fori(0, 3 * KD // 2) as i:
                for j in range(2):
                    pe.wait_ge(w_split, 2 * i + T_GATE + j + 1)
                    pe.wait_ge(gate_done[j], before(i))
                    tile_products(pe, psum[2 + j], act0, (T_GATE + j) % 2).then_inc(gemm_done, 1)

            def scores(s):
                h, qb, ps = s // TB % 2, query(s), psum[s % 2]
                n = (qb + 1) * P
                q = slice(qb * P, n)
                for c in range(0, n, HALF):
                    k = slice(c, min(n, c + HALF))
                    for a, b in ((HI, HI), (HI, LO), (LO, HI)):
                        last = pe.matmul(ps[:, k], qh[h][:, a, q], kh[h][:, b, k], start=(a == b),
                                         stop=(a == LO and k.stop < n))
                last = pe.matmul(ps[:, q], ident_r[:, :], mask_r[:, :], start=False, stop=True)
                last.then_inc(s_ready, 1)

            def transposes(i, s):
                pe.wait_ge(pt_lo, done(N_CHUNK * i + (first_chunk[s - 1] if s >= 2 else 0) - 1))
                for j0, j1, bank in chunks(s):
                    for j in range(j0, j1):
                        last = pe.transpose(bank[:, (j - j0) * P:(j - j0 + 1) * P],
                                            prob[:, s % 2, j * P:(j + 1) * P], ident[:, :])
                    last.then_inc(t_done, 1)

            def outputs(i, k):
                h, u, s = quarter(k)
                half = u // 2
                pe.wait_ge(pt_lo, done(N_CHUNK * i + first_chunk[s + 1] - 1))
                if k % 4 < 2:
                    pe.wait_ge(o_free[half], before(2 * i + h))
                o0 = half * HALF + u % 2 * 2 * P
                last_j = 2 * u + 1
                for j in range(last_j + 1):
                    c0 = P if j == last_j else 0
                    for a, b in ((HI, HI), (HI, LO), (LO, HI)):
                        last = pe.matmul(psum[3][:, o0 + c0:o0 + 2 * P], vh[h][:, a, j, :],
                                         pt[k % 2][:, b, j, c0:2 * P], start=(j == 0 and a == b),
                                         stop=(j == last_j and a == LO))
                last.then_inc(pv_done[k % 2], 1)

            pe.wait_ge(au_ready, done(KD - 1))
            pe.wait_ge(y_ready, done(KD - 1))
            pe.wait_ge(u_summed, done(KD - 1))
            for half in range(2):
                c = slice(half * HALF, (half + 1) * HALF)
                last = pe.matmul(psum[0][:, c], ones[:, :], u_sum[:, c], start=True, stop=True)
            last.then_inc(mean_ps, 1)
            pe.wait_ge(mean_done, 1)
            for s in gate_done:
                pe.wait_ge(s, done(3 * KD // 2 - 1))
            pe.wait_ge(const_r, 2)
            pe.wait_ge(qkv_loaded[0], 48)
            scores(0)
            scores(1)

            def pair(i, last):
                for s in range(N_STEP):
                    if not (last and s + 2 >= N_STEP):
                        if s + 2 == TB:
                            pe.wait_ge(qkv_loaded[1], 48 * i + 48)
                        if s + 2 == N_STEP:
                            pe.wait_ge(qkv_loaded[0], 48 * i + 96)
                        pe.wait_ge(e_ready, N_STEP * i + s + 1)
                        scores(s + 2)
                    pe.wait_ge(p_ready, N_STEP * i + s + 1)
                    transposes(i, s)
                    for k in range(8):
                        if quarter(k)[2] == s - 1:
                            outputs(i, k)
                outputs(i, 7)

            attention_pairs(pe, pair)

            for s in o_free:
                pe.wait_ge(s, done(2 * (NH // 2) - 1))
            for br, act in enumerate((act0, act1, act0)):
                if br == 0:
                    pe.wait_ge(act0_loaded, 16 * KD)
                if br == 1:
                    pe.wait_ge(sq_added, KD + 1)
                    for half in range(2):
                        c = slice(half * HALF, (half + 1) * HALF)
                        last = pe.matmul(psum[3][:, c], ones[:, :], sq_sum[:, c], start=True, stop=True)
                    last.then_inc(var_ps, 1)
                    pe.wait_ge(act1_loaded, 16 * KD)
                if br == 2:
                    pe.wait_ge(z_lo, KD)
                with pe.Fori(0, N_IT) as i:
                    for j in range(2):
                        n = T_MERGE + KD * br + j
                        pe.wait_ge(w_split, 2 * i + n + 1)
                        pe.wait_ge(merged[j], before(N_IT * br + i))
                        tile_products(pe, psum[j], act, n % 2).then_inc(gemm_done, 1)

            def token_gemm(n0, n_kd, stationary, ready, free, first):
                for h in range(2):
                    for kd in range(n_kd):
                        n = n0 + n_kd * h + kd
                        pe.wait_ge(w_split, n + 1)
                        if h == 0:
                            ready(kd)
                        for t in range(4):
                            if kd == 0 and h == 0:
                                free(t)
                            if kd == 0 and h == 1:
                                pe.wait_ge(res_added, first + t + 1)
                            last = row_products(pe, psum[t], stationary(kd, 4 * h + t), n % 2,
                                                kd == 0, kd == n_kd - 1)
                            if kd == n_kd - 1 and t < 3:
                                last.then_inc(tok_done, 1)
                        last.then_inc(gemm_done, 1)

            def blocks_of(act, kd, t):
                return [act[:, kd, s, t * P:(t + 1) * P] for s in (HI, LO)]

            def free_o(t):
                if t < 2:
                    pe.wait_ge(merged[t], done(3 * N_IT - 1))
                if t == 3:
                    pe.wait_ge(root_done, 1)

            token_gemm(T_O, KD, lambda kd, t: blocks_of(act1, kd, t),
                       lambda kd: pe.wait_ge(mg_lo, done(kd)), free_o, 0)

            def pair_added(first):
                return lambda t: pe.wait_ge(res_added, first + TB - 1 + min(t, 1))

            def memory_transposes():
                for b in range(MB):
                    norm_transpose(pe, B_MEM + b, xn2)

            norm_then_gemm(pe, B_X1, xn2, act0, [(psum[k], T_XQ + k, (T_XQ + k) % 2) for k in range(2)],
                           pair_added(0), memory_transposes)

            def x_project(n, k, act, halves=range(2), n_tok=HALF):
                pe.wait_ge(w_split, n + 1)
                pe.wait_ge(x_lo, k - 1)
                tile_products(pe, psum[k % 2], act, n % 2, halves, n_tok).then_inc(gemm_done, 1)

            pe.wait_ge(n_lo, B_MEM + MB)
            for h in range(XH):
                x_project(T_XK + h, 2 + h, mem_t, range(1), N_MEM)
            for c in range(KD // 2):
                pe.wait_ge(w_split, T_XV + c + 1)
                w = [t.rearrange("p (k e) -> p k e", k=2) for t in weights((T_XV + c) % 2)]
                for b in range(MB):
                    for k in range(2):
                        for a, p in ((HI, HI), (HI, LO), (LO, HI)):
                            last = pe.matmul(psum[2][:, b * HALF:(b + 1) * HALF],
                                             mem_t[:, 2 * c + k, a, b * P:(b + 1) * P], w[p][:, k, :],
                                             start=(c == 0 and k == 0 and a == p),
                                             stop=(c == KD // 2 - 1 and k == 1 and a == LO))
                last.then_inc(gemm_done, 1)
            def late_queries(m):
                for k, m0 in enumerate((Q2_STEP, Q3_STEP)):
                    if m == m0:
                        pe.wait_ge(w_split, T_XQ2 + k + 1)
                        pe.wait_ge(x_lo, (5, 8)[k])
                    if 0 <= m - m0 < 4:
                        kds = range(2 * (m - m0), 2 * (m - m0) + 2)
                        last = tile_products(pe, psum[0], act0, (T_XQ2 + k) % 2, kds=kds)
                        if m - m0 == 3:
                            last.then_inc(gemm_done, 1)

            def x_scores(m):
                h = m // X_STEPS
                for k in range(2):
                    t = m % X_STEPS * 2 + k
                    c0 = m % 2 * HALF + k * N_MEM
                    for a, b in ((HI, HI), (HI, LO), (LO, HI)):
                        last = pe.matmul(psum[2][:, c0:c0 + N_MEM], q_x[h][:, a, t * P:(t + 1) * P],
                                         k_x[:, h, b, :], start=(a == b), stop=(a == LO))
                last.then_inc(xs_ready, 1)

            def x_outputs(g):
                h = g // 2
                pe.wait_ge(xpt_lo, 2 * g + 2)
                if g >= 2:
                    pe.wait_ge(xo_lo, g - 1)
                for b in range(MB):
                    for a, p in ((HI, HI), (HI, LO), (LO, HI)):
                        last = pe.matmul(psum[3][:, g % 2 * HALF:(g % 2 + 1) * HALF], v_x[:, b, a, h * XD:(h + 1) * XD],
                                         pt_x[:, p, b, :], start=(b == 0 and a == p), stop=(b == MB - 1 and a == LO))
                last.then_inc(xpv_done, 1)

            pe.wait_ge(x_lo, 2 + XH + 1)
            x_scores(0)
            x_scores(1)
            for m in range(XH * X_STEPS):
                if m + 2 < XH * X_STEPS:
                    pe.wait_ge(xe_ready, m + 1)
                    if m + 2 in (2 * X_STEPS, 3 * X_STEPS):
                        pe.wait_ge(x_lo, 2 + XH + (m + 2) // X_STEPS)
                    x_scores(m + 2)
                if m >= 2 and m % 2 == 0:
                    x_outputs(m // 2 - 1)
                late_queries(m)
                pe.wait_ge(xp_ready, m + 1)
                if m >= 2:
                    pe.wait_ge(xpt_lo, m - 1)
                for k in range(2):
                    for b in range(MB):
                        c0 = m % 2 * HALF + (2 * b + k) * P
                        last = pe.transpose(psum[1][:, c0:c0 + P], xn2[:, m % 2, (2 * k + b) * P:(2 * k + b + 1) * P],
                                            ident[:, :])
                last.then_inc(xt_done, 1)
            x_outputs(2 * XH - 1)

            def free_xo(t):
                if t == 3:
                    pe.wait_ge(xo_lo, 2 * XH)

            token_gemm(T_XO, XH, lambda kd, t: blocks_of(o_x, kd, t),
                       lambda kd: pe.wait_ge(xo_lo, 2 * kd + 2), free_xo, TB)
            norm_then_gemm(pe, B_X2, xn2, act0, [(psum[k], T_FF + k, (T_FF + k) % 2) for k in range(2)], pair_added(TB))

            def ff_tile(n, i, out, ready, value):
                pe.wait_ge(w_split, 6 * i + n + 1)
                pe.wait_ge(ready, value)
                tile_products(pe, out, act0, n % 2).then_inc(gemm_done, 1)

            def down_first(i, t):
                if t == 0:
                    pe.wait_ge(ff_gate, done(2 * i + 1))
                elif t == 1:
                    pe.wait_ge(ff_prod, done(2 * i + 1))
                elif t < 4:
                    pe.wait_ge(d_added[t % 2], before(4 * i))
                else:
                    pe.wait_ge(d_added[t % 2], done(4 * i + t // 2 - 2))
                return row_products(pe, psum[t % 4], blocks_of(act1, 0, t), D0 % 2, True, False)

            def ff_pair(i, last):
                ff_tile(G1, i, psum[0], ff_gate, done(2 * i))
                ff_tile(U1, i, psum[1], ff_prod, done(2 * i))
                pe.wait_ge(w_split, 6 * i + D0 + 1)
                pe.wait_ge(ff_lo, done(2 * i))
                for t in (0, 2, 3, 1):
                    down_first(i, t)
                pe.wait_ge(w_split, 6 * i + D1 + 1)
                pe.wait_ge(ff_lo, done(2 * i + 1))
                for t in range(TB):
                    row_products(pe, psum[t % 4], blocks_of(act1, 1, t), D1 % 2, False, True)\
                        .then_inc(d_ready if t < TB - 1 else gemm_done, 1)
                    if 1 <= t < TB - 3:
                        first = down_first(i, t + 3)
                        if t + 3 == TB - 1:
                            first.then_inc(gemm_done, 1)
                if not last:
                    ff_tile(G0 + 6, i, psum[0], d_added[0], done(4 * i + 2))
                    ff_tile(U0 + 6, i, psum[1], d_added[1], done(4 * i + 2))

            with pe.Fori(0, N_PAIR - 1) as i:
                ff_pair(i, False)
            ff_pair(N_PAIR - 1, True)

        @block.scalar
        def _(act):
            act.wait_ge(const_done, 6)
            act.activation(ident_r[:, :], ident[:, :], ACT.Copy).then_inc(const_r, 1)
            act.activation(mask_r[:, :], mask_f[:, :], ACT.Copy).then_inc(const_r, 1)

            def x_ready(t):
                act.wait_ge(x_loaded[t % 4], 16 * (t // 4 + 1))
            norm_blocks_act(act, B_X, lambda t: xin[:, t % 4, :], act0, u_acc[:, :], x_ready,
                            lambda: hi_next(act, T_FORGET))

            hi_next(act, T_FORGET + 1)
            r = slice(0, NH)
            act.wait_ge(gemm_done, T_FORGET + 1)
            act.wait_ge(params_in, 16)
            act.activation(t_f[r, 0, :], psum[1][r, :], ACT.Abs, bias=par[r, C_BF:C_BF + 1]).then_inc(f_abs, 1)
            act.wait_ge(f_abs, 1)
            act.activation(t_f[r, 1, :], t_f[r, 0, :], ACT.Exp, scale=-1.0).then_inc(f_exp, 1)
            act.wait_ge(f_exp, 1)
            act.activation(t_f[r, 0, :], t_f[r, 1, :], ACT.Ln, bias=ones[r, 0:1]).then_inc(f_ln, 1)
            act.wait_ge(f_cum, 1)
            act.activation(q_st[r, HI, :], a_y[r, :], ACT.Copy).then_inc(f_hi, 1)
            act.activation(k_st[r, HI, :], a_y[r, :], ACT.Copy, scale=-1.0).then_inc(f_hi, 1)

            with act.Fori(0, KD) as i:
                for j in range(8):
                    hi_next(act, T_BRANCH + j + 1, i, 8)
                    if j >= 2:
                        act.wait_ge(gemm_done, 8 * i + T_BRANCH + j)
                    if j == 2:
                        act.wait_ge(u_ready, before(i))
                        act.activation(sig[:, :], psum[1][:, :], ACT.Sigmoid).then_inc(sig_ready, 1)
                    if j == 3:
                        act.wait_ge(stage_free, before(i))
                        act.activation(q_st[:, HI, :], psum[2][:, :], ACT.Copy, scale=DH ** -0.5).then_inc(q_hi, 1)
                    if j == 4:
                        act.wait_ge(stage_free, before(i))
                        act.activation(k_st[:, HI, :], psum[0][:, :], ACT.Copy).then_inc(k_hi, 1)
                    if j == 5:
                        act.wait_ge(v_trans, before(i))
                        act.activation(v_t[:, :], psum[1][:, :], ACT.Copy).then_inc(v_copied, 1)
                    if j == 6:
                        act.wait_ge(au_ready, before(i))
                        act.activation(a_c[:, :], psum[2][:, :], ACT.Copy).then_inc(ac_ready, 1)
                        act.wait_ge(v_trans, done(i))
                        act.wait_ge(stage_free, before(i))
                        act.activation(v_st[:, HI, :], psum[3][:, :], ACT.Copy).then_inc(v_hi, 1)
                act.wait_ge(y_ready, done(i))
                act.wait_ge(stage_free, before(i))
                act.activation(a_st[:, HI, :], a_y[:, :], ACT.Copy).then_inc(y_hi, 1)

            with act.Fori(0, 3 * KD // 2) as i:
                for j in range(2):
                    hi_next(act, T_GATE + j + 1, i, 2)
                    act.wait_ge(gemm_done, 2 * i + T_GATE + j + 1)
                    act.wait_ge(gate_free[j], before(i))
                    act.activation(g_st[:, j, :], psum[2 + j][:, :], ACT.Sigmoid,
                                   bias=par[:, bass.ds(2 * i + (C_BGATE + j), 1)]).then_inc(gate_done[j], 1)

            def exps(i, s):
                n = (query(s) + 1) * P
                act.wait_ge(m_ready, N_STEP * i + s + 1)
                act.activation(prob[:, s % 2, 0:n], psum[s % 2][:, 0:n], ACT.Exp, bias=nmax[:, s % 2:s % 2 + 1],
                               accum_out=prob_sum[:, s % 2:s % 2 + 1]).then_inc(e_ready, 1)

            act.wait_ge(mean_ps, 1)
            act.activation(row[:, :], psum[0][:, :], ACT.Copy, scale=1.0 / D).then_inc(mean_done, 1)
            exps(0, 0)
            for stored in gate_stored:
                act.wait_ge(stored, 16 * (3 * KD // 2))

            def outputs_hi(i, g):
                act.wait_ge(pv_done[g % 2], done(4 * i + g // 2 * 2 + 1))
                r, c = half_head(g)
                act.activation(o_st[r, HI, c], psum[3][r, c], ACT.Copy).then_inc(o_hi, 1)

            def pair(i, last):
                for s in range(N_STEP):
                    if not (last and s == N_STEP - 1):
                        exps(i, s + 1)
                    if s == TB:
                        act.wait_ge(o_stage_free, before(i))
                    if s in (TB, TB + 1):
                        outputs_hi(i, s - TB)
                    if s % 4 < 2:
                        act.wait_ge(pv_done[s % 2], before(4 * i + s // 4))
                    q0 = query(s) % 2 * P
                    for c, (j0, j1, bank) in enumerate(chunks(s), first_chunk[s]):
                        act.wait_ge(t_done, N_CHUNK * i + c + 1)
                        act.activation(pt[s % 2][:, HI, j0:j1, q0:q0 + P],
                                       bank[:, 0:(j1 - j0) * P].rearrange("p (j q) -> p j q", q=P),
                                       ACT.Copy).then_inc(pt_hi, 1)
                outputs_hi(i, 2)
                outputs_hi(i, 3)

            attention_pairs(act, pair)

            for br in range(3):
                if br == 1:
                    act.wait_ge(var_ps, 1)
                    act.activation(rstd[:, :], psum[3][:, :], ACT.Sqrt, bias=eps[:, 0:1], scale=1.0 / D)\
                       .then_inc(root_done, 1)
                with act.Fori(0, N_IT) as i:
                    for j in range(2):
                        hi_next(act, T_MERGE + KD * br + j + 1, i, 2)
                        if br == 0:
                            act.wait_ge(xc_ready, done(2 * i + j))
                            act.activation(sq[:, :], xc[:, :], ACT.Square).then_inc(sq_ready, 1)
                        if br == 1:
                            act.wait_ge(ln_ready, 2 * i + j + 1)
                            act.activation(xc[:, :], uin[:, j, :], ACT.Sigmoid,
                                           bias=par[:, bass.ds(2 * i + (C_LNB + j), 1)],
                                           scale=par[:, bass.ds(2 * i + (C_LNG + j), 1)]).then_inc(zs_ready, 1)
                            act.wait_ge(zz_ready, 2 * i + j + 1)
                            act.activation(act0[:, 2 * i + j, HI, :], sq[:, :], ACT.Copy).then_inc(z_hi, 1)
                        if br == 2:
                            act.wait_ge(merged[j], done(2 * N_IT + i))
                            act.activation(act1[:, 2 * i + j, HI, :], part[:, j, :], ACT.Copy).then_inc(mg_hi, 1)

            def residual_norm(b0, first, n0, n1, middle):
                def added(t):
                    act.wait_ge(res_added, first + t + 1)
                for n in range(n0, n1 + 1):
                    if n == middle:
                        for t in range(TB // 2):
                            added(t)
                            norm_stats(act, b0 + t, res[:, t, :], junk)
                    hi_next(act, n)
                norm_blocks_act(act, b0, lambda t: res[:, t, :], act0, junk, added, lambda: hi_next(act, n1 + 1),
                                TB // 2)

            residual_norm(B_X1, 0, T_O + 1, T_XQ, T_O + KD + 3)

            mem_parts = [[mem_t[:, :, s, b * P:(b + 1) * P] for s in (HI, LO)] for b in range(MB)]

            def x_evacuate(k, gemms, dst, src):
                act.wait_ge(gemm_done, gemms)
                act.activation(dst[HI], src, ACT.Copy).then_inc(x_hi, 1)

            act.wait_ge(mem_loaded, 16 * MB)
            for b in range(MB):
                norm_stats(act, B_MEM + b, xn2[:, b, :], junk)
            for b in range(MB):
                norm_hi(act, B_MEM + b, mem_parts[b])
            hi_next(act, T_XQ + 2)
            x_evacuate(0, T_XQ + 1, [q_x[0][:, HI, :]], psum[0][:, :])
            hi_next(act, T_XQ + 3)
            x_evacuate(1, T_XQ + 2, [q_x[1][:, HI, :]], psum[1][:, :])
            for h in range(XH):
                x_evacuate(2 + h, T_XK + h + 1, [k_x[:, h, HI, :]], psum[h % 2][:, 0:N_MEM])
                hi_next(act, T_XK + h + 2)
            for c in range(KD // 2):
                if c < KD // 2 - 1:
                    hi_next(act, T_XV + c + 2)
            x_evacuate(6, T_XV + KD // 2, [v_x[:, :, HI, :]], psum[2][:, :].rearrange("p (b n) -> p b n", b=MB))
            hi_next(act, T_XQ2 + 1)
            act.wait_ge(x_lo, 7)

            def x_exp(m):
                s = m % 2
                act.wait_ge(xm_ready, m + 1)
                if m >= 2:
                    act.wait_ge(xt_done, m - 1)
                for k in range(2):
                    c0 = s * HALF + k * N_MEM
                    ins = act.activation(xn2[:, s, k * N_MEM:(k + 1) * N_MEM], psum[2][:, c0:c0 + N_MEM], ACT.Exp,
                                         bias=xstat[:, 1, s, k:k + 1], scale=XD ** -0.5,
                                         accum_out=xstat[:, 2, s, k:k + 1])
                ins.then_inc(xe_ready, 1)

            def x_outputs_hi(g):
                act.wait_ge(xpv_done, g + 1)
                act.activation(o_x[:, g // 2, HI, g % 2 * HALF:(g % 2 + 1) * HALF],
                               psum[3][:, g % 2 * HALF:(g % 2 + 1) * HALF], ACT.Copy).then_inc(xo_hi, 1)

            x_exp(0)
            for m in range(XH * X_STEPS):
                if m + 1 < XH * X_STEPS:
                    x_exp(m + 1)
                if m >= 3 and m % 2:
                    x_outputs_hi((m - 3) // 2)
                act.wait_ge(xt_done, m + 1)
                if m >= 2 and m % 2 == 0:
                    act.wait_ge(xpv_done, m // 2)
                act.activation(pt_x[:, HI, :, m % 2 * 2 * P:(m % 2 + 1) * 2 * P],
                               psum[1][:, m % 2 * HALF:(m % 2 + 1) * HALF].rearrange("p (b t) -> p b t", b=MB),
                               ACT.Copy).then_inc(xpt_hi, 1)
                for k, m0 in enumerate((Q2_STEP, Q3_STEP)):
                    if m == m0 + 4:
                        x_evacuate(7 + k, T_XQ2 + k + 1, [q_x[2 + k][:, HI, :]], psum[0][:, :])
                        hi_next(act, T_XO + k)
            x_outputs_hi(2 * XH - 1)

            residual_norm(B_X2, TB, T_XO + 2, T_FF, T_XO + XH + 2)

            def ff_sigmoid(f, gemms):
                act.wait_ge(gemm_done, gemms)
                act.wait_ge(ff_lo, before(f))
                act.activation(xn2[:, 0, :], psum[0][:, :], ACT.Sigmoid).then_inc(ff_sig, 1)

            def ff_high(f, fs):
                act.wait_ge(ff_prod, done(f))
                act.activation(act1[:, fs, HI, :], xn2[:, 0, :], ACT.Copy).then_inc(ff_hi, 1)

            def ff_pair(i, last):
                hi_next(act, U1, i, 6)
                ff_high(2 * i, 0)
                hi_next(act, D0, i, 6)
                ff_sigmoid(2 * i + 1, 6 * i + G1 + 1)
                hi_next(act, D1, i, 6)
                ff_high(2 * i + 1, 1)
                if not last:
                    hi_next(act, G0 + 6, i, 6)
                    hi_next(act, U0 + 6, i, 6)
                    ff_sigmoid(2 * i + 2, 6 * i + G0 + 7)
                    hi_next(act, G1 + 6, i, 6)

            ff_sigmoid(0, G0 + 1)
            hi_next(act, G1)
            with act.Fori(0, N_PAIR - 1) as i:
                ff_pair(i, False)
            ff_pair(N_PAIR - 1, True)

            def block_done(t):
                act.wait_ge(d_added[t % 2], done(4 * (N_PAIR - 1) + t // 2))
            for t in range(TB):
                block_done(t)
                norm_stats(act, B_OUT + t, res[:, t, :], junk)

        @block.vector
        def _(v):
            v.wait_ge(gain_in, 16)
            norm_blocks_dve(v, B_X, lambda t: xin[:, t % 4, :], xn, act0, lambda: lo_next(v, T_FORGET))
            v.memset(u_pad[:, 0:KC - 1], 0.0).then_inc(pads, 1)
            v.memset(a_pad[:, 0:KA - 1], 0.0).then_inc(pads, 1)
            v.memset(u_sum[:, :], 0.0).then_inc(pads, 1)

            r = slice(0, NH)
            lo_next(v, T_FORGET + 1)
            v.memset(v_t[r, :], 1.0).then_inc(pads, 1)
            v.memset(a_st[r, HI, :].bitcast(F32), 1.0).then_inc(f_rows, 1)
            v.memset(a_st[r, LO, :].bitcast(F32), 0.0).then_inc(f_rows, 1)
            v.wait_ge(gemm_done, T_FORGET + 1)
            v.wait_ge(params_in, 16)
            v.wait_ge(f_abs, 1)
            v.tensor_scalar(a_c[r, :], psum[1][r, :], par[r, C_BF:C_BF + 1], 0.0, ALU.add, ALU.min).then_inc(f_min, 1)
            v.wait_ge(f_min, 1)
            v.wait_ge(f_ln, 1)
            dve.link(v, v.tensor_tensor(a_acc[r, :], a_c[r, :], t_f[r, 0, :], ALU.subtract))
            v.wait_ge(pads, 4)
            v.tensor_tensor_scan(a_y[r, :], v_t[r, :], a_acc[r, :], 0.0, ALU.mult, ALU.add).then_inc(f_cum, 1)
            v.wait_ge(f_cum, 1)
            v.wait_ge(f_hi, 2)
            dve.link(v, v.tensor_tensor(q_st[r, LO, :], a_y[r, :], q_st[r, HI, :].bitcast(F32), ALU.subtract))
            v.scalar_tensor_tensor(k_st[r, LO, :], a_y[r, :], -1.0, k_st[r, HI, :].bitcast(F32), ALU.mult,
                                   ALU.subtract).then_inc(f_rows, 1)

            with v.Fori(0, KD) as i:
                dve.enter(i, KC + KA)

                def conv_taps(count, k0, pad, out, width, col, bias_col):
                    for k in range(k0, k0 + count):
                        w = par[:, bass.ds(width * i + (col + k), 1)]
                        if k == 0 and bias_col is not None:
                            ins = v.tensor_scalar(out[:, :], pad[:, 0:T], w, par[:, bass.ds(i + bias_col, 1)],
                                                  ALU.mult, ALU.add)
                        elif k == 0:
                            ins = v.tensor_scalar(out[:, :], pad[:, 0:T], w, None, ALU.mult)
                        else:
                            ins = v.scalar_tensor_tensor(out[:, :], pad[:, k:k + T], w, out[:, :], ALU.mult, ALU.add)
                        dve.link(v, ins)

                taps = 0
                for j in range(8):
                    lo_next(v, T_BRANCH + j + 1, i, 8)
                    if j == 2:
                        v.wait_ge(sig_ready, done(i))
                        v.tensor_tensor(u_pad[:, KC - 1:], psum[0][:, :], sig[:, :], ALU.mult).then_inc(u_ready, 1)
                        v.wait_ge(u_ready, done(i))
                        v.wait_ge(stage_free, before(i))
                    if j == 3:
                        v.wait_ge(q_hi, done(i))
                        v.scalar_tensor_tensor(q_st[:, LO, :], psum[2][:, :], DH ** -0.5, q_st[:, HI, :].bitcast(F32),
                                               ALU.mult, ALU.subtract).then_inc(q_lo, 1)
                    if j == 4:
                        v.wait_ge(k_hi, done(i))
                        v.tensor_tensor(k_st[:, LO, :], psum[0][:, :], k_st[:, HI, :].bitcast(F32), ALU.subtract)\
                         .then_inc(k_lo, 1)
                    if j == 7:
                        v.wait_ge(v_hi, done(i))
                        v.tensor_tensor(v_st[:, LO, :], psum[3][:, :], v_st[:, HI, :].bitcast(F32), ALU.subtract)\
                         .then_inc(v_lo, 1)
                    if j == 7:
                        v.wait_ge(ac_ready, done(i))
                        v.wait_ge(gemm_done, 8 * i + T_BRANCH + 7)
                        v.tensor_tensor(a_pad[:, KA - 1:], psum[0][:, :], a_c[:, :], ALU.mult).then_inc(au_ready, 1)
                        v.wait_ge(au_ready, done(i))
                        conv_taps(KA, 0, a_pad, a_acc, KA, C_CONVA, None)
                    if j in CONV_TAPS:
                        conv_taps(CONV_TAPS[j], taps, u_pad, u_acc, KC, C_CONVC, C_CBIAS)
                        taps += CONV_TAPS[j]
                    if j == 7:
                        v.tensor_tensor(u_sum[:, :], u_sum[:, :], u_acc[:, :], ALU.add).then_inc(u_summed, 1)
                v.wait_ge(gemm_done, 8 * i + T_BRANCH + 8)
                v.tensor_tensor(a_y[:, :], psum[1][:, :], a_acc[:, :], ALU.mult).then_inc(y_ready, 1)
                v.wait_ge(y_hi, done(i))
                v.tensor_tensor(a_st[:, LO, :], a_y[:, :], a_st[:, HI, :].bitcast(F32), ALU.subtract).then_inc(y_lo, 1)
            dve.leave(KD)

            with v.Fori(0, 3 * KD // 2) as i:
                for j in range(2):
                    lo_next(v, T_GATE + j + 1, i, 2)

            def maxima(i, s):
                n = (query(s) + 1) * P
                v.wait_ge(s_ready, N_STEP * i + s + 1)
                v.tensor_reduce(nmax[:, s % 2:s % 2 + 1], psum[s % 2][:, 0:n], AX.X, ALU.max, negate=True)\
                 .then_inc(m_ready, 1)

            def normalise(i, s):
                k, n = s % 2, (query(s) + 1) * P
                v.wait_ge(e_ready, N_STEP * i + s + 1)
                v.reciprocal(rsum[:, k:k + 1], prob_sum[:, k:k + 1]).then_inc(r_ready, 1)
                v.wait_ge(r_ready, N_STEP * i + s + 1)
                v.tensor_scalar(prob[:, k, 0:n], prob[:, k, 0:n], rsum[:, k:k + 1], None, ALU.mult)\
                 .then_inc(p_ready, 1)

            def probabilities_lo(i, s):
                q0 = query(s) % 2 * P
                for c, (j0, j1, bank) in enumerate(chunks(s), first_chunk[s]):
                    v.wait_ge(pt_hi, N_CHUNK * i + c + 1)
                    v.tensor_tensor(pt[s % 2][:, LO, j0:j1, q0:q0 + P],
                                    bank[:, 0:(j1 - j0) * P].rearrange("p (j q) -> p j q", q=P),
                                    pt[s % 2][:, HI, j0:j1, q0:q0 + P].bitcast(F32), ALU.subtract)\
                     .then_inc(pt_lo, 1)

            def outputs_lo(i, g):
                v.wait_ge(o_hi, done(4 * i + g))
                r, c = half_head(g)
                v.tensor_tensor(o_st[r, LO, c], psum[3][r, c], o_st[r, HI, c].bitcast(F32), ALU.subtract)\
                 .then_inc(o_free[1 - g % 2], 1)

            maxima(0, 0)
            maxima(0, 1)

            def pair(i, last):
                for s in range(N_STEP):
                    normalise(i, s)
                    if s:
                        probabilities_lo(i, s - 1)
                    if s in (TB, TB + 1):
                        outputs_lo(i, s - TB)
                    if not (last and s + 2 >= N_STEP):
                        maxima(i, s + 2)
                probabilities_lo(i, N_STEP - 1)
                outputs_lo(i, 2)
                outputs_lo(i, 3)

            attention_pairs(v, pair)

            v.wait_ge(o_stored, 16 * (NH // 2))
            v.wait_ge(mean_done, 1)
            v.memset(sq_sum[:, :], 0.0).then_inc(sq_added, 1)
            for br in range(3):
                if br == 1:
                    v.wait_ge(root_done, 1)
                    v.reciprocal(rstd[:, :], rstd[:, :]).then_inc(rstd_done, 1)
                with v.Fori(0, N_IT) as i:
                    if br == 1:
                        dve.enter(i, 2)
                    for j in range(2):
                        n = T_MERGE + KD * br + j
                        e = 2 * i + j
                        lo_next(v, n + 1, i, 2)
                        if br == 0:
                            v.wait_ge(u_loaded[j], 16 * i + 16)
                            v.tensor_tensor(xc[:, :], uin[:, j, :], row[:, :], ALU.subtract).then_inc(xc_ready, 1)
                            v.wait_ge(sq_ready, e + 1)
                            v.wait_ge(sq_added, e + 1)
                            v.tensor_tensor(sq_sum[:, :], sq_sum[:, :], sq[:, :], ALU.add).then_inc(sq_added, 1)
                        if br == 1:
                            v.wait_ge(ln_ready, e + 1)
                            dve.link(v, v.tensor_scalar(sq[:, :], uin[:, j, :], par[:, bass.ds(2 * i + (C_LNG + j), 1)],
                                                        par[:, bass.ds(2 * i + (C_LNB + j), 1)], ALU.mult, ALU.add))
                            v.wait_ge(zs_ready, e + 1)
                            v.tensor_tensor(sq[:, :], sq[:, :], xc[:, :], ALU.mult).then_inc(zz_ready, 1)
                            v.wait_ge(z_hi, e + 1)
                            v.tensor_tensor(act0[:, e, LO, :], sq[:, :], act0[:, e, HI, :].bitcast(F32), ALU.subtract)\
                             .then_inc(z_lo, 1)
                        v.wait_ge(gemm_done, 2 * i + n + 1)
                        v.wait_ge(g_loaded[j], 16 * i + 16 * N_IT * br + 16)
                        if br < 2:
                            v.wait_ge(part_free[j], before(N_IT * br + i))
                        else:
                            v.wait_ge(part_free[j], done(2 * N_IT - 1))
                        if br == 0:
                            v.tensor_tensor(part[:, j, :], psum[j][:, :], gin[:, j, :], ALU.mult).then_inc(merged[j], 1)
                        else:
                            v.tensor_tensor(part[:, j, :], psum[j][:, :], gin[:, j, :], ALU.mult).then_inc(gated, 1)
                            v.wait_ge(gated, e + KD * (br - 1) + 1)
                            v.wait_ge(m_loaded[j], 16 * i + 16 * N_IT * (br - 1) + 16)
                            v.tensor_tensor(part[:, j, :], part[:, j, :], m_in[:, j, :], ALU.add).then_inc(merged[j], 1)
                        if br == 2:
                            v.wait_ge(mg_hi, done(e))
                            v.tensor_tensor(act1[:, e, LO, :], part[:, j, :], act1[:, e, HI, :].bitcast(F32),
                                            ALU.subtract).then_inc(mg_lo, 1)
                if br == 1:
                    dve.leave(N_IT)

            def residual_norm(b0, first, n0, n_kd, already_split, middle, gain):
                for h in range(2):
                    for kd in range(n_kd):
                        n = n0 + n_kd * h + kd
                        if n + 1 == middle:
                            v.wait_ge(gain_in, gain)
                            for t in range(2):
                                norm_scale(v, b0 + t, res[:, t, :], xn2, row)
                        if n + 1 >= already_split:
                            lo_next(v, n + 1)
                    if first == 0:
                        v.wait_ge(res_loaded, 16 * TB)
                    for t in range(4):
                        if t < 3:
                            v.wait_ge(tok_done, 3 * (first // 4 + h) + t + 1)
                        else:
                            v.wait_ge(gemm_done, n0 + n_kd * (h + 1))
                        v.tensor_tensor(res[:, 4 * h + t, :], res[:, 4 * h + t, :], psum[t][:, :], ALU.add)\
                         .then_inc(res_added, 1)
                v.wait_ge(res_added, first + TB)
                norm_blocks_dve(v, b0, lambda t: res[:, t, :], xn2, act0, lambda: lo_next(v, n0 + 2 * n_kd + 1), 2)

            residual_norm(B_X1, 0, T_O, KD, 0, T_O + KD + 4, 32)

            def x_split(k, dst_hi, dst_lo, src):
                v.wait_ge(x_hi, k + 1)
                v.tensor_tensor(dst_lo, src, dst_hi.bitcast(F32), ALU.subtract).then_inc(x_lo, 1)

            v.wait_ge(gain_in, 48)
            for b in range(MB):
                norm_scale(v, B_MEM + b, xn2[:, b, :], xn2, row)
            for b in range(MB):
                norm_lo(v, B_MEM + b, [mem_t[:, :, s, b * P:(b + 1) * P] for s in (HI, LO)])
            lo_next(v, T_XQ + 2)
            x_split(0, q_x[0][:, HI, :], q_x[0][:, LO, :], psum[0][:, :])
            lo_next(v, T_XQ + 3)
            x_split(1, q_x[1][:, HI, :], q_x[1][:, LO, :], psum[1][:, :])
            for h in range(XH):
                x_split(2 + h, k_x[:, h, HI, :], k_x[:, h, LO, :], psum[h % 2][:, 0:N_MEM])
                lo_next(v, T_XK + h + 2)
            for c in range(KD // 2 - 1):
                lo_next(v, T_XV + c + 2)
            x_split(6, v_x[:, :, HI, :], v_x[:, :, LO, :], psum[2][:, :].rearrange("p (b n) -> p b n", b=MB))
            lo_next(v, T_XQ2 + 1)

            def x_max(m):
                s = m % 2
                v.wait_ge(xs_ready, m + 1)
                dve.link(v, v.tensor_reduce(xstat[:, 0, s, :], psum[2][:, s * HALF:(s + 1) * HALF]
                                            .rearrange("p (k n) -> p k n", k=2), AX.X, ALU.max, negate=True))
                v.tensor_scalar(xstat[:, 1, s, :], xstat[:, 0, s, :], XD ** -0.5, None, ALU.mult).then_inc(xm_ready, 1)

            def x_normalise(m):
                s = m % 2
                v.wait_ge(xe_ready, m + 1)
                dve.link(v, v.reciprocal(xstat[:, 3, s, :], xstat[:, 2, s, :]))
                for k in range(2):
                    c = slice(k * N_MEM, (k + 1) * N_MEM)
                    ins = v.tensor_scalar(xn2[:, s, c], xn2[:, s, c], xstat[:, 3, s, k:k + 1], None, ALU.mult)
                ins.then_inc(xp_ready, 1)

            def x_probabilities_lo(m):
                v.wait_ge(xpt_hi, m + 1)
                c = slice(m % 2 * 2 * P, (m % 2 + 1) * 2 * P)
                v.tensor_tensor(pt_x[:, LO, :, c],
                                psum[1][:, m % 2 * HALF:(m % 2 + 1) * HALF].rearrange("p (b t) -> p b t", b=MB),
                                pt_x[:, HI, :, c].bitcast(F32), ALU.subtract).then_inc(xpt_lo, 1)

            def x_outputs_lo(g):
                c = slice(g % 2 * HALF, (g % 2 + 1) * HALF)
                v.wait_ge(xo_hi, g + 1)
                v.tensor_tensor(o_x[:, g // 2, LO, c], psum[3][:, c], o_x[:, g // 2, HI, c].bitcast(F32),
                                ALU.subtract).then_inc(xo_lo, 1)

            x_max(0)
            x_max(1)
            for m in range(XH * X_STEPS):
                x_normalise(m)
                if m:
                    x_probabilities_lo(m - 1)
                if m >= 3 and m % 2:
                    x_outputs_lo((m - 3) // 2)
                if m + 2 < XH * X_STEPS:
                    x_max(m + 2)
                for k, m0 in enumerate((Q2_STEP, Q3_STEP)):
                    if m == m0 + 4:
                        x_split(7 + k, q_x[2 + k][:, HI, :], q_x[2 + k][:, LO, :], psum[0][:, :])
                        lo_next(v, T_XO + k)
            x_probabilities_lo(XH * X_STEPS - 1)
            x_outputs_lo(2 * XH - 1)

            residual_norm(B_X2, TB, T_XO, XH, T_XO + 2, T_XO + XH + 3, 64)

            def ff_gated(f):
                v.wait_ge(ff_sig, done(f))
                v.tensor_tensor(xn2[:, 1, :], psum[0][:, :], xn2[:, 0, :], ALU.mult).then_inc(ff_gate, 1)

            def ff_product(f, fs, gemms, between=lambda: None):
                v.wait_ge(ff_gate, done(f))
                v.wait_ge(gemm_done, gemms)
                v.tensor_tensor(xn2[:, 0, :], psum[1][:, :], xn2[:, 1, :], ALU.mult).then_inc(ff_prod, 1)
                between()
                v.wait_ge(ff_hi, done(f))
                v.tensor_tensor(act1[:, fs, LO, :], xn2[:, 0, :], act1[:, fs, HI, :].bitcast(F32), ALU.subtract)\
                 .then_inc(ff_lo, 1)

            def ff_add(i, t):
                if t < TB - 1:
                    v.wait_ge(d_ready, (TB - 1) * i + t + 1)
                else:
                    v.wait_ge(gemm_done, 6 * i + D1 + 1)
                v.tensor_tensor(res[:, t, :], res[:, t, :], psum[t % 4][:, :], ALU.add).then_inc(d_added[t % 2], 1)

            def final_norm(t):
                s, k = t % 2, (B_OUT + t) % 4
                v.wait_ge(n_root, B_OUT + t + 1)
                v.reciprocal(stat[:, 2, k:k + 1], stat[:, 1, k:k + 1]).then_inc(n_rstd, 1)
                v.wait_ge(n_rstd, B_OUT + t + 1)
                if t >= 2:
                    v.wait_ge(out_stored[s], 16 * (t // 2))
                v.scalar_tensor_tensor(xn2[:, s, :], res[:, t, :], stat[:, 2, k:k + 1], row[:, :], ALU.mult, ALU.mult)\
                 .then_inc(n_ready, 1)

            def ff_pair(i, last):
                lo_next(v, U1, i, 6)
                ff_product(2 * i, 0, 6 * i + U0 + 1)
                lo_next(v, D0, i, 6)
                ff_gated(2 * i + 1)
                ff_product(2 * i + 1, 1, 6 * i + U1 + 1, lambda: lo_next(v, D1, i, 6))
                if last:
                    v.wait_ge(gain_in, 80)
                for t in range(TB):
                    if t == 5 and not last:
                        lo_next(v, G0 + 6, i, 6)
                    ff_add(i, t)
                    if last and t:
                        final_norm(t - 1)
                if last:
                    final_norm(TB - 1)
                else:
                    lo_next(v, U0 + 6, i, 6)
                    ff_gated(2 * i + 2)
                    lo_next(v, G1 + 6, i, 6)

            ff_gated(0)
            lo_next(v, G1)
            with v.Fori(0, N_PAIR - 1) as i:
                ff_pair(i, False)
            ff_pair(N_PAIR - 1, True)


def row_tiles(w):
    return np.ascontiguousarray(w.reshape(-1, P, T))


def column_tiles(w, starts):
    return np.ascontiguousarray(
        np.stack([w[:, c:c + P].reshape(KD, P, P).transpose(1, 0, 2).reshape(P, T) for c in starts]))


def kernel(**inputs):
    import concourse.bacc as bacc
    from concourse.bass_utils import run_bass_kernel_spmd

    a = {k: np.asarray(v) for k, v in inputs.items()}
    w_in = a["w_in"][0]
    a_b, a_c, a_u, q, k, v, f = (D * n for n in range(7))
    c_val = f + NH
    c_gate, g = c_val + D, c_val + 2 * D
    order = [f] + [start + e * P for e in range(KD) for start in (c_val, c_gate, q, k, v, a_c, a_u, a_b)]
    order += [g + n * P for n in range(3 * KD)]
    w_xkv = a["w_xkv"][0]
    XW = XH * XD

    def per_channel(m):
        return m.reshape(m.shape[0], -1, P).transpose(2, 1, 0).reshape(P, -1)

    params = np.concatenate([
        per_channel(a["conv_c"][0]), per_channel(a["conv_c_bias"]), per_channel(a["conv_a"][0]),
        per_channel(a["b_gate"]), per_channel(a["ln_c_gain"]), per_channel(a["ln_c_bias"]),
        np.pad(a["b_forget"][0], (0, P - NH))[:, None]], axis=1)
    arrays = {
        "x": a["x"][0],
        "mem": a["mem"][0],
        "w_in": column_tiles(w_in, order),
        "w_out": np.concatenate([column_tiles(a[n][0], range(0, D, P)) for n in ("w_out_a", "w_out_b", "w_out_c")]),
        "w_o": row_tiles(a["w_o"][0]),
        "w_xq": column_tiles(a["w_xq"][0], range(0, XW, P)),
        "w_xk": column_tiles(w_xkv, range(0, XW, P)),
        "w_xv": w_xkv[:, XW:].reshape(KD // 2, 2, P, XW).transpose(0, 2, 1, 3).reshape(KD // 2, P, T),
        "w_xo": row_tiles(a["w_xo"][0]),
        "w_gu": column_tiles(a["w_gate_up"][0], [h * FF + n * P for n in range(NF) for h in range(2)]),
        "w_down": row_tiles(a["w_down"][0]),
        "params": params,
        "norms": np.stack([a["mix_norm"][0], a["xattn_norm"][0], a["mem_norm"], a["ffn_norm"][0], a["final_norm"]]),
    }
    nc = bacc.Bacc("TRN2", target_bir_lowering=False, num_devices=1)
    arrays = {n: np.ascontiguousarray(m) for n, m in arrays.items()}
    args = [nc.dram_tensor(n, m.shape, F32, kind="ExternalInput").ap() for n, m in arrays.items()]
    out = nc.dram_tensor("out", (T, D), F32, kind="ExternalOutput").ap()
    build(nc, *args, out)
    r = run_bass_kernel_spmd(nc, [arrays], core_ids=[0])
    return r.results[0]["out"].reshape(1, T, D)
```
